# Optimizing a Trainium2 kernel written in Bass

```python
import math
import jax, jax.numpy as jnp
from jax import lax
import numpy as np
import jax
import jax.numpy as jnp

D_MODEL = 1024
BATCH = 1
SEQ = 1024
DEPTH = 2

N_MIXERS = 2
N_ATTN_LAYERS = (DEPTH + 1) // 2
N_POOL_LAYERS = DEPTH // 2
N_HEADS = 8
HEAD_DIM = D_MODEL // (2 * N_HEADS)
V_DIM = 2 * HEAD_DIM
QK_WIDTH = 2 * N_HEADS * HEAD_DIM
ROT_DIM = HEAD_DIM // 4
ROPE_THETA = 500000.0
Q_BLOCK = 128
SUBLN_EPS = 1e-5
POOL_WINDOWS = (2, 4, 8, 16)
N_POOL_GROUPS = len(POOL_WINDOWS)
POOL_GROUP_DIM = D_MODEL // N_POOL_GROUPS
N_GROUPS = 4
EXPERTS_PER_GROUP = 8
N_EXPERTS = N_GROUPS * EXPERTS_PER_GROUP
TOP_K = 2
D_EXPERT = D_MODEL // 2
MOE_BLOCK = 128
ROUTER_BIAS_SCALE = 0.01
DEEPNORM_ALPHA = (2 * DEPTH) ** 0.25
DEEPNORM_BETA = (8 * DEPTH) ** -0.25
LN_EPS = 1e-5


def layer_norm(x, g, b):
    xf = x.astype(jnp.float32)
    mu = jnp.mean(xf, -1, keepdims=True)
    var = jnp.mean(jnp.square(xf - mu), -1, keepdims=True)
    return ((xf - mu) * lax.rsqrt(var + LN_EPS) * g + b).astype(x.dtype)

def rotary_tables(seq):
    inv = ROPE_THETA ** (-jnp.arange(0, ROT_DIM, 2, dtype=jnp.float32) / ROT_DIM)
    ang = jnp.arange(seq, dtype=jnp.float32)[:, None] * inv[None, :]
    return jnp.cos(ang), jnp.sin(ang)

def apply_partial_rope(t, cos, sin):
    half = ROT_DIM // 2
    shape = (1, cos.shape[0]) + (1,) * (t.ndim - 3) + (half,)
    c = cos.reshape(shape).astype(t.dtype)
    s = sin.reshape(shape).astype(t.dtype)
    r1, r2, rest = t[..., :half], t[..., half:ROT_DIM], t[..., ROT_DIM:]
    return jnp.concatenate([r1 * c - r2 * s, r1 * s + r2 * c, rest], axis=-1)

def diff_attention(x, w_qkv, w_o, lq1, lk1, lq2, lk2, sub_g, lambda_init, cos, sin):
    B, S, _ = x.shape
    qkv = x @ w_qkv
    q, k, v = jnp.split(qkv, [QK_WIDTH, 2 * QK_WIDTH], axis=-1)
    q = apply_partial_rope(q.reshape(B, S, N_HEADS, 2, HEAD_DIM), cos, sin)
    k = apply_partial_rope(k.reshape(B, S, N_HEADS, 2, HEAD_DIM), cos, sin)
    q = q.transpose(0, 2, 3, 1, 4)
    k = k.transpose(0, 2, 3, 1, 4)
    v = v.reshape(B, S, N_HEADS, V_DIM).transpose(0, 2, 1, 3)
    lam = (jnp.exp(jnp.sum(lq1 * lk1).astype(jnp.float32))
           - jnp.exp(jnp.sum(lq2 * lk2).astype(jnp.float32)) + lambda_init)
    scale = HEAD_DIM ** -0.5
    outs = []
    for blk in range(S // Q_BLOCK):
        lo, hi = blk * Q_BLOCK, (blk + 1) * Q_BLOCK
        qb = q[:, :, :, lo:hi]
        kb = k[:, :, :, :hi]
        vb = v[:, :, :hi]
        s = jnp.einsum('bhmqd,bhmkd->bhmqk', qb, kb).astype(jnp.float32) * scale
        mask = jnp.arange(lo, hi)[:, None] >= jnp.arange(hi)[None, :]
        p = jax.nn.softmax(jnp.where(mask, s, -jnp.inf), axis=-1)
        a = (p[:, :, 0] - lam * p[:, :, 1]).astype(v.dtype)
        outs.append(jnp.einsum('bhqk,bhkd->bhqd', a, vb))
    o = jnp.concatenate(outs, axis=2).astype(jnp.float32)
    o = o * lax.rsqrt(jnp.mean(jnp.square(o), -1, keepdims=True) + SUBLN_EPS) * sub_g
    o = (o * (1.0 - lambda_init)).astype(x.dtype)
    o = o.transpose(0, 2, 1, 3).reshape(B, S, N_HEADS * V_DIM)
    return o @ w_o

def pool_mixer(x, w_in, w_grp, ls, w_out):
    B, S, _ = x.shape
    u = (x @ w_in).reshape(B, S, N_POOL_GROUPS, POOL_GROUP_DIM)
    count = jnp.arange(1, S + 1, dtype=jnp.float32)
    feats = []
    for g, w in enumerate(POOL_WINDOWS):
        ug = u[:, :, g].astype(jnp.float32)
        cs = jnp.cumsum(ug, axis=1)
        lag = jnp.pad(cs[:, :S - w], ((0, 0), (w, 0), (0, 0)))
        mean = (cs - lag) / jnp.minimum(count, float(w))[None, :, None]
        feats.append(mean - ug)
    p = jnp.stack(feats, axis=2).astype(x.dtype)
    y = jnp.einsum('bsgc,gcd->bsgd', p, w_grp).reshape(B, S, D_MODEL) * ls
    return y @ w_out

def hier_moe(x, w_grp_router, b_grp_router, w_exp_router, b_exp_router, w_gate, w_up, w_down):
    B, S, D = x.shape
    N = B * S
    xf = x.reshape(N, D)
    g_logits = (xf @ w_grp_router + b_grp_router).astype(jnp.float32)
    g_idx = jnp.argmax(g_logits, axis=-1)
    g_p = jnp.take_along_axis(jax.nn.softmax(g_logits, -1), g_idx[:, None], -1)
    e_logits = (xf @ w_exp_router + b_exp_router).astype(jnp.float32)
    e_logits = e_logits.reshape(N, N_GROUPS, EXPERTS_PER_GROUP)
    e_in = jnp.take_along_axis(e_logits, g_idx[:, None, None], axis=1)[:, 0]
    top_v, top_i = lax.top_k(e_in, TOP_K)
    gate = g_p * jax.nn.softmax(top_v, axis=-1)
    expert_id = g_idx[:, None] * EXPERTS_PER_GROUP + top_i
    A = N * TOP_K
    eid = expert_id.reshape(A)
    tok = jnp.repeat(jnp.arange(N, dtype=jnp.int32), TOP_K)
    wts = gate.reshape(A)
    order = jnp.argsort(eid)
    eid_s, tok_s, w_s = eid[order], tok[order], wts[order]
    counts = jnp.bincount(eid, length=N_EXPERTS)
    starts = jnp.cumsum(counts) - counts
    padded = (counts + MOE_BLOCK - 1) // MOE_BLOCK * MOE_BLOCK
    pad_ends = jnp.cumsum(padded)
    pad_starts = pad_ends - padded
    dest = pad_starts[eid_s] + jnp.arange(A) - starts[eid_s]
    P = A + N_EXPERTS * MOE_BLOCK
    NB = P // MOE_BLOCK
    tok_pad = jnp.zeros((P,), jnp.int32).at[dest].set(tok_s)
    w_pad = jnp.zeros((P,), wts.dtype).at[dest].set(w_s)
    blk_e = jnp.minimum(jnp.searchsorted(pad_ends, jnp.arange(NB) * MOE_BLOCK, side='right'),
                        N_EXPERTS - 1)
    xin = xf[tok_pad].reshape(NB, MOE_BLOCK, D)

    def run_block(args):
        xb, e = args
        h = jax.nn.silu(xb @ w_gate[e]) * (xb @ w_up[e])
        return h @ w_down[e]

    y = lax.map(run_block, (xin, blk_e)).reshape(P, D)
    out = jnp.zeros((N, D), x.dtype).at[tok_pad].add(y * w_pad[:, None].astype(y.dtype))
    return out.reshape(B, S, D)

def first_inputs(seed: int = 0) -> dict:
    key = jax.random.key(seed)
    ks = jax.random.split(key, 24)
    f32 = jnp.float32
    nrm = lambda k, shp, sc: jax.random.normal(k, shp, f32) * sc
    D = D_MODEL
    w_qk = nrm(ks[1], (N_ATTN_LAYERS, D, 2 * QK_WIDTH), D ** -0.5)
    w_v = nrm(ks[2], (N_ATTN_LAYERS, D, N_HEADS * V_DIM), D ** -0.5) * DEEPNORM_BETA
    return {
        "x": jax.random.normal(ks[0], (BATCH, SEQ, D), f32),
        "attn_w_qkv": jnp.concatenate([w_qk, w_v], axis=-1),
        "attn_w_o": nrm(ks[3], (N_ATTN_LAYERS, N_HEADS * V_DIM, D), (N_HEADS * V_DIM) ** -0.5) * DEEPNORM_BETA,
        "attn_lq1": nrm(ks[4], (N_ATTN_LAYERS, HEAD_DIM), 0.1),
        "attn_lk1": nrm(ks[5], (N_ATTN_LAYERS, HEAD_DIM), 0.1),
        "attn_lq2": nrm(ks[6], (N_ATTN_LAYERS, HEAD_DIM), 0.1),
        "attn_lk2": nrm(ks[7], (N_ATTN_LAYERS, HEAD_DIM), 0.1),
        "attn_sub_g": 1.0 + nrm(ks[8], (N_ATTN_LAYERS, V_DIM), 0.02),
        "pool_w_in": nrm(ks[9], (N_POOL_LAYERS, D, D), D ** -0.5),
        "pool_w_grp": nrm(ks[10], (N_POOL_LAYERS, N_POOL_GROUPS, POOL_GROUP_DIM, POOL_GROUP_DIM), POOL_GROUP_DIM ** -0.5),
        "pool_scale": 1.0 + nrm(ks[11], (N_POOL_LAYERS, D), 0.02),
        "pool_w_out": nrm(ks[12], (N_POOL_LAYERS, D, D), D ** -0.5) * DEEPNORM_BETA,
        "ln_g": 1.0 + nrm(ks[13], (DEPTH, 2, D), 0.02),
        "ln_b": nrm(ks[14], (DEPTH, 2, D), 0.02),
        "moe_w_grp_router": nrm(ks[15], (DEPTH, D, N_GROUPS), D ** -0.5),
        "moe_b_grp_router": nrm(ks[16], (DEPTH, N_GROUPS), ROUTER_BIAS_SCALE),
        "moe_w_exp_router": nrm(ks[17], (DEPTH, D, N_EXPERTS), D ** -0.5),
        "moe_b_exp_router": nrm(ks[18], (DEPTH, N_EXPERTS), ROUTER_BIAS_SCALE),
        "moe_w_gate": nrm(ks[19], (DEPTH, N_EXPERTS, D, D_EXPERT), D ** -0.5),
        "moe_w_up": nrm(ks[20], (DEPTH, N_EXPERTS, D, D_EXPERT), D ** -0.5),
        "moe_w_down": nrm(ks[21], (DEPTH, N_EXPERTS, D_EXPERT, D), D_EXPERT ** -0.5) * DEEPNORM_BETA,
    }

def first_block(x, attn_w_qkv, attn_w_o, attn_lq1, attn_lk1, attn_lq2, attn_lk2, attn_sub_g,
              pool_w_in, pool_w_grp, pool_scale, pool_w_out, ln_g, ln_b,
              moe_w_grp_router, moe_b_grp_router, moe_w_exp_router, moe_b_exp_router,
              moe_w_gate, moe_w_up, moe_w_down):
    cos, sin = rotary_tables(x.shape[1])
    h = x
    for i in range(DEPTH):
        j = i // N_MIXERS
        if i % N_MIXERS == 0:
            lambda_init = 0.8 - 0.6 * math.exp(-0.3 * i)
            mix = diff_attention(h, attn_w_qkv[j], attn_w_o[j], attn_lq1[j], attn_lk1[j],
                                 attn_lq2[j], attn_lk2[j], attn_sub_g[j], lambda_init, cos, sin)
        else:
            mix = pool_mixer(h, pool_w_in[j], pool_w_grp[j], pool_scale[j], pool_w_out[j])
        h = layer_norm(DEEPNORM_ALPHA * h + mix, ln_g[i, 0], ln_b[i, 0])
        ffn = hier_moe(h, moe_w_grp_router[i], moe_b_grp_router[i], moe_w_exp_router[i],
                       moe_b_exp_router[i], moe_w_gate[i], moe_w_up[i], moe_w_down[i])
        h = layer_norm(DEEPNORM_ALPHA * h + ffn, ln_g[i, 1], ln_b[i, 1])
    return h


CHUNK = 64
EPS = 1e-6
ROPE_THETA_2 = 10000.0

RET_HEADS = 4
RET_HEAD_DIM = 64
RET_WIDTH = RET_HEADS * RET_HEAD_DIM

MLA_HEADS = 8
MLA_NOPE = 64
MLA_ROPE = 32
MLA_V = 64
MLA_WIDTH = MLA_HEADS * MLA_V
MLA_Q_RANK = 256
MLA_KV_RANK = 128

GLA_HEADS = 4
GLA_DK = 32
GLA_DV = 64
GLA_KWIDTH = GLA_HEADS * GLA_DK
GLA_WIDTH = GLA_HEADS * GLA_DV
GLA_GATE_RANK = 16
GLA_TAU = 16.0

MIX_WIDTH = RET_WIDTH + MLA_WIDTH + GLA_WIDTH

RET_SPLIT = (RET_WIDTH, RET_WIDTH, RET_WIDTH, RET_WIDTH)
MLA_SPLIT = (MLA_Q_RANK, MLA_KV_RANK, MLA_ROPE, MLA_WIDTH)
GLA_SPLIT = (GLA_KWIDTH, GLA_KWIDTH, GLA_WIDTH, GLA_GATE_RANK, GLA_WIDTH)
IN_COLS = sum(RET_SPLIT) + sum(MLA_SPLIT) + sum(GLA_SPLIT)


def rms_norm(x, w=None):
    xf = x.astype(jnp.float32)
    y = xf * lax.rsqrt(jnp.mean(xf * xf, axis=-1, keepdims=True) + EPS)
    if w is not None:
        y = y * w.astype(jnp.float32)
    return y.astype(x.dtype)

def split_cols(t, sizes):
    cuts = [int(s) for s in np.cumsum(sizes)[:-1]]
    return jnp.split(t, cuts, axis=-1)

def to_heads(t, n_heads):
    b, s, _ = t.shape
    return t.reshape(b, s, n_heads, -1)

def rope(x, pos):
    half = x.shape[-1] // 2
    inv = ROPE_THETA_2 ** (-jnp.arange(half, dtype=jnp.float32) / half)
    ang = pos.astype(jnp.float32)[..., None] * inv
    cos = jnp.cos(ang)[:, :, None, :]
    sin = jnp.sin(ang)[:, :, None, :]
    x1 = x[..., :half].astype(jnp.float32)
    x2 = x[..., half:].astype(jnp.float32)
    out = jnp.concatenate([x1 * cos - x2 * sin, x2 * cos + x1 * sin], axis=-1)
    return out.astype(x.dtype)

def chunk_states(u, a):
    u_t = jnp.moveaxis(u, 1, 0)
    a_t = jnp.moveaxis(a, 1, 0)

    def step(s, inp):
        ui, ai = inp
        return ai[..., None] * s + ui, s

    _, s_prev = lax.scan(step, jnp.zeros_like(u_t[0]), (u_t, a_t))
    return jnp.moveaxis(s_prev, 0, 1)

def retention(q, k, v):
    b, s, h, d = q.shape
    dv = v.shape[-1]
    nc = s // CHUNK
    f32 = jnp.float32
    log_gamma = jnp.log1p(-jnp.exp2(-5.0 - jnp.arange(h, dtype=f32)))
    q = q.astype(f32).reshape(b, nc, CHUNK, h, d)
    k = k.astype(f32).reshape(b, nc, CHUNK, h, d) * (d ** -0.5)
    v = v.astype(f32).reshape(b, nc, CHUNK, h, dv)
    idx = jnp.arange(CHUNK, dtype=f32)
    decay = jnp.exp(log_gamma[:, None, None] * jnp.abs(idx[:, None] - idx[None, :]))
    scores = jnp.einsum('bnihd,bnjhd->bnhij', q, k) * decay
    intra = jnp.einsum('bnhij,bnjhe->bnihe', scores, v)
    k_w = jnp.exp((CHUNK - 1.0 - idx)[:, None] * log_gamma[None, :])
    u = jnp.einsum('bnjhd,jh,bnjhe->bnhde', k, k_w, v)
    a = jnp.broadcast_to(jnp.exp(CHUNK * log_gamma)[:, None], (b, nc, h, d))
    s_prev = chunk_states(u, a)
    q_w = jnp.exp((idx + 1.0)[:, None] * log_gamma[None, :])
    inter = jnp.einsum('bnihd,ih,bnhde->bnihe', q, q_w, s_prev)
    return (intra + inter).reshape(b, s, h, dv)

def mla(q_lat, kv_lat, k_rope, q_norm_w, w_uq, kv_norm_w, w_ukv, pos):
    b, s, _ = q_lat.shape
    q = (rms_norm(q_lat, q_norm_w) @ w_uq).reshape(b, s, MLA_HEADS, MLA_NOPE + MLA_ROPE)
    q_nope = q[..., :MLA_NOPE]
    q_pe = rope(q[..., MLA_NOPE:], pos)
    kv = (rms_norm(kv_lat, kv_norm_w) @ w_ukv).reshape(b, s, MLA_HEADS, MLA_NOPE + MLA_V)
    k_nope = kv[..., :MLA_NOPE]
    v = kv[..., MLA_NOPE:]
    k_pe = rope(k_rope[:, :, None, :], pos)[:, :, 0, :]
    scale = (MLA_NOPE + MLA_ROPE) ** -0.5
    key_chunk = jnp.arange(s) // CHUNK
    nb = s // Q_BLOCK
    qn_b = jnp.moveaxis(q_nope.reshape(b, nb, Q_BLOCK, MLA_HEADS, MLA_NOPE), 1, 0)
    qp_b = jnp.moveaxis(q_pe.reshape(b, nb, Q_BLOCK, MLA_HEADS, MLA_ROPE), 1, 0)
    starts = jnp.arange(nb, dtype=jnp.int32) * Q_BLOCK

    def block(args):
        qn, qp, i0 = args
        sc = (jnp.einsum('bqhd,bkhd->bhqk', qn, k_nope)
              + jnp.einsum('bqhd,bkd->bhqk', qp, k_pe)).astype(jnp.float32) * scale
        q_chunk = (i0 + jnp.arange(Q_BLOCK)) // CHUNK
        mask = key_chunk[None, :] <= q_chunk[:, None]
        sc = jnp.where(mask, sc, -jnp.inf)
        p = jax.nn.softmax(sc, axis=-1).astype(v.dtype)
        return jnp.einsum('bhqk,bkhe->bqhe', p, v)

    out = lax.map(block, (qn_b, qp_b, starts))
    return jnp.moveaxis(out, 0, 1).reshape(b, s, MLA_WIDTH)

def gla(q, k, v, g_low, w_g2, b_g2):
    b, s, h, dk = q.shape
    dv = v.shape[-1]
    nc = s // CHUNK
    f32 = jnp.float32
    log_a = jax.nn.log_sigmoid((g_low @ w_g2 + b_g2).astype(f32)) / GLA_TAU
    cum = jnp.cumsum(log_a.reshape(b, nc, CHUNK, h, dk), axis=2)
    q = q.astype(f32).reshape(b, nc, CHUNK, h, dk)
    k = k.astype(f32).reshape(b, nc, CHUNK, h, dk) * (dk ** -0.5)
    v = v.astype(f32).reshape(b, nc, CHUNK, h, dv)
    e_pos = jnp.exp(cum)
    e_neg = jnp.exp(-cum)
    q_pos = q * e_pos
    past = jnp.einsum('bnihd,bnjhd->bnhij', q_pos, k * e_neg)
    fut = jnp.einsum('bnihd,bnjhd->bnhij', q * e_neg, k * e_pos)
    idx = jnp.arange(CHUNK)
    attn = jnp.where(idx[:, None] >= idx[None, :], past, fut)
    intra = jnp.einsum('bnhij,bnjhe->bnihe', attn, v)
    last = cum[:, :, -1]
    u = jnp.einsum('bnjhd,bnjhe->bnhde', k * jnp.exp(last[:, :, None] - cum), v)
    s_prev = chunk_states(u, jnp.exp(last))
    inter = jnp.einsum('bnihd,bnhde->bnihe', q_pos, s_prev)
    return (intra + inter).reshape(b, s, h, dv)

def second_inputs(seed: int = 0) -> dict:
    key = jax.random.key(seed)
    ks = jax.random.split(key, 16)
    f32 = jnp.float32

    def normal(k, shape, scale):
        return jax.random.normal(k, shape, f32) * scale

    def gain(k, shape):
        return 1.0 + 0.02 * jax.random.normal(k, shape, f32)

    x = normal(ks[0], (BATCH, SEQ, D_MODEL), 1.0)
    c = normal(ks[1], (BATCH, D_MODEL), 1.0)
    offset = jax.random.randint(ks[2], (BATCH, 1), 0, 4096, dtype=jnp.int32)
    positions = offset + jnp.arange(SEQ, dtype=jnp.int32)[None, :]
    norm_w = gain(ks[3], (DEPTH, D_MODEL))
    ada_w = normal(ks[4], (DEPTH, D_MODEL, 3 * D_MODEL), 0.5 * D_MODEL ** -0.5)
    ada_b = normal(ks[5], (DEPTH, 3 * D_MODEL), 0.02)
    w_in = normal(ks[6], (DEPTH, D_MODEL, IN_COLS), D_MODEL ** -0.5)
    mla_q_norm = gain(ks[7], (DEPTH, MLA_Q_RANK))
    w_uq = normal(ks[8], (DEPTH, MLA_Q_RANK, MLA_HEADS * (MLA_NOPE + MLA_ROPE)), MLA_Q_RANK ** -0.5)
    mla_kv_norm = gain(ks[9], (DEPTH, MLA_KV_RANK))
    w_ukv = normal(ks[10], (DEPTH, MLA_KV_RANK, MLA_HEADS * (MLA_NOPE + MLA_V)), MLA_KV_RANK ** -0.5)
    gla_w_g2 = normal(ks[11], (DEPTH, GLA_GATE_RANK, GLA_KWIDTH), GLA_GATE_RANK ** -0.5)
    gla_b_g2 = normal(ks[12], (DEPTH, GLA_KWIDTH), 0.02)
    gla_norm = gain(ks[13], (DEPTH, GLA_DV))
    w_out = normal(ks[14], (DEPTH, MIX_WIDTH, D_MODEL), MIX_WIDTH ** -0.5)
    final_norm = gain(ks[15], (D_MODEL,))
    return {"x": x, "c": c, "positions": positions, "norm_w": norm_w, "ada_w": ada_w,
            "ada_b": ada_b, "w_in": w_in, "mla_q_norm": mla_q_norm, "w_uq": w_uq,
            "mla_kv_norm": mla_kv_norm, "w_ukv": w_ukv, "gla_w_g2": gla_w_g2,
            "gla_b_g2": gla_b_g2, "gla_norm": gla_norm, "w_out": w_out,
            "final_norm": final_norm}

def second_block(x, c, positions, norm_w, ada_w, ada_b, w_in, mla_q_norm, w_uq, mla_kv_norm,
              w_ukv, gla_w_g2, gla_b_g2, gla_norm, w_out, final_norm):
    b, s, _ = x.shape
    c_act = jax.nn.silu(c)
    for l in range(DEPTH):
        shift, scale, gate = jnp.split(c_act @ ada_w[l] + ada_b[l], 3, axis=-1)
        h = rms_norm(x, norm_w[l]) * (1.0 + scale[:, None, :]) + shift[:, None, :]
        proj = h @ w_in[l]
        ret_p, mla_p, gla_p = split_cols(proj, (sum(RET_SPLIT), sum(MLA_SPLIT), sum(GLA_SPLIT)))

        rq, rk, rv, rz = split_cols(ret_p, RET_SPLIT)
        r_o = retention(rope(to_heads(rq, RET_HEADS), positions),
                        rope(to_heads(rk, RET_HEADS), positions),
                        to_heads(rv, RET_HEADS))
        r_o = rms_norm(r_o).astype(x.dtype).reshape(b, s, RET_WIDTH)

        mq, mkv, mkr, mz = split_cols(mla_p, MLA_SPLIT)
        m_o = mla(mq, mkv, mkr, mla_q_norm[l], w_uq[l], mla_kv_norm[l], w_ukv[l], positions)

        gq, gk, gv, gg, gz = split_cols(gla_p, GLA_SPLIT)
        g_o = gla(to_heads(gq, GLA_HEADS), to_heads(gk, GLA_HEADS), to_heads(gv, GLA_HEADS),
                  gg, gla_w_g2[l], gla_b_g2[l])
        g_o = rms_norm(g_o, gla_norm[l]).astype(x.dtype).reshape(b, s, GLA_WIDTH)

        mixed = jnp.concatenate([r_o * jax.nn.silu(rz), m_o * jax.nn.silu(mz),
                                 g_o * jax.nn.silu(gz)], axis=-1)
        x = x + gate[:, None, :] * (mixed @ w_out[l])
    return rms_norm(x, final_norm)


def setup_inputs(seed=0):
    out = dict(first_inputs(seed))
    for name, value in second_inputs(seed + 1).items():
        if name != "x":
            out[name + "_2"] = value
    return out


def reference(
    x, attn_w_qkv, attn_w_o, attn_lq1, attn_lk1, attn_lq2, attn_lk2, attn_sub_g, pool_w_in,
    pool_w_grp, pool_scale, pool_w_out, ln_g, ln_b, moe_w_grp_router, moe_b_grp_router,
    moe_w_exp_router, moe_b_exp_router, moe_w_gate, moe_w_up, moe_w_down, c_2, positions_2,
    norm_w_2, ada_w_2, ada_b_2, w_in_2, mla_q_norm_2, w_uq_2, mla_kv_norm_2, w_ukv_2,
    gla_w_g2_2, gla_b_g2_2, gla_norm_2, w_out_2, final_norm_2,
):
    x = first_block(
        x, attn_w_qkv, attn_w_o, attn_lq1, attn_lk1, attn_lq2, attn_lk2, attn_sub_g, pool_w_in,
        pool_w_grp, pool_scale, pool_w_out, ln_g, ln_b, moe_w_grp_router, moe_b_grp_router,
        moe_w_exp_router, moe_b_exp_router, moe_w_gate, moe_w_up, moe_w_down,
    )
    return second_block(
        x, c_2, positions_2, norm_w_2, ada_w_2, ada_b_2, w_in_2, mla_q_norm_2, w_uq_2,
        mla_kv_norm_2, w_ukv_2, gla_w_g2_2, gla_b_g2_2, gla_norm_2, w_out_2, final_norm_2,
    )


_drawn_inputs = setup_inputs


def setup_inputs(seed=0):
    import zlib

    import numpy as np

    out = dict(_drawn_inputs(seed))
    spreads = {}
    factors = {'attn_lk1': 3.566,
     'attn_lq2': 4.2,
     'attn_sub_g': 4.379,
     'pool_scale': 6.112,
     'moe_b_grp_router': 6.973,
     'moe_b_exp_router': 5.045,
     'norm_w_2': 6.9,
     'ada_b_2': 2.87,
     'mla_q_norm_2': 8.0,
     'w_uq_2': 2.723,
     'mla_kv_norm_2': 8.0,
     'gla_b_g2_2': 8.0,
     'gla_norm_2': 8.0,
     'final_norm_2': 2.874}
    for name, (base, spread) in spreads.items():
        noise = np.random.default_rng([zlib.crc32(name.encode()), seed]).standard_normal(out[name].shape)
        drawn = base * np.exp(spread * noise) if base else spread * noise
        out[name] = jnp.asarray(drawn.astype(out[name].dtype))
    for name, factor in factors.items():
        out[name] = (out[name] * factor).astype(out[name].dtype)
    return out
```

```python
import math
from contextlib import ExitStack

import numpy as np
import concourse.bass as bass
from concourse import mybir

F32 = mybir.dt.float32
I32 = mybir.dt.int32
ALU = mybir.AluOpType
ACT = mybir.ActivationFunctionType
AX = mybir.AxisListType

P = 128
SEQ = 1024
D = 1024
TILES = SEQ // P
KC = D // P
HALF = 512

HEADS = 8
HD = 64
VD = 2 * HD
QKV = 3 * D
ROT = HD // 4
LAMBDA_INIT = 0.8 - 0.6 * math.exp(0.0)
ALPHA = 4 ** 0.25
LN_EPS = 1e-5
RMS_EPS = 1e-6
NEG = -1.0e30

GROUPS, PER_GROUP = 4, 8
EXPERTS = GROUPS * PER_GROUP
DE = D // 2
OVER = 2 * SEQ // P
BLOCKS = EXPERTS + OVER
BCOLS = BLOCKS + 2
POOL_WINDOWS = (2, 4, 8, 16)
PG = D // len(POOL_WINDOWS)

RH, RD = 4, 64
MH, NOPE, ROPE_D, MV = 8, 64, 32, 64
MQ = NOPE + ROPE_D
MQR, MKVR = 256, 128
GH, GDK, GDV, GRANK = 4, 32, 64, 16
CH = 64
COLS = {}
_at = 0
for _n, _w in (("rq", 256), ("rk", 256), ("rv", 256), ("rz", 256), ("mq", 256), ("mkv", 128), ("mkr", 32),
               ("mz", 512), ("gq", 128), ("gk", 128), ("gv", 256), ("gg", 16), ("gz", 256)):
    COLS[_n] = (_at, _at + _w)
    _at += _w
IN_COLS = _at
NCHUNK = 6
CW = IN_COLS // NCHUNK


def constant_parts():
    p = np.arange(P)[:, None]
    c = np.arange(P)[None, :]
    f = np.float32
    parts = {
        "ident": (p == c).astype(f),
        "causal": np.where(c > p, f(NEG), f(0)),
        "chunked": np.where((c >= CH) & (p < CH), f(NEG), f(0)),
        "before": (p < c).astype(f),
        "iota": np.broadcast_to(np.arange(P, dtype=f), (P, P)),
        "token": (p + P * np.arange(TILES)[None, :]).astype(f),
    }
    inv = f(500000.0) ** (-np.arange(0, ROT, 2, dtype=f) / f(ROT))
    ang = np.arange(SEQ, dtype=f)[:, None] * inv[None, :].astype(f)
    for name, t in (("rcos", np.cos(ang)), ("rsin", np.sin(ang))):
        parts[name] = t.astype(f).reshape(TILES, P, ROT // 2).transpose(1, 0, 2).reshape(P, -1)
    parts["inv"] = np.broadcast_to(f(10000.0) ** (-np.arange(RD // 2, dtype=f) / f(RD // 2)), (P, RD // 2))
    t = np.arange(SEQ)
    parts["invcount"] = np.concatenate(
        [np.broadcast_to((1.0 / np.minimum(t + 1, w)).astype(f), (P, SEQ)) for w in POOL_WINDOWS], axis=1)
    lg = np.log1p(-np.exp2(-5.0 - np.arange(RH, dtype=f))).astype(np.float64)
    j, i = np.arange(P)[:, None, None] % CH, np.arange(CH)[None, None, :]
    scale = RD ** -0.5
    parts["decay"] = (np.exp(lg[None, :, None] * np.abs(i - j)) * scale).reshape(P, -1)
    head = 2 * np.arange(2)[None, :, None] + (np.arange(P) // RD)[:, None, None]
    parts["rqw"] = np.exp(lg[head] * (np.arange(P)[None, None, :] % CH + 1.0)).reshape(P, -1)
    parts["rkw"] = np.exp(lg[None, :] * (CH - 1.0 - np.arange(P)[:, None] % CH)) * scale
    parts["ra"] = np.exp(CH * lg[head[:, :, 0]])
    parts["rbd"] = (p // RD == c // RD).astype(f)
    parts["gbd"] = (p // GDK == np.arange(GH * GDV)[None, :] // GDV).astype(f)
    parts["ghead"] = (p // GDK == np.arange(GH)[None, :]).astype(f)
    parts["scan"] = np.broadcast_to((np.arange(P) % CH != 0).astype(f), (P, P))
    parts["past"] = (np.arange(CH)[None, :] >= p % CH).astype(f)
    return {n: np.ascontiguousarray(a, dtype=f) for n, a in parts.items()}


class Phase:

    def __init__(self, nc, name):
        self.nc, self.name = nc, name

    def __enter__(self):
        self.stack = ExitStack()
        self.sems = []
        return self

    def sb(self, name, shape, dt=F32):
        return self.stack.enter_context(self.nc.sbuf_tensor(f"{self.name}_{name}", shape, dt))

    def ps(self, name, shape):
        return self.stack.enter_context(self.nc.psum_tensor(f"{self.name}_{name}", shape, F32))

    def sem(self, name):
        s = self.nc.alloc_semaphore(f"{self.name}_{name}")
        self.sems.append(s)
        return s

    def __exit__(self, *exc):
        self.stack.close()
        if exc[0] is None:
            self.nc.clear_and_free_semaphores(self.sems)
            self.nc.all_engine_barrier()


class Chain:

    def __init__(self, eng, sem, base=0):
        self.eng, self.sem, self.base, self.n = eng, sem, base, 0

    def __call__(self, ins):
        self.n += 1
        ins.then_inc(self.sem, 1)
        return ins

    def wait(self):
        self.eng.wait_ge(self.sem, self.base + self.n)


def rows(ap, i):
    return ap[i * P:(i + 1) * P, :] if isinstance(i, int) else ap[bass.ds(i * P, P), :]


SETTLED = []


def settle(eng):
    eng.sem_inc(SETTLED[-1], 1)


def phase_qkv(nc, K, x, w_qkv, qkv, y=None):
    with Phase(nc, "qkv") as ph:
        w = ph.sb("w", [P, KC, QKV])
        xin = ph.sb("x", [P, D])
        xT = ph.sb("xT", [P, KC, P])
        row = ph.sb("row", [P, QKV])
        t1 = ph.sb("t1", [P, 4, 32, ROT // 2])
        tp = ph.ps("tp", [P, 2, 4, P])
        acc = ph.ps("acc", [P, NCHUNK, HALF])
        w_in, x_in, tp_ready, xT_ready = (ph.sem(n) for n in ("w_in", "x_in", "tp_ready", "xT_ready"))
        acc_ready, row_ready, stored, rope = (ph.sem(n) for n in ("acc_ready", "row_ready", "stored", "rope"))
        rot_done, zero_set, zeroed = ph.sem("rot_done"), ph.sem("zero_set"), ph.sem("zeroed")
        zero = ph.sb("zero", [P, D])

        with nc.Block() as block:
            @block.sync
            def _(sp):
                sp.dma_start(xin[:, :], x[0:P, :]).then_inc(x_in, 16)
                for k in range(KC):
                    sp.dma_start(w[:, k, :], w_qkv[k * P:(k + 1) * P, :]).then_inc(w_in, 16)

                sp.wait_ge(zero_set, 1)
                if y is not None:
                    for b in range(EXPERTS, BLOCKS):
                        sp.dma_start(y[b * P:(b + 1) * P, :], zero[:, :]).then_inc(zeroed, 16)

                def store(i):
                    sp.wait_ge(rot_done, i + 1)
                    sp.dma_start(rows(qkv, i), row[:, :]).then_inc(stored, 16)

                with sp.Fori(0, TILES - 1) as i:
                    sp.wait_ge(tp_ready, 2 * i + 2)
                    sp.dma_start(xin[:, :], rows(x, i + 1)).then_inc(x_in, 16)
                    store(i)
                store(TILES - 1)
                sp.wait_ge(stored, 16 * (TILES + 1))
                if y is not None:
                    sp.wait_ge(zeroed, 16 * OVER)

            @block.gpsimd
            def _(pool):
                pool.memset(zero[:, :], 0.0).then_inc(zero_set, 1)

            @block.tensor
            def _(pe):
                with pe.Fori(0, TILES) as i:
                    pe.wait_ge(x_in, 16 * i + 16)
                    for b in range(2):
                        for k in range(4):
                            last = nc.tensor.transpose(tp[:, b, k, :], xin[:, (4 * b + k) * P:(4 * b + k + 1) * P],
                                                       K["ident"])
                        last.then_inc(tp_ready, 1)
                    pe.wait_ge(w_in, 16 * KC)
                    pe.wait_ge(xT_ready, 2 * i + 2)
                    for c in range(NCHUNK):
                        pe.wait_ge(row_ready, NCHUNK * i + c + 1)
                        for k in range(KC):
                            last = nc.tensor.matmul(acc[:, c, :], xT[:, k, :], w[:, k, c * HALF:(c + 1) * HALF],
                                                    start=(k == 0), stop=(k == KC - 1))
                        last.then_inc(acc_ready, 1)

            @block.scalar
            def _(act):
                for _ in range(NCHUNK):
                    act.sem_inc(row_ready, 1)
                act.sem_inc(stored, 16)
                with act.Fori(0, TILES) as i:
                    for b in range(2):
                        act.wait_ge(tp_ready, 2 * i + b + 1)
                        act.copy(xT[:, 4 * b:4 * b + 4, :], tp[:, b, :, :]).then_inc(xT_ready, 1)
                    for c in range(NCHUNK):
                        act.wait_ge(acc_ready, NCHUNK * i + c + 1)
                        if c == 0:
                            act.wait_ge(stored, 16 * i + 16)
                        act.copy(row[:, c * HALF:(c + 1) * HALF], acc[:, c, :]).then_inc(row_ready, 1)

            @block.vector
            def _(dve):
                g = row[:, 0:2 * D].rearrange("p (h d) -> p h d", d=HD)
                r1, r2 = g[:, :, 0:ROT // 2], g[:, :, ROT // 2:ROT]
                with dve.Fori(0, TILES) as i:
                    ch = Chain(dve, rope, 5 * i)
                    cos = K["rcos"].rearrange("p (t c) -> p t c", t=TILES)[:, bass.ds(i, 1), :].to_broadcast([P, 32, ROT // 2])
                    sin = K["rsin"].rearrange("p (t c) -> p t c", t=TILES)[:, bass.ds(i, 1), :].to_broadcast([P, 32, ROT // 2])
                    dve.wait_ge(row_ready, NCHUNK * (i + 1) + 4)
                    ch(dve.tensor_tensor(t1[:, 0], r1, cos, ALU.mult))
                    ch(dve.tensor_tensor(t1[:, 1], r2, sin, ALU.mult))
                    ch(dve.tensor_tensor(t1[:, 2], r1, sin, ALU.mult))
                    ch(dve.tensor_tensor(t1[:, 3], r2, cos, ALU.mult))
                    ch.wait()
                    ch(dve.tensor_tensor(r1, t1[:, 0], t1[:, 1], ALU.subtract))
                    dve.wait_ge(row_ready, NCHUNK * (i + 2))
                    dve.tensor_tensor(r2, t1[:, 2], t1[:, 3], ALU.add).then_inc(rot_done, 1)


def evens(n):
    return (n + 3) // 4


def phase_attention(nc, K, name, q, k, v, out, maps, dk, dv, mask, scale, lam_parts=None, sub_g=None):
    dq = maps * dk
    U = TILES * maps
    groups = [evens(i + 1) for i in range(TILES)]
    G = 4 + sum(groups)
    diff = maps == 2
    with Phase(nc, name) as ph:
        qs, ks, vs = ph.sb("q", [P, TILES, dq]), ph.sb("k", [P, TILES, dq]), ph.sb("v", [P, TILES, dv])
        qT, kT = ph.sb("qT", [dq, SEQ]), ph.sb("kT", [dq, SEQ])
        prob = ph.sb("prob", [P, 2, maps, SEQ])
        aT = ph.sb("aT", [P, TILES, P])
        o_sb = ph.sb("o", [P, TILES, dv])
        mx, bias, total, inv = (ph.sb(n, [P, U]) for n in ("mx", "bias", "total", "inv"))
        s_ps = ph.ps("s", [P, 2, SEQ])
        tp = ph.ps("tp", [P, 2, 4, P])
        o_ps = ph.ps("o_ps", [P, 2, HALF])
        qk_in, v_in, tp_ready, tp_copied, s_ready, exp_done, bias_ready, a_ready, o_ready, o_done, stored, own = (
            ph.sem(n) for n in ("qk_in", "v_in", "tp_ready", "tp_copied", "s_ready", "exp_done", "bias_ready",
                                "a_ready", "o_ready", "o_done", "stored", "own"))
        out_ready = o_done
        if diff:
            lq = ph.sb("lq", [P, 4, HD])
            lt = ph.sb("lt", [P, 2, HD])
            ls = ph.sb("ls", [P, 4])
            lam = ph.sb("lam", [P, 1])
            gsub = ph.sb("gsub", [P, dv])
            sq = ph.sb("sq", [P, TILES, dv])
            ms, rstd, half = (ph.sb(n, [P, TILES]) for n in ("ms", "rstd", "half"))
            l_in, l_sum, l_exp, ms_ready, rstd_ready, normed = (
                ph.sem(n) for n in ("l_in", "l_sum", "l_exp", "ms_ready", "rstd_ready", "normed"))
            out_ready = normed

        with nc.Block() as block:
            @block.sync
            def _(sp):
                def load_qk(h):
                    sp.dma_start(qs[:, :, :], q(h)).then_inc(qk_in, 16)
                    sp.dma_start(ks[:, :, :], k(h)).then_inc(qk_in, 16)

                def store(h):
                    if diff:
                        sp.wait_ge(normed, h + 1)
                    else:
                        sp.wait_ge(o_done, TILES * h + TILES + 2)
                    sp.dma_start(out(h), o_sb[:, :, :]).then_inc(stored, 16)

                if diff:
                    for n, part in enumerate(lam_parts):
                        sp.dma_start(lq[:, n, :], part.partition_broadcast(P)).then_inc(l_in, 16)
                    sp.dma_start(gsub[:, :], sub_g.partition_broadcast(P)).then_inc(l_in, 16)
                load_qk(0)
                sp.dma_start(vs[:, :, :], v(0)).then_inc(v_in, 16)
                with sp.Fori(0, HEADS - 1) as h:
                    sp.wait_ge(tp_ready, G * h + 4)
                    load_qk(h + 1)
                    sp.wait_ge(o_ready, TILES * h + TILES)
                    sp.dma_start(vs[:, :, :], v(h + 1)).then_inc(v_in, 16)
                    store(h)
                store(HEADS - 1)
                sp.wait_ge(stored, 16 * (HEADS + 1))

            @block.tensor
            def _(pe):
                with pe.Fori(0, HEADS) as h:
                    g = 0

                    def group(pieces):
                        nonlocal g
                        pe.wait_ge(tp_copied, G * h + g + 1)
                        for n, piece in enumerate(pieces):
                            last = nc.tensor.transpose(tp[0:piece.shape[-1], g % 2, n, :], piece, K["ident"])
                        last.then_inc(tp_ready, 1)
                        g += 1

                    def scores(i):
                        n = (i + 1) * P
                        for m in range(maps):
                            u = i * maps + m
                            pe.wait_ge(exp_done, U * h + u + 1)
                            for c in range(0, n, HALF):
                                w = min(HALF, n - c)
                                last = nc.tensor.matmul(s_ps[:, u % 2, c:c + w], qT[m * dk:(m + 1) * dk, i * P:(i + 1) * P],
                                                        kT[m * dk:(m + 1) * dk, c:c + w], start=True, stop=True)
                            last.then_inc(s_ready, 1)

                    pe.wait_ge(qk_in, 32 * h + 32)
                    for src in (qs, ks):
                        for b in range(2):
                            group([src[:, 4 * b + n, :] for n in range(4)])
                    pe.wait_ge(tp_copied, G * h + 6)
                    scores(0)
                    for i in range(TILES):
                        if i + 1 < TILES:
                            scores(i + 1)
                        if diff:
                            pe.wait_ge(a_ready, TILES * h + i + 1)
                        else:
                            pe.wait_ge(exp_done, U * h + i + 3)
                        for b in range(groups[i]):
                            group([prob[:, i % 2, 0, j * P:(j + 1) * P] for j in range(4 * b, min(4 * b + 4, i + 1))])
                        if i == 0:
                            pe.wait_ge(v_in, 16 * h + 16)
                        pe.wait_ge(o_done, TILES * h + i + 1)
                        for j in range(i + 1):
                            if j % 4 == 0:
                                pe.wait_ge(tp_copied, G * h + g - groups[i] + j // 4 + 3)
                            last = nc.tensor.matmul(o_ps[:, i % 2, 0:dv], aT[:, j, :], vs[:, j, :],
                                                    start=(j == 0), stop=(j == i))
                        last.then_inc(o_ready, 1)

            @block.scalar
            def _(act):
                for _ in range(2):
                    act.sem_inc(tp_copied, 1)
                    act.sem_inc(exp_done, 1)
                if diff:
                    act.wait_ge(l_sum, 1)
                    act.activation(ls[:, 2:4], ls[:, 0:2], ACT.Exp).then_inc(l_exp, 1)
                with act.Fori(0, HEADS) as h:
                    g = 0

                    def copy_group(dst, n, rows_):
                        nonlocal g
                        act.wait_ge(tp_ready, G * h + g + 1)
                        act.copy(dst, tp[0:rows_, g % 2, 0:n, :]).then_inc(tp_copied, 1)
                        g += 1

                    def exps(i):
                        n = (i + 1) * P
                        for m in range(maps):
                            u = i * maps + m
                            act.wait_ge(bias_ready, U * h + u + 1)
                            act.activation(prob[:, i % 2, m, 0:n], s_ps[:, u % 2, 0:n], ACT.Exp, bias=bias[:, u:u + 1],
                                           scale=scale, accum_out=total[:, u:u + 1]).then_inc(exp_done, 1)

                    for dst in (qT, kT):
                        for b in range(2):
                            copy_group(dst[:, b * HALF:(b + 1) * HALF].rearrange("p (n c) -> p n c", n=4), 4, dq)
                    exps(0)
                    for i in range(TILES):
                        for b in range(groups[i]):
                            n = min(4, i + 1 - 4 * b)
                            copy_group(aT[:, 4 * b:4 * b + n, :], n, P)
                        if i + 1 < TILES:
                            exps(i + 1)

            @block.vector
            def _(dve):
                dve.sem_inc(o_done, 1)
                dve.sem_inc(o_done, 1)
                first = 0
                if diff:
                    ch = Chain(dve, own)
                    dve.wait_ge(l_in, 16 * 5)
                    ch(dve.tensor_tensor(lt[:, 0], lq[:, 0], lq[:, 1], ALU.mult))
                    ch(dve.tensor_tensor(lt[:, 1], lq[:, 2], lq[:, 3], ALU.mult))
                    ch(dve.tensor_scalar(gsub[:, :], gsub[:, :], 1.0 - LAMBDA_INIT, None, ALU.mult))
                    ch.wait()
                    dve.reduce_sum(ls[:, 0:2], lt[:, :, :], axis=AX.X).then_inc(l_sum, 1)
                    dve.wait_ge(l_exp, 1)
                    ch(dve.tensor_tensor(lam[:, :], ls[:, 2:3], ls[:, 3:4], ALU.subtract))
                    ch.wait()
                    ch(dve.tensor_scalar(lam[:, :], lam[:, :], LAMBDA_INIT, None, ALU.add))
                    ch.wait()
                    first = ch.n
                per_head = 2 * U + (3 * TILES + 3 if diff else TILES)
                dve.sem_inc(stored, 16)
                with dve.Fori(0, HEADS) as h:
                    ch = Chain(dve, own, per_head * h + first)

                    def biases(i):
                        n = (i + 1) * P
                        for m in range(maps):
                            u = i * maps + m
                            dve.wait_ge(s_ready, U * h + u + 1)
                            ch(dve.tensor_tensor(s_ps[:, u % 2, n - P:n], s_ps[:, u % 2, n - P:n], mask, ALU.add))
                            ch.wait()
                            ch(dve.reduce_max(mx[:, u:u + 1], s_ps[:, u % 2, 0:n], axis=AX.X))
                            ch.wait()
                            dve.tensor_scalar(bias[:, u:u + 1], mx[:, u:u + 1], -scale, None, ALU.mult).then_inc(bias_ready, 1)

                    def combine(i):
                        n = (i + 1) * P
                        u = i * maps
                        dve.wait_ge(exp_done, U * h + u + maps + 2)
                        ch(dve.reciprocal(inv[:, u:u + maps], total[:, u:u + maps]))
                        if diff:
                            ch.wait()
                            ch(dve.tensor_tensor(inv[:, u + 1:u + 2], inv[:, u + 1:u + 2], lam[:, :], ALU.mult))
                            ch.wait()
                            ch(dve.tensor_scalar(prob[:, i % 2, 1, 0:n], prob[:, i % 2, 1, 0:n], inv[:, u + 1:u + 2], None, ALU.mult))
                            ch.wait()
                            dve.scalar_tensor_tensor(prob[:, i % 2, 0, 0:n], prob[:, i % 2, 0, 0:n], inv[:, u:u + 1],
                                                     prob[:, i % 2, 1, 0:n], ALU.mult, ALU.subtract).then_inc(a_ready, 1)

                    def evacuate(i):
                        dve.wait_ge(o_ready, TILES * h + i + 1)
                        if i == 0:
                            dve.wait_ge(stored, 16 * h + 16)
                        if diff:
                            dve.tensor_copy(o_sb[:, i, :], o_ps[:, i % 2, 0:dv]).then_inc(o_done, 1)
                        else:
                            ch.wait()
                            dve.tensor_scalar(o_sb[:, i, :], o_ps[:, i % 2, 0:dv], inv[:, i:i + 1], None,
                                              ALU.mult).then_inc(o_done, 1)

                    biases(0)
                    for i in range(TILES):
                        combine(i)
                        if i + 1 < TILES:
                            biases(i + 1)
                        if i > 0:
                            evacuate(i - 1)
                    evacuate(TILES - 1)
                    if diff:
                        dve.wait_ge(o_done, TILES * h + TILES + 2)
                        ch(dve.tensor_tensor(sq[:, :, :], o_sb[:, :, :], o_sb[:, :, :], ALU.mult))
                        ch.wait()
                        ch(dve.reduce_sum(ms[:, :], sq[:, :, :], axis=AX.X))
                        ch.wait()
                        dve.tensor_scalar(ms[:, :], ms[:, :], 1.0 / dv, LN_EPS, ALU.mult, ALU.add).then_inc(ms_ready, 1)
                        dve.wait_ge(rstd_ready, h + 2)
                        ch(dve.tensor_tensor(o_sb[:, :, :], o_sb[:, :, :], rstd[:, :].unsqueeze(2).to_broadcast([P, TILES, dv]), ALU.mult))
                        ch.wait()
                        dve.tensor_tensor(o_sb[:, :, :], o_sb[:, :, :], gsub[:, :].unsqueeze(1).to_broadcast([P, TILES, dv]),
                                          ALU.mult).then_inc(normed, 1)
                    assert ch.n == per_head, ch.n

            if diff:
                @block.gpsimd
                def _(pool):
                    pool.memset(half[:, :], -0.5).then_inc(rstd_ready, 1)
                    pool.wait_ge(rstd_ready, 1)
                    with pool.Fori(0, HEADS) as h:
                        pool.wait_ge(ms_ready, h + 1)
                        pool.tensor_tensor(rstd[:, :], ms[:, :], half[:, :], ALU.pow).then_inc(rstd_ready, 1)


def with_constants(nc, stack, consts, body):
    parts = constant_parts()
    width = sum(a.shape[1] for a in parts.values())
    held = stack.enter_context(nc.sbuf_tensor("constants", [P, width], F32))
    K, at = {}, 0
    for name, a in parts.items():
        K[name] = held[:, at:at + a.shape[1]]
        at += a.shape[1]
    SETTLED.append(nc.alloc_semaphore("settled"))
    with Phase(nc, "load") as ph:
        loaded = ph.sem("loaded")
        with nc.Block() as block:
            @block.sync
            def _(sp):
                sp.dma_start(held[:, :], consts).then_inc(loaded, 16)
                sp.wait_ge(loaded, 16)
    body(K)


def diff_attention(nc, K, qkv, lam_parts, sub_g, mix):
    def heads(base, width, ap=None):
        return lambda h: (ap if ap is not None else qkv)[:, bass.ds(h * width + base, width)].rearrange("(t p) c -> p t c", p=P)

    phase_attention(nc, K, "diff", heads(0, VD), heads(D, VD), heads(2 * D, VD), heads(0, VD, mix), 2, HD, VD,
                    K["causal"], HD ** -0.5, lam_parts, sub_g)


def layer_norm_steps(dve, ch, r, stats, mv, ms_ready):
    for c in range(2):
        ch(dve.bn_stats(stats[:, c, :], r[:, c * HALF:(c + 1) * HALF]))
    ch.wait()
    settle(dve)
    ch(dve.bn_aggr(mv[:, :], stats[:, :, :]))
    ch.wait()
    dve.tensor_scalar(mv[:, 1:2], mv[:, 1:2], LN_EPS, None, ALU.add).then_inc(ms_ready, 1)


def phase_out_norm(nc, K, name, mix, w_out, h_in, g, b, w_gr, b_gr, w_er, b_er, h_out, logits):
    NL = GROUPS + EXPERTS
    with Phase(nc, name) as ph:
        w = ph.sb("w", [P, KC, D])
        wr = ph.sb("wr", [P, KC, NL])
        br = ph.sb("br", [P, NL])
        gb = ph.sb("gb", [P, 2, D])
        xin, res, r, hn = (ph.sb(n, [P, D]) for n in ("x", "res", "r", "hn"))
        xT, hT = ph.sb("xT", [P, KC, P]), ph.sb("hT", [P, KC, P])
        stats, mv = ph.sb("stats", [P, 2, 6]), ph.sb("mv", [P, 2])
        rstd, half = ph.sb("rstd", [P, 1]), ph.sb("half", [P, 1])
        tp = ph.ps("tp", [P, 2, 4, P])
        acc = ph.ps("acc", [P, 2, HALF])
        lg = ph.ps("lg", [P, 1, HALF])
        w_in, small_in, x_in, res_in, tp_ready, tp_copied, acc_ready, r_ready = (ph.sem(n) for n in (
            "w_in", "small_in", "x_in", "res_in", "tp_ready", "tp_copied", "acc_ready", "r_ready"))
        ms_ready, rstd_ready, h_scaled, h_ready, lg_ready, lg_done, stored, own, gown = (ph.sem(n) for n in (
            "ms_ready", "rstd_ready", "h_scaled", "h_ready", "lg_ready", "lg_done", "stored", "own", "gown"))

        with nc.Block() as block:
            @block.sync
            def _(sp):
                sp.dma_start(xin[:, :], mix[0:P, :]).then_inc(x_in, 16)
                for k in range(KC):
                    sp.dma_start(w[:, k, :], w_out[k * P:(k + 1) * P, :]).then_inc(w_in, 16)
                sp.dma_start(res[:, :], h_in[0:P, :]).then_inc(res_in, 16)
                for n, row in enumerate((g, b)):
                    sp.dma_start(gb[:, n, :], row.partition_broadcast(P)).then_inc(small_in, 16)
                sp.dma_start(wr[:, :, 0:GROUPS], w_gr.rearrange("(k p) n -> p k n", p=P)).then_inc(small_in, 16)
                sp.dma_start(wr[:, :, GROUPS:NL], w_er.rearrange("(k p) n -> p k n", p=P)).then_inc(small_in, 16)
                sp.dma_start(br[:, 0:GROUPS], b_gr.partition_broadcast(P)).then_inc(small_in, 16)
                sp.dma_start(br[:, GROUPS:NL], b_er.partition_broadcast(P)).then_inc(small_in, 16)

                def turn(i, transposed):
                    sp.wait_ge(tp_ready, transposed)
                    sp.dma_start(xin[:, :], rows(mix, i + 1)).then_inc(x_in, 16)
                    sp.wait_ge(r_ready, 2 * i + 4)
                    sp.dma_start(res[:, :], rows(h_in, i + 1)).then_inc(res_in, 16)
                    sp.wait_ge(h_ready, i + 1)
                    sp.dma_start(rows(h_out, i), hn[:, :]).then_inc(stored, 16)

                turn(0, 2)
                with sp.Fori(1, TILES - 1) as i:
                    turn(i, 4 * i)
                sp.wait_ge(h_ready, TILES)
                sp.dma_start(rows(h_out, TILES - 1), hn[:, :]).then_inc(stored, 16)
                sp.wait_ge(stored, 16 * (TILES + 1))

            @block.tensor
            def _(pe):
                def transposes(src, n):
                    for bnk in range(2):
                        pe.wait_ge(tp_copied, 2 * n + bnk + 1)
                        for k in range(4):
                            last = nc.tensor.transpose(tp[:, bnk, k, :], src[:, (4 * bnk + k) * P:(4 * bnk + k + 1) * P], K["ident"])
                        last.then_inc(tp_ready, 1)

                def project(i, n):
                    pe.wait_ge(x_in, 16 * i + 16)
                    transposes(xin, n)
                    pe.wait_ge(w_in, 16 * KC)
                    pe.wait_ge(tp_copied, 2 * n + 4)
                    for c in range(2):
                        pe.wait_ge(r_ready, 2 * i + c + 1)
                        for k in range(KC):
                            last = nc.tensor.matmul(acc[:, c, :], xT[:, k, :], w[:, k, c * HALF:(c + 1) * HALF],
                                                    start=(k == 0), stop=(k == KC - 1))
                        last.then_inc(acc_ready, 1)

                def route(i, n):
                    pe.wait_ge(h_ready, i + 1)
                    transposes(hn, n)
                    pe.wait_ge(small_in, 16 * 6)
                    pe.wait_ge(tp_copied, 2 * n + 4)
                    pe.wait_ge(lg_done, i + 1)
                    for k in range(KC):
                        last = nc.tensor.matmul(lg[:, 0, 0:NL], hT[:, k, :], wr[:, k, :], start=(k == 0), stop=(k == KC - 1))
                    last.then_inc(lg_ready, 1)

                project(0, 0)
                with pe.Fori(1, TILES) as i:
                    project(i, 2 * i - 1)
                    route(i - 1, 2 * i)
                route(TILES - 1, 2 * TILES - 1)

            @block.scalar
            def _(act):
                act.sem_inc(tp_copied, 1)
                act.sem_inc(tp_copied, 1)

                def copies(dst, n):
                    for bnk in range(2):
                        act.wait_ge(tp_ready, 2 * n + bnk + 1)
                        act.copy(dst[:, 4 * bnk:4 * bnk + 4, :], tp[:, bnk, :, :]).then_inc(tp_copied, 1)

                copies(xT, 0)
                with act.Fori(1, TILES) as i:
                    copies(xT, 2 * i - 1)
                    copies(hT, 2 * i)
                copies(hT, 2 * TILES - 1)

            @block.vector
            def _(dve):
                dve.sem_inc(r_ready, 1)
                dve.sem_inc(r_ready, 1)
                dve.sem_inc(lg_done, 1)
                dve.sem_inc(stored, 16)

                def norm(i, ch):
                    dve.wait_ge(res_in, 16 * i + 16)
                    for c in range(2):
                        s = slice(c * HALF, (c + 1) * HALF)
                        dve.wait_ge(acc_ready, 2 * i + c + 1)
                        dve.scalar_tensor_tensor(r[:, s], res[:, s], ALPHA, acc[:, c, :], ALU.mult, ALU.add).then_inc(r_ready, 1)
                    dve.wait_ge(r_ready, 2 * i + 4)
                    layer_norm_steps(dve, ch, r, stats, mv, ms_ready)
                    dve.wait_ge(rstd_ready, i + 2)
                    dve.wait_ge(stored, 16 * i + 16)
                    dve.tensor_scalar(hn[:, :], r[:, :], mv[:, 0:1], rstd[:, 0:1], ALU.subtract, ALU.mult).then_inc(h_scaled, 1)

                def put_logits(i):
                    dve.wait_ge(lg_ready, i + 1)
                    dve.wait_ge(small_in, 16 * 6)
                    dve.tensor_tensor(logits[:, bass.ds(i, 1), :], lg[:, 0:1, 0:NL], br[:, :].unsqueeze(1), ALU.add).then_inc(lg_done, 1)

                norm(0, Chain(dve, own))
                with dve.Fori(1, TILES) as i:
                    put_logits(i - 1)
                    norm(i, Chain(dve, own, 3 * i))
                put_logits(TILES - 1)

            @block.gpsimd
            def _(pool):
                pool.memset(half[:, :], -0.5).then_inc(rstd_ready, 1)
                pool.wait_ge(rstd_ready, 1)
                pool.wait_ge(small_in, 16 * 6)
                with pool.Fori(0, TILES) as i:
                    pool.wait_ge(ms_ready, i + 1)
                    pool.tensor_tensor(rstd[:, :], mv[:, 1:2], half[:, :], ALU.pow).then_inc(rstd_ready, 1)
                    pool.wait_ge(h_scaled, i + 1)
                    pool.tensor_tensor(hn[:, :], hn[:, :], gb[:, 0, :], ALU.mult).then_inc(gown, 1)
                    pool.wait_ge(gown, i + 1)
                    pool.tensor_tensor(hn[:, :], hn[:, :], gb[:, 1, :], ALU.add).then_inc(h_ready, 1)


def phase_route(nc, K, name, logits, gates, dest_i, tok_i, blk_i, pairs_i):
    T = TILES
    NL = GROUPS + EXPERTS
    with Phase(nc, name) as ph:
        def t3(n, w=EXPERTS):
            return ph.sb(n, [P, T, w])

        def t2(n, w=T):
            return ph.sb(n, [P, w])

        gmax, gsum, v1, v2, ex, w1, w2, ones_c = (t2(n) for n in ("gmax", "gsum", "v1", "v2", "ex", "w1", "w2", "pr"))
        ge, G4, rank4 = t3("ge", GROUPS), t3("G4", GROUPS), t3("rank4", GROUPS)
        em, em2, M1, M2, M, S, R, Q, q1, Dst, tmp = (t3(n) for n in (
            "em", "em2", "M1", "M2", "M", "S", "R", "Q", "q1", "Dst", "tmp"))
        S8 = t2("S8", EXPERTS)
        ones = ph.sb("ones", [P, P])
        cnt, nov, cum, ob, obe, zero = (t2(n, EXPERTS) for n in ("cnt", "nov", "cum", "ob", "obe", "zero"))
        d1, d2, s1, s2, b1, b2 = (t2(n) for n in ("d1", "d2", "s1", "s2", "b1", "b2"))
        A = ph.sb("A", [P, T, 2, P])
        B = ph.sb("B", [P, T, 2, BCOLS])
        over = ph.sb("over", [P, OVER + 2, EXPERTS])
        over2 = ph.sb("over2", [P, OVER + 2, EXPERTS])
        bexp = ph.sb("bexp", [P, BCOLS])
        tot = ph.sb("tot", [P, 2])
        sevens = ph.sb("sevens", [P, 8])
        pr = ph.ps("pr_ps", [P, T, EXPERTS])
        pc = ph.ps("pc", [P, EXPERTS])
        pt = ph.ps("pt", [P, BCOLS])
        own, m_ready, ranked, exp_in, exp_out, ab_ready, tok_ready = (ph.sem(n) for n in (
            "own", "m_ready", "ranked", "exp_in", "exp_out", "ab_ready", "tok_ready"))
        with nc.Block() as block:
            @block.scalar
            def _(act):
                act.wait_ge(exp_in, 1)
                act.activation(ge[:, :, :], ge[:, :, :], ACT.Exp).then_inc(exp_out, 1)
                act.wait_ge(exp_in, 2)
                act.activation(ex[:, :], ex[:, :], ACT.Exp).then_inc(exp_out, 1)

            @block.tensor
            def _(pe):
                pe.wait_ge(m_ready, 1)
                nc.tensor.matmul(pr[:, :, :], K["before"], M[:, :, :], start=True, stop=False)
                nc.tensor.matmul(pr[:, :, :], ones[:, :], S[:, :, :], start=False, stop=True)
                nc.tensor.matmul(pc[:, :], ones[:, :], S8[:, :], start=True, stop=True).then_inc(ranked, 1)
                pe.wait_ge(ab_ready, 1)
                for t in range(T):
                    for c in range(2):
                        last = nc.tensor.matmul(pt[:, :], A[:, t, c, :], B[:, t, c, :], start=(t + c == 0),
                                                stop=(t == T - 1 and c == 1))
                last.then_inc(tok_ready, 1)

            @block.vector
            def _(dve):
                ch = Chain(dve, own)

                def step(ins):
                    ch(ins)
                    ch.wait()

                def tt(o, a, b, op):
                    step(dve.tensor_tensor(o, a, b, op))

                def ts(o, a, x, op, y=None, op2=None):
                    step(dve.tensor_scalar(o, a, x, y, op, *([op2] if op2 is not None else [])))

                def wide(a, w):
                    return a.unsqueeze(2).to_broadcast([P, T, w])

                def first_max(out, src, top, w, work, rev):
                    tt(work, src, wide(top, w), ALU.is_equal)
                    tt(work, work, rev, ALU.mult)
                    step(dve.reduce_max(w1[:, :], work, axis=AX.X))
                    tt(out, work, wide(w1[:, :], w), ALU.is_equal)

                step(dve.memset(ones[:, :], 1.0))
                step(dve.memset(zero[:, :], 0.0))
                rev = tmp[:, :, :]
                revs = ph.sb("revs", [P, EXPERTS])
                ts(revs[:, :], K["iota"][:, 0:EXPERTS], -1.0, ALU.mult, float(EXPERTS), ALU.add)
                revx = revs[:, :].unsqueeze(1).to_broadcast([P, T, EXPERTS])
                revg = revs[:, 0:GROUPS].unsqueeze(1).to_broadcast([P, T, GROUPS])
                gl, el = logits[:, :, 0:GROUPS], logits[:, :, GROUPS:NL]
                step(dve.reduce_max(gmax[:, :], gl, axis=AX.X))
                first_max(G4[:, :, :], gl, gmax[:, :], GROUPS, rank4[:, :, :], revg)
                dve.tensor_tensor(ge[:, :, :], gl, wide(gmax[:, :], GROUPS), ALU.subtract).then_inc(exp_in, 1)
                gx = G4[:, :, :].unsqueeze(3).to_broadcast([P, T, GROUPS, PER_GROUP])
                e4 = em[:, :, :].rearrange("p t (g e) -> p t g e", g=GROUPS)
                q4 = q1[:, :, :].rearrange("p t (g e) -> p t g e", g=GROUPS)
                for t in range(T):
                    step(dve.tensor_copy(q4[:, t], gx[:, t]))
                tt(em[:, :, :], el, q1[:, :, :], ALU.mult)
                ts(q1[:, :, :], q1[:, :, :], -NEG, ALU.mult, NEG, ALU.add)
                tt(em[:, :, :], em[:, :, :], q1[:, :, :], ALU.add)
                step(dve.reduce_max(v1[:, :], em[:, :, :], axis=AX.X))
                first_max(M1[:, :, :], em[:, :, :], v1[:, :], EXPERTS, tmp[:, :, :], revx)
                step(dve.scalar_tensor_tensor(em2[:, :, :], M1[:, :, :], 3 * NEG, em[:, :, :], ALU.mult, ALU.add))
                step(dve.reduce_max(v2[:, :], em2[:, :, :], axis=AX.X))
                first_max(M2[:, :, :], em2[:, :, :], v2[:, :], EXPERTS, tmp[:, :, :], revx)
                dve.tensor_tensor(ex[:, :], v2[:, :], v1[:, :], ALU.subtract).then_inc(exp_in, 1)
                tt(M[:, :, :], M1[:, :, :], M2[:, :, :], ALU.add)
                step(dve.tensor_copy(S[:, 0, :], zero[:, :]))
                for t in range(1, T):
                    tt(S[:, t, :], S[:, t - 1, :], M[:, t - 1, :], ALU.add)
                dve.tensor_tensor(S8[:, :], S[:, T - 1, :], M[:, T - 1, :], ALU.add).then_inc(m_ready, 1)
                dve.wait_ge(exp_out, 2)
                step(dve.reduce_sum(gsum[:, :], ge[:, :, :], axis=AX.X))
                ts(w1[:, :], ex[:, :], 1.0, ALU.add)
                tt(w1[:, :], w1[:, :], gsum[:, :], ALU.mult)
                step(dve.reciprocal(gates[:, 0, :], w1[:, :]))
                tt(gates[:, 1, :], gates[:, 0, :], ex[:, :], ALU.mult)
                dve.wait_ge(ranked, 1)
                step(dve.tensor_copy(R[:, :, :], pr[:, :, :]))
                step(dve.tensor_copy(cnt[:, :], pc[:, :]))
                ts(Q[:, :, :], R[:, :, :], float(P), ALU.is_ge)
                ts(nov[:, :], cnt[:, :], float(P), ALU.is_gt)
                for m in range(2, T):
                    step(dve.scalar_tensor_tensor(Q[:, :, :], R[:, :, :], float(m * P), Q[:, :, :], ALU.is_ge, ALU.add))
                    step(dve.scalar_tensor_tensor(nov[:, :], cnt[:, :], float(m * P), nov[:, :], ALU.is_gt, ALU.add))
                step(dve.tensor_tensor_scan(cum[:, :], nov[:, :], zero[:, :], 0.0, ALU.add, ALU.add))
                tt(ob[:, :], cum[:, :], nov[:, :], ALU.subtract)
                step(dve.tensor_copy(tot[:, 0:1], cum[:, EXPERTS - 1:EXPERTS]))
                ts(obe[:, :], ob[:, :], float(EXPERTS - 1), ALU.add)
                tt(obe[:, :], obe[:, :], K["iota"][:, 0:EXPERTS], ALU.subtract)
                ts(q1[:, :, :], Q[:, :, :], 1.0, ALU.min)
                tt(tmp[:, :, :], q1[:, :, :], obe[:, :].unsqueeze(1).to_broadcast([P, T, EXPERTS]), ALU.mult)
                tt(tmp[:, :, :], tmp[:, :, :], Q[:, :, :], ALU.add)
                tt(tmp[:, :, :], tmp[:, :, :], K["iota"][:, 0:EXPERTS].unsqueeze(1).to_broadcast([P, T, EXPERTS]), ALU.add)
                step(dve.scalar_tensor_tensor(R[:, :, :], Q[:, :, :], -float(P), R[:, :, :], ALU.mult, ALU.add))
                for Mk, s, b in ((M1, s1, b1), (M2, s2, b2)):
                    tt(S[:, :, :], Mk[:, :, :], R[:, :, :], ALU.mult)
                    step(dve.reduce_sum(s[:, :], S[:, :, :], axis=AX.X))
                    tt(S[:, :, :], Mk[:, :, :], tmp[:, :, :], ALU.mult)
                    step(dve.reduce_sum(b[:, :], S[:, :, :], axis=AX.X))
                for n, (s, b, d) in enumerate(((s1, b1, d1), (s2, b2, d2))):
                    step(dve.scalar_tensor_tensor(d[:, :], b[:, :], float(P), s[:, :], ALU.mult, ALU.add))
                    step(dve.tensor_copy(dest_i[:, n, :], d[:, :]))
                for t in range(T):
                    for c, (s, b) in enumerate(((s1, b1), (s2, b2))):
                        ch(dve.tensor_scalar(A[:, t, c, :], K["iota"], s[:, t:t + 1], None, ALU.is_equal))
                        ch(dve.tensor_scalar(B[:, t, c, :], K["iota"][:, 0:BCOLS], b[:, t:t + 1], K["token"][:, t:t + 1],
                                             ALU.is_equal, ALU.mult))
                ch.wait()
                step(dve.tensor_copy(sevens[:, :], K["iota"][:, 0:8]))
                dve.sem_inc(ab_ready, 1)
                bi = K["iota"][:, 0:OVER + 2].unsqueeze(2).to_broadcast([P, OVER + 2, EXPERTS])

                def over_b(a):
                    return a.unsqueeze(1).to_broadcast([P, OVER + 2, EXPERTS])

                tt(over[:, :, :], bi, over_b(ob[:, :]), ALU.is_ge)
                tt(over2[:, :, :], bi, over_b(cum[:, :]), ALU.is_lt)
                tt(over[:, :, :], over[:, :, :], over2[:, :, :], ALU.mult)
                tt(over[:, :, :], over[:, :, :], over_b(K["iota"][:, 0:EXPERTS]), ALU.mult)
                step(dve.reduce_sum(bexp[:, EXPERTS:BCOLS], over[:, :, :], axis=AX.X))
                step(dve.tensor_copy(bexp[:, 0:EXPERTS], K["iota"][:, 0:EXPERTS]))
                step(dve.tensor_copy(blk_i[:, :], bexp[:, :]))
                ts(sevens[:, :], sevens[:, :], 2.0, ALU.mult)
                ts(sevens[:, :], sevens[:, :], tot[:, 0:1], ALU.is_lt)
                step(dve.reduce_sum(tot[:, 1:2], sevens[:, :], axis=AX.X))
                ts(tot[:, 1:2], tot[:, 1:2], float(EXPERTS // 2), ALU.add)
                step(dve.tensor_copy(pairs_i[:, :], tot[:, 1:2]))
                dve.wait_ge(tok_ready, 1)
                step(dve.tensor_copy(tok_i[:, :], pt[:, :]))


def phase_experts(nc, K, name, h, w_gate, w_up, w_down, tok_i, blk_i, pairs_i, y):
    FC = DE // P
    with Phase(nc, name) as ph:
        wg, wu = ph.sb("wg", [P, 2, KC, DE]), ph.sb("wu", [P, 2, KC, DE])
        wd = ph.sb("wd", [P, 2, FC, D])
        idx = ph.sb("idx", [P, 2, 1], I32)
        xg = ph.sb("xg", [P, 2, D])
        xT = ph.sb("xT", [P, KC, P])
        sg, hh = ph.sb("sg", [P, DE]), ph.sb("hh", [P, DE])
        hT = ph.sb("hT", [P, FC, P])
        ysb = ph.sb("y", [P, 2, D])
        tp = ph.ps("tp", [P, 2, 4, P])
        gp, up = ph.ps("gp", [P, HALF]), ph.ps("up", [P, HALF])
        hp = ph.ps("hp", [P, FC, P])
        yp = ph.ps("yp", [P, 2, HALF])
        gu_in = [ph.sem(f"gu_in{u}") for u in range(2)]
        d_in = [ph.sem(f"d_in{u}") for u in range(2)]
        x_in, idx_ready, tp_ready, xT_ready, g_ready, gu_ready, silu_done, h_ready, hp_ready, hT_ready = (
            ph.sem(n) for n in ("x_in", "idx_ready", "tp_ready", "xT_ready", "g_ready", "gu_ready", "silu_done",
                                "h_ready", "hp_ready", "hT_ready"))
        y_ready, y_done = ph.sem("y_ready"), ph.sem("y_done")
        stored = [ph.sem(f"stored{u}") for u in range(2)]

        def pairs(eng):
            return eng.value_load(pairs_i[0:1, 0:1], min_val=EXPERTS // 2, max_val=BLOCKS // 2)

        with nc.Block() as block:
            @block.sync
            def _(sp):
                n = pairs(sp)
                with sp.Fori(0, n) as p:
                    for u in range(2):
                        b = 2 * p + u
                        e = sp.value_load(blk_i[0:1, bass.ds(b, 1)], min_val=0, max_val=EXPERTS - 1)
                        sp.wait_ge(gu_ready, b + 1)
                        for src, dst in ((w_gate, wg), (w_up, wu)):
                            sp.dma_start(dst[:, u, :, :], src[bass.ds(e, 1), :, :].rearrange("o (k p) n -> p (o k) n", p=P)).then_inc(gu_in[u], 16)
                        sp.wait_ge(y_ready, 2 * b + 2)
                        sp.dma_start(wd[:, u, :, :], w_down[bass.ds(e, 1), :, :].rearrange("o (k p) n -> p (o k) n", p=P)).then_inc(d_in[u], 16)

            @block.gpsimd
            def _(pool):
                n = pairs(pool)

                def gather(b, u):
                    pool.tensor_copy(idx[:, u, :], tok_i[:, bass.ds(b, 1)] if not isinstance(b, int) else tok_i[:, b:b + 1]).then_inc(idx_ready, 1)
                    pool.wait_ge(idx_ready, b + 1)
                    settle(pool)
                    pool.indirect_dma_start(out=xg[:, u, :], out_offset=None, in_=h,
                                            in_offset=bass.IndirectOffsetOnAxis(ap=idx[:, u, :], axis=0)).then_inc(x_in, 16)

                gather(0, 0)
                with pool.Fori(0, n) as p:
                    for u in range(2):
                        b = 2 * p + u
                        pool.wait_ge(tp_ready, 2 * b + 2)
                        gather(b + 1, 1 - u)
                pool.wait_ge(x_in, n * 32 + 16)
                settle(pool)

            @block.tensor
            def _(pe):
                n = pairs(pe)

                def transposes(b, u):
                    pe.wait_ge(x_in, 16 * b + 16)
                    for bnk in range(2):
                        for k in range(4):
                            last = nc.tensor.transpose(tp[:, bnk, k, :], xg[:, u, (4 * bnk + k) * P:(4 * bnk + k + 1) * P], K["ident"])
                        last.then_inc(tp_ready, 1)

                for _ in range(2):
                    pe.sem_inc(gu_ready, 1)
                    pe.sem_inc(y_ready, 2)
                transposes(0, 0)
                with pe.Fori(0, n) as p:
                    for u in range(2):
                        b = 2 * p + u
                        pe.wait_ge(gu_in[u], 32 * p + 32)
                        pe.wait_ge(xT_ready, 2 * b + 2)
                        pe.wait_ge(h_ready, b + 1)
                        for k in range(KC):
                            last = nc.tensor.matmul(gp[:, :], xT[:, k, :], wg[:, u, k, :], start=(k == 0), stop=(k == KC - 1))
                        last.then_inc(g_ready, 1)
                        for k in range(KC):
                            last = nc.tensor.matmul(up[:, :], xT[:, k, :], wu[:, u, k, :], start=(k == 0), stop=(k == KC - 1))
                        last.then_inc(gu_ready, 1)
                        transposes(b + 1, 1 - u)
                        pe.wait_ge(h_ready, b + 2)
                        for k in range(FC):
                            last = nc.tensor.transpose(hp[:, k, :], hh[:, k * P:(k + 1) * P], K["ident"])
                        last.then_inc(hp_ready, 1)
                        pe.wait_ge(d_in[u], 16 * p + 16)
                        pe.wait_ge(hT_ready, b + 1)
                        for c in range(2):
                            pe.wait_ge(y_done, 2 * b + c + 1)
                            for k in range(FC):
                                last = nc.tensor.matmul(yp[:, c, :], hT[:, k, :], wd[:, u, k, c * HALF:(c + 1) * HALF],
                                                        start=(k == 0), stop=(k == FC - 1))
                            last.then_inc(y_ready, 1)

            @block.scalar
            def _(act):
                n = pairs(act)
                for u in range(2):
                    act.sem_inc(stored[u], 16)

                def copies(b):
                    for bnk in range(2):
                        act.wait_ge(tp_ready, 2 * b + bnk + 1)
                        act.copy(xT[:, 4 * bnk:4 * bnk + 4, :], tp[:, bnk, :, :]).then_inc(xT_ready, 1)

                copies(0)
                with act.Fori(0, n) as p:
                    for u in range(2):
                        b = 2 * p + u
                        act.wait_ge(g_ready, b + 1)
                        act.wait_ge(h_ready, b + 1)
                        act.activation(sg[:, :], gp[:, :], ACT.Silu).then_inc(silu_done, 1)
                        copies(b + 1)
                        act.wait_ge(y_done, 2 * b + 4)
                        act.dma_start(y[bass.ds(b * P, P), :], ysb[:, u, :]).then_inc(stored[u], 16)
                for u in range(2):
                    act.wait_ge(stored[u], n * 16 + 16)
                    settle(act)

            @block.vector
            def _(dve):
                n = pairs(dve)
                dve.sem_inc(h_ready, 1)
                dve.sem_inc(y_done, 2)
                with dve.Fori(0, n) as p:
                    for u in range(2):
                        b = 2 * p + u
                        dve.wait_ge(silu_done, b + 1)
                        dve.wait_ge(gu_ready, b + 3)
                        dve.tensor_tensor(hh[:, :], sg[:, :], up[:, :], ALU.mult).then_inc(h_ready, 1)
                        dve.wait_ge(hp_ready, b + 1)
                        dve.tensor_copy(hT[:, :, :], hp[:, :, :]).then_inc(hT_ready, 1)
                        dve.wait_ge(stored[u], 16 * p + 16)
                        for c in range(2):
                            dve.wait_ge(y_ready, 2 * b + c + 5)
                            dve.tensor_copy(ysb[:, u, c * HALF:(c + 1) * HALF], yp[:, c, :]).then_inc(y_done, 1)


def phase_combine(nc, K, name, h, y, gates, dest_i, g, b, out):
    with Phase(nc, name) as ph:
        gb = ph.sb("gb", [P, 2, D])
        idx = ph.sb("idx", [P, 2, 1], I32)
        gt = ph.sb("gt", [P, 2])
        hin = ph.sb("h", [P, D])
        yin = ph.sb("y", [P, 2, D])
        r, hn = ph.sb("r", [P, D]), ph.sb("hn", [P, D])
        stats, mv = ph.sb("stats", [P, 2, 6]), ph.sb("mv", [P, 2])
        rstd, half = ph.sb("rstd", [P, 1]), ph.sb("half", [P, 1])
        small_in, h_in, y_in, idx_ready, used, ms_ready, rstd_ready, h_scaled, h_ready, stored, own, gown = (
            ph.sem(n) for n in ("small_in", "h_in", "y_in", "idx_ready", "used", "ms_ready", "rstd_ready",
                                "h_scaled", "h_ready", "stored", "own", "gown"))
        with nc.Block() as block:
            @block.sync
            def _(sp):
                for n, row in enumerate((g, b)):
                    sp.dma_start(gb[:, n, :], row.partition_broadcast(P)).then_inc(small_in, 16)
                sp.dma_start(hin[:, :], h[0:P, :]).then_inc(h_in, 16)
                with sp.Fori(0, TILES - 1) as i:
                    sp.wait_ge(used, i + 1)
                    sp.dma_start(hin[:, :], rows(h, i + 1)).then_inc(h_in, 16)
                    sp.wait_ge(h_ready, i + 1)
                    sp.dma_start(rows(out, i), hn[:, :]).then_inc(stored, 16)
                sp.wait_ge(h_ready, TILES)
                sp.dma_start(rows(out, TILES - 1), hn[:, :]).then_inc(stored, 16)
                sp.wait_ge(stored, 16 * (TILES + 1))

            @block.gpsimd
            def _(pool):
                pool.memset(half[:, :], -0.5).then_inc(rstd_ready, 1)
                pool.wait_ge(rstd_ready, 1)
                pool.wait_ge(small_in, 32)

                def gather(i):
                    col = slice(i, i + 1) if isinstance(i, int) else bass.ds(i, 1)
                    for c in range(2):
                        pool.tensor_copy(idx[:, c, :], dest_i[:, c, col]).then_inc(idx_ready, 1)
                        pool.wait_ge(idx_ready, 2 * i + c + 1)
                        settle(pool)
                        pool.indirect_dma_start(out=yin[:, c, :], out_offset=None, in_=y,
                                                in_offset=bass.IndirectOffsetOnAxis(ap=idx[:, c, :], axis=0)).then_inc(y_in, 16)

                def affine(i):
                    pool.wait_ge(ms_ready, i + 1)
                    pool.tensor_tensor(rstd[:, :], mv[:, 1:2], half[:, :], ALU.pow).then_inc(rstd_ready, 1)
                    pool.wait_ge(h_scaled, i + 1)
                    pool.tensor_tensor(hn[:, :], hn[:, :], gb[:, 0, :], ALU.mult).then_inc(gown, 1)
                    pool.wait_ge(gown, i + 1)
                    pool.tensor_tensor(hn[:, :], hn[:, :], gb[:, 1, :], ALU.add).then_inc(h_ready, 1)

                gather(0)
                with pool.Fori(0, TILES - 1) as i:
                    pool.wait_ge(used, i + 1)
                    gather(i + 1)
                    affine(i)
                affine(TILES - 1)

            @block.vector
            def _(dve):
                dve.sem_inc(stored, 16)
                with dve.Fori(0, TILES) as i:
                    ch = Chain(dve, own, 6 * i)
                    ch(dve.tensor_copy(gt[:, :].unsqueeze(2), gates[:, :, bass.ds(i, 1)]))
                    dve.wait_ge(h_in, 16 * i + 16)
                    ch(dve.tensor_scalar(r[:, :], hin[:, :], ALPHA, None, ALU.mult))
                    ch.wait()
                    dve.wait_ge(y_in, 32 * i + 32)
                    ch(dve.scalar_tensor_tensor(r[:, :], yin[:, 0, :], gt[:, 0:1], r[:, :], ALU.mult, ALU.add))
                    ch.wait()
                    dve.scalar_tensor_tensor(r[:, :], yin[:, 1, :], gt[:, 1:2], r[:, :], ALU.mult, ALU.add).then_inc(used, 1)
                    dve.wait_ge(used, i + 1)
                    layer_norm_steps(dve, ch, r, stats, mv, ms_ready)
                    dve.wait_ge(rstd_ready, i + 2)
                    dve.wait_ge(stored, 16 * i + 16)
                    dve.tensor_scalar(hn[:, :], r[:, :], mv[:, 0:1], rstd[:, 0:1], ALU.subtract, ALU.mult).then_inc(h_scaled, 1)
                    dve.wait_ge(h_scaled, i + 1)
                    settle(dve)


def phase_pool(nc, K, h, w_in, w_grp, ls, mix):
    PADW = 16
    NG = len(POOL_WINDOWS)
    CG = PG // P
    with Phase(nc, "pool") as ph:
        w = ph.sb("w", [P, KC, D])
        wg = ph.sb("wg", [P, NG, CG, PG])
        lsb = ph.sb("ls", [P, D])
        xin = ph.sb("x", [P, D])
        hT = ph.sb("hT", [P, KC, SEQ])
        u = ph.sb("u", [P, PADW + SEQ])
        s = ph.sb("s", [P, 2, PADW + SEQ])
        pT = ph.sb("pT", [P, CG, SEQ])
        ysb = ph.sb("y", [P, TILES, PG])
        tp = ph.ps("tp", [P, 2, 4, P])
        up = ph.ps("up", [P, 2, HALF])
        yp = ph.ps("yp", [P, 2, HALF])
        w_in_s, small_in, x_in, tp_ready, tp_copied, u_ready, u_copied, p_ready, y_ready, y_done, stored, own, padded = (
            ph.sem(n) for n in ("w_in", "small_in", "x_in", "tp_ready", "tp_copied", "u_ready", "u_copied", "p_ready",
                                "y_ready", "y_done", "stored", "own", "padded"))
        with nc.Block() as block:
            @block.sync
            def _(sp):
                sp.dma_start(xin[:, :], h[0:P, :]).then_inc(x_in, 16)
                for k in range(KC):
                    sp.dma_start(w[:, k, :], w_in[k * P:(k + 1) * P, :]).then_inc(w_in_s, 16)
                for g in range(NG):
                    sp.dma_start(wg[:, g, :, :], w_grp[g].rearrange("(k p) n -> p k n", p=P)).then_inc(small_in, 16)
                sp.dma_start(lsb[:, :], ls.partition_broadcast(P)).then_inc(small_in, 16)
                with sp.Fori(0, TILES - 1) as i:
                    sp.wait_ge(tp_ready, 2 * i + 2)
                    sp.dma_start(xin[:, :], rows(h, i + 1)).then_inc(x_in, 16)
                for g in range(NG):
                    sp.wait_ge(y_done, 2 + TILES // 2 * (g + 1))
                    sp.dma_start(mix[:, g * PG:(g + 1) * PG].rearrange("(t p) c -> p t c", p=P), ysb[:, :, :]).then_inc(stored, 16)
                sp.wait_ge(stored, 16 * NG)

            @block.tensor
            def _(pe):
                with pe.Fori(0, TILES) as i:
                    pe.wait_ge(x_in, 16 * i + 16)
                    for b in range(2):
                        pe.wait_ge(tp_copied, 2 * i + b + 1)
                        for k in range(4):
                            last = nc.tensor.transpose(tp[:, b, k, :], xin[:, (4 * b + k) * P:(4 * b + k + 1) * P], K["ident"])
                        last.then_inc(tp_ready, 1)
                pe.wait_ge(w_in_s, 16 * KC)
                pe.wait_ge(small_in, 16 * (NG + 1))
                pe.wait_ge(tp_copied, 2 + 2 * TILES)

                def channels(ct):
                    for c in range(2):
                        pe.wait_ge(u_copied, 2 * ct + c + 1)
                        for k in range(KC):
                            last = nc.tensor.matmul(up[:, c, :], w[:, k, ct * P:(ct + 1) * P], hT[:, k, c * HALF:(c + 1) * HALF],
                                                    start=(k == 0), stop=(k == KC - 1))
                        last.then_inc(u_ready, 1)

                def outputs(g):
                    pe.wait_ge(p_ready, CG * (g + 1))
                    for t in range(TILES):
                        if t % 2 == 0:
                            pe.wait_ge(y_done, TILES // 2 * g + t // 2 + 1)
                        for k in range(CG):
                            last = nc.tensor.matmul(yp[:, t // 2 % 2, t % 2 * PG:(t % 2 + 1) * PG], pT[:, k, t * P:(t + 1) * P],
                                                    wg[:, g, k, :], start=(k == 0), stop=(k == CG - 1))
                        if t % 2:
                            last.then_inc(y_ready, 1)

                channels(0)
                channels(1)
                for g in range(NG):
                    if g + 1 < NG:
                        channels(CG * (g + 1))
                    outputs(g)
                    if g + 1 < NG:
                        channels(CG * (g + 1) + 1)

            @block.scalar
            def _(act):
                act.sem_inc(tp_copied, 2)
                act.sem_inc(u_copied, 2)
                with act.Fori(0, TILES) as i:
                    for b in range(2):
                        act.wait_ge(tp_ready, 2 * i + b + 1)
                        act.activation(hT[:, 4 * b:4 * b + 4, bass.ds(i * P, P)], tp[:, b, :, :], ACT.Copy).then_inc(tp_copied, 1)
                act.wait_ge(padded, 1)
                for ct in range(KC):
                    if ct > 0:
                        act.wait_ge(p_ready, ct)
                    for c in range(2):
                        act.wait_ge(u_ready, 2 * ct + c + 1)
                        act.copy(u[:, PADW + c * HALF:PADW + (c + 1) * HALF], up[:, c, :]).then_inc(u_copied, 1)

            @block.vector
            def _(dve):
                ch = Chain(dve, own)
                ch(dve.memset(s[:, :, 0:PADW], 0.0))
                dve.memset(u[:, 0:PADW], 0.0).then_inc(padded, 1)
                ch.wait()
                dve.wait_ge(padded, 1)
                dve.sem_inc(y_done, 2)

                def window(ct):
                    g = ct // CG
                    dve.wait_ge(u_copied, 2 * ct + 4)
                    src, step, n = u[:, :], 1, 0
                    while step < POOL_WINDOWS[g]:
                        ch(dve.tensor_tensor(s[:, n % 2, PADW:], src[:, PADW:], src[:, PADW - step:PADW + SEQ - step], ALU.add))
                        ch.wait()
                        src, step, n = s[:, n % 2, :], 2 * step, n + 1
                    ch(dve.tensor_tensor(s[:, n % 2, PADW:], src[:, PADW:], K["invcount"][:, g * SEQ:(g + 1) * SEQ], ALU.mult))
                    ch.wait()
                    if ct % CG == 0 and g > 0:
                        dve.wait_ge(y_ready, TILES // 2 * g)
                    dve.tensor_tensor(pT[:, ct % CG, :], s[:, n % 2, PADW:], u[:, PADW:], ALU.subtract).then_inc(p_ready, 1)
                    dve.wait_ge(p_ready, ct + 1)

                def outputs(g):
                    if g > 0:
                        dve.wait_ge(stored, 16 * g)
                    for t in range(0, TILES, 2):
                        dve.wait_ge(y_ready, TILES // 2 * g + t // 2 + 1)
                        dve.tensor_tensor(ysb[:, t:t + 2, :], yp[:, t // 2 % 2, :].rearrange("p (a c) -> p a c", a=2),
                                          lsb[:, g * PG:(g + 1) * PG].unsqueeze(1).to_broadcast([P, 2, PG]), ALU.mult).then_inc(y_done, 1)

                dve.wait_ge(small_in, 16 * (NG + 1))
                window(0)
                window(1)
                for g in range(NG):
                    outputs(g)
                    if g + 1 < NG:
                        window(CG * (g + 1))
                        window(CG * (g + 1) + 1)


def phase_modulation(nc, K, name, c, ada_w, ada_b, norm_w, mod):
    with Phase(nc, name) as ph:
        w = ph.sb("w", [P, KC, 3 * D])
        cs = ph.sb("c", [P, KC])
        cb = ph.sb("cb", [P, KC, P])
        bb = ph.sb("bb", [P, 3 * D])
        nw = ph.sb("nw", [P, D])
        acc = ph.ps("acc", [P, NCHUNK, HALF])
        w_in, c_in, b_in, c_ready, c_act, acc_ready, own = (ph.sem(n) for n in (
            "w_in", "c_in", "b_in", "c_ready", "c_act", "acc_ready", "own"))
        with nc.Block() as block:
            @block.sync
            def _(sp):
                with nc.allow_non_contiguous_dma(reason="one column of c"):
                    sp.dma_start(cs[:, :], c.rearrange("o (k p) -> p (o k)", p=P)).then_inc(c_in, 16)
                for k in range(KC):
                    sp.dma_start(w[:, k, :], ada_w[k * P:(k + 1) * P, :]).then_inc(w_in, 16)
                sp.dma_start(bb[:, :], ada_b.partition_broadcast(P)).then_inc(b_in, 16)
                sp.dma_start(nw[:, :], norm_w.partition_broadcast(P)).then_inc(b_in, 16)
                sp.wait_ge(w_in, 16 * KC)

            @block.scalar
            def _(act):
                act.wait_ge(c_in, 16)
                act.activation(cs[:, :], cs[:, :], ACT.Silu).then_inc(c_act, 1)
                act.wait_ge(c_act, 1)
                act.copy(cb[:, :, :], cs[:, :].unsqueeze(2).to_broadcast([P, KC, P])).then_inc(c_ready, 1)

            @block.tensor
            def _(pe):
                pe.wait_ge(c_ready, 1)
                for k in range(KC):
                    pe.wait_ge(w_in, 16 * KC)
                    for n in range(NCHUNK):
                        last = nc.tensor.matmul(acc[:, n, :], cb[:, k, :], w[:, k, n * HALF:(n + 1) * HALF],
                                                start=(k == 0), stop=(k == KC - 1))
                last.then_inc(acc_ready, 1)

            @block.vector
            def _(dve):
                ch = Chain(dve, own)
                dve.wait_ge(b_in, 32)
                dve.wait_ge(acc_ready, 1)

                def chunk(part, out):
                    for n in range(2):
                        s = slice(n * HALF, (n + 1) * HALF)
                        ch(dve.tensor_tensor(out[:, s], acc[:, 2 * part + n, :], bb[:, part * D + n * HALF:part * D + (n + 1) * HALF], ALU.add))

                chunk(0, mod[:, 1, :])
                chunk(1, mod[:, 0, :])
                chunk(2, mod[:, 2, :])
                ch.wait()
                ch(dve.scalar_tensor_tensor(mod[:, 0, :], mod[:, 0, :], 1.0, nw[:, :], ALU.add, ALU.mult))
                ch.wait()


def phase_angles(nc, K, positions, tabs):
    NF = RD // 2
    two_pi = 2 * math.pi
    c1 = 6.28125
    c2 = float(np.float32(np.round((two_pi - c1) * 2 ** 22) / 2 ** 22))
    c3 = two_pi - c1 - c2
    with Phase(nc, "angles") as ph:
        pi = ph.sb("pi", [P, TILES], I32)
        pf = ph.sb("pf", [P, TILES])
        ang, kf, r = (ph.sb(n, [P, TILES, NF]) for n in ("ang", "kf", "r"))
        ki = ph.sb("ki", [P, TILES, NF], I32)
        p_in, own, r_ready, t_ready = (ph.sem(n) for n in ("p_in", "own", "r_ready", "t_ready"))
        with nc.Block() as block:
            @block.sync
            def _(sp):
                with nc.allow_non_contiguous_dma(reason="1024 positions"):
                    sp.dma_start(pi[:, :], positions.rearrange("o (t p) -> p (o t)", p=P)).then_inc(p_in, 16)

            @block.vector
            def _(dve):
                ch = Chain(dve, own)

                def step(ins):
                    ch(ins)
                    ch.wait()

                dve.wait_ge(p_in, 16)
                step(dve.tensor_copy(pf[:, :], pi[:, :]))
                step(dve.tensor_tensor(ang[:, :, :], pf[:, :].unsqueeze(2).to_broadcast([P, TILES, NF]),
                                       K["inv"].unsqueeze(1).to_broadcast([P, TILES, NF]), ALU.mult))
                for n, turn in enumerate((0.25, 0.0)):
                    step(dve.tensor_scalar(kf[:, :, :], ang[:, :, :], 1.0 / two_pi, turn, ALU.mult, ALU.add))
                    step(dve.tensor_copy(ki[:, :, :], kf[:, :, :]))
                    step(dve.tensor_copy(kf[:, :, :], ki[:, :, :]))
                    if n:
                        dve.wait_ge(t_ready, 1)
                    step(dve.scalar_tensor_tensor(r[:, :, :], kf[:, :, :], -c1, ang[:, :, :], ALU.mult, ALU.add))
                    step(dve.scalar_tensor_tensor(r[:, :, :], kf[:, :, :], -c2, r[:, :, :], ALU.mult, ALU.add))
                    step(dve.scalar_tensor_tensor(r[:, :, :], kf[:, :, :], -c3, r[:, :, :], ALU.mult, ALU.add))
                    step(dve.tensor_scalar(r[:, :, :], r[:, :, :], turn * two_pi, None, ALU.add))
                    for op, whole in ((ALU.is_gt, -1), (ALU.is_lt, 1)):
                        step(dve.tensor_scalar(kf[:, :, :], r[:, :, :], -whole * math.pi, whole * two_pi, op, ALU.mult))
                        step(dve.tensor_tensor(r[:, :, :], r[:, :, :], kf[:, :, :], ALU.add))
                    dve.tensor_scalar(r[:, :, :], r[:, :, :], 3.1415925, -3.1415925, ALU.min, ALU.max).then_inc(r_ready, 1)

            @block.scalar
            def _(act):
                for n in range(2):
                    act.wait_ge(r_ready, n + 1)
                    act.activation(tabs[:, n, :, :], r[:, :, :], ACT.Sin).then_inc(t_ready, 1)


def phase_project(nc, K, name, x, w_in, q_norm, w_uq, kv_norm, w_ukv, mod, tabs, proj, mq, mk, mkv):
    AB = 3
    with Phase(nc, name) as ph:
        w = ph.sb("w", [P, KC, IN_COLS])
        wq, wkv = ph.sb("wq", [P, 2, MH * MQ]), ph.sb("wkv", [P, D])
        ln = ph.sb("ln", [P, MQR + MKVR])
        xin, h = ph.sb("x", [P, D]), ph.sb("h", [P, D])
        ss, rstd, half = ph.sb("ss", [P, 2]), ph.sb("rstd", [P, 1]), ph.sb("half", [P, 2])
        hT = ph.sb("hT", [P, KC, P])
        row = ph.sb("row", [P, IN_COLS])
        t1 = ph.sb("t1", [P, 4, 8, 32])
        ks = ph.sb("ks", [P, 4, 16])
        lsq, ms, lr, lat = ph.sb("lsq", [P, MQR + MKVR]), ph.sb("ms", [P, 2]), ph.sb("lr", [P, 2]), ph.sb("lat", [P, MQR + MKVR])
        latT = ph.sb("latT", [P, 3, P])
        kpe_new, kpe = ph.sb("kpe_new", [P, ROPE_D]), ph.sb("kpe", [P, ROPE_D])
        q_sb, k_sb, kv_sb = ph.sb("q", [P, MH, MQ]), ph.sb("k", [P, MH, MQ]), ph.sb("kv", [P, MH, NOPE + MV])
        tp = ph.ps("tp", [P, 2, 4, P])
        acc = ph.ps("acc", [P, AB, HALF])
        lt = ph.ps("lt", [P, 4, P])
        lp = ph.ps("lp", [P, 2, HALF])
        names = ("w_in", "small_in", "x_in", "x_sq", "h_step", "h_ready", "tp_ready", "tp_copied", "acc_ready", "row_copied",
                 "ms_ready", "lr_ready", "lat_ready", "lt_ready", "latT_ready", "lp_ready", "lp_copied", "row_done",
                 "row_stored", "mla_done", "mla_stored", "own")
        (w_ready, small_in, x_in, x_sq, h_step, h_ready, tp_ready, tp_copied, acc_ready, row_copied, ms_ready, lr_ready,
         lat_ready, lt_ready, latT_ready, lp_ready, lp_copied, row_done, row_stored, mla_done, mla_stored, own) = (
            ph.sem(n) for n in names)
        col = {n: row[:, a:b] for n, (a, b) in COLS.items()}

        with nc.Block() as block:
            @block.sync
            def _(sp):
                sp.dma_start(xin[:, :], x[0:P, :]).then_inc(x_in, 16)
                for k in range(KC):
                    sp.dma_start(w[:, k, :], w_in[k * P:(k + 1) * P, :]).then_inc(w_ready, 16)
                sp.dma_start(ln[:, 0:MQR], q_norm.partition_broadcast(P)).then_inc(small_in, 16)
                sp.dma_start(ln[:, MQR:], kv_norm.partition_broadcast(P)).then_inc(small_in, 16)
                sp.dma_start(wq[:, :, :], w_uq.rearrange("(k p) n -> p k n", p=P)).then_inc(small_in, 16)
                sp.dma_start(wkv[:, :], w_ukv).then_inc(small_in, 16)

                def load(i):
                    sp.wait_ge(h_ready, i)
                    sp.dma_start(xin[:, :], rows(x, i)).then_inc(x_in, 16)

                def store_row(i):
                    sp.wait_ge(row_done, i + 1)
                    sp.dma_start(rows(proj, i), row[:, :]).then_inc(row_stored, 16)

                def store_mla(i):
                    sp.wait_ge(mla_done, i + 1)
                    for dst, src in ((mq, q_sb), (mk, k_sb), (mkv, kv_sb)):
                        sp.dma_start(rows(dst, i), src[:, :, :].rearrange("p h c -> p (h c)")).then_inc(mla_stored, 16)

                load(1)
                store_row(0)
                with sp.Fori(1, TILES - 1) as i:
                    load(i + 1)
                    store_row(i)
                    store_mla(i - 1)
                store_row(TILES - 1)
                store_mla(TILES - 2)
                store_mla(TILES - 1)
                sp.wait_ge(row_stored, 16 * (TILES + 1))
                sp.wait_ge(mla_stored, 48 * (TILES + 1))

            @block.gpsimd
            def _(pool):
                pool.memset(half[:, :], -0.5).then_inc(h_step, 1)
                pool.wait_ge(h_step, 1)

                def modulate(i):
                    ch = Chain(pool, h_step, 4 * i + 1)
                    pool.wait_ge(x_sq, i + 1)
                    settle(pool)
                    ch(pool.tensor_scalar(ss[:, 1:2], ss[:, 0:1], 1.0 / D, RMS_EPS, ALU.mult, ALU.add))
                    ch.wait()
                    ch(pool.tensor_tensor(rstd[:, :], ss[:, 1:2], half[:, 0:1], ALU.pow))
                    ch.wait()
                    if not (isinstance(i, int) and i == 0):
                        pool.wait_ge(tp_ready, 2 * i)
                    settle(pool)
                    ch(pool.tensor_scalar(h[:, :], xin[:, :], rstd[:, 0:1], None, ALU.mult))
                    ch.wait()
                    ch(pool.tensor_tensor(h[:, :], h[:, :], mod[:, 0, :], ALU.mult))
                    ch.wait()
                    pool.tensor_tensor(h[:, :], h[:, :], mod[:, 1, :], ALU.add).then_inc(h_ready, 1)

                def latent_power(i):
                    pool.wait_ge(ms_ready, i + 1)
                    pool.tensor_tensor(lr[:, :], ms[:, :], half[:, :], ALU.pow).then_inc(lr_ready, 1)

                modulate(0)
                with pool.Fori(0, TILES - 1) as i:
                    latent_power(i)
                    modulate(i + 1)
                latent_power(TILES - 1)

            @block.tensor
            def _(pe):
                def project(i):
                    pe.wait_ge(h_ready, i + 1)
                    for b in range(2):
                        pe.wait_ge(tp_copied, 2 * i + b + 1)
                        for k in range(4):
                            last = nc.tensor.transpose(tp[:, b, k, :], h[:, (4 * b + k) * P:(4 * b + k + 1) * P], K["ident"])
                        last.then_inc(tp_ready, 1)
                    pe.wait_ge(w_ready, 16 * KC)
                    pe.wait_ge(tp_copied, 2 * i + 4)
                    for c in range(NCHUNK):
                        pe.wait_ge(row_copied, NCHUNK * i + c + 1)
                        for k in range(KC):
                            last = nc.tensor.matmul(acc[:, c % AB, 0:CW], hT[:, k, :], w[:, k, c * CW:(c + 1) * CW],
                                                    start=(k == 0), stop=(k == KC - 1))
                        last.then_inc(acc_ready, 1)

                def latents(i):
                    pe.wait_ge(lat_ready, i + 1)
                    for k in range(3):
                        last = nc.tensor.transpose(lt[:, k, :], lat[:, k * P:(k + 1) * P], K["ident"])
                    last.then_inc(lt_ready, 1)
                    pe.wait_ge(small_in, 64)
                    pe.wait_ge(latT_ready, i + 1)
                    for c in range(4):
                        pe.wait_ge(lp_copied, 4 * i + c + 1)
                        if c < 2:
                            n = MH * MQ // 2
                            for k in range(2):
                                last = nc.tensor.matmul(lp[:, c % 2, 0:n], latT[:, k, :], wq[:, k, c * n:(c + 1) * n],
                                                        start=(k == 0), stop=(k == 1))
                        else:
                            last = nc.tensor.matmul(lp[:, c % 2, :], latT[:, 2, :], wkv[:, (c - 2) * HALF:(c - 1) * HALF],
                                                    start=True, stop=True)
                        last.then_inc(lp_ready, 1)

                project(0)
                with pe.Fori(1, TILES) as i:
                    project(i)
                    latents(i - 1)
                latents(TILES - 1)

            @block.scalar
            def _(act):
                act.sem_inc(tp_copied, 2)
                act.sem_inc(row_copied, AB)
                act.sem_inc(lp_copied, 2)
                act.sem_inc(row_stored, 16)
                act.sem_inc(mla_stored, 48)

                def square(i):
                    act.wait_ge(x_in, 16 * i + 16)
                    act.activation(t1[:, :, :, :].rearrange("p a b c -> p (a b c)"), xin[:, :], ACT.Square,
                                   accum_out=ss[:, 0:1]).then_inc(x_sq, 1)

                def row_chunks(i):
                    for b in range(2):
                        act.wait_ge(tp_ready, 2 * i + b + 1)
                        act.copy(hT[:, 4 * b:4 * b + 4, :], tp[:, b, :, :]).then_inc(tp_copied, 1)
                    act.wait_ge(row_stored, 16 * i + 16)
                    for c in range(NCHUNK):
                        act.wait_ge(acc_ready, NCHUNK * i + c + 1)
                        act.copy(row[:, c * CW:(c + 1) * CW], acc[:, c % AB, 0:CW]).then_inc(row_copied, 1)

                def latent_chunks(i):
                    act.wait_ge(lt_ready, i + 1)
                    act.copy(latT[:, :, :], lt[:, 0:3, :]).then_inc(latT_ready, 1)
                    act.wait_ge(mla_stored, 48 * i + 48)
                    for c in range(4):
                        act.wait_ge(lp_ready, 4 * i + c + 1)
                        dst = q_sb if c < 2 else kv_sb
                        n = MH // 2
                        act.copy(dst[:, c % 2 * n:(c % 2 + 1) * n, :],
                                 lp[:, c % 2, 0:n * dst.shape[-1]].rearrange("p (h c) -> p h c", h=n)).then_inc(lp_copied, 1)

                square(0)
                row_chunks(0)
                with act.Fori(1, TILES) as i:
                    square(i)
                    row_chunks(i)
                    latent_chunks(i - 1)
                latent_chunks(TILES - 1)

            @block.vector
            def _(dve):
                def rotate(ch, r1, r2, o1, o2, cos, sin, t):
                    ch(dve.tensor_tensor(t[0], r1, cos, ALU.mult))
                    ch(dve.tensor_tensor(t[1], r2, sin, ALU.mult))
                    ch(dve.tensor_tensor(t[2], r2, cos, ALU.mult))
                    ch(dve.tensor_tensor(t[3], r1, sin, ALU.mult))
                    ch.wait()
                    ch(dve.tensor_tensor(o1, t[0], t[1], ALU.subtract))
                    ch(dve.tensor_tensor(o2, t[2], t[3], ALU.add))
                    ch.wait()

                rt = ph.sb("rt", [P, 4, 8, 32])

                def angles(i, heads, step):
                    a = slice(i, i + 1) if isinstance(i, int) else bass.ds(i, 1)
                    n = RD // 2 // step
                    return [tabs[:, k, a, ::step].to_broadcast([P, heads, n]) for k in range(2)]

                N1, N2 = 6 + 6 + 4, 6 + 3

                def first_part(i, base):
                    ch = Chain(dve, own, base)
                    dve.wait_ge(row_copied, NCHUNK * i + AB + NCHUNK)
                    g = row[:, 0:2 * RH * RD].rearrange("p (h c) -> p h c", c=RD)
                    cos, sin = angles(i, 2 * RH, 1)
                    rotate(ch, g[:, :, 0:32], g[:, :, 32:64], g[:, :, 0:32], g[:, :, 32:64], cos, sin, [rt[:, n] for n in range(4)])
                    kr = col["mkr"].unsqueeze(1)
                    cos, sin = angles(i, 1, 2)
                    rotate(ch, kr[:, :, 0:16], kr[:, :, 16:32], kpe_new[:, 0:16].unsqueeze(1), kpe_new[:, 16:32].unsqueeze(1),
                           cos, sin, [ks[:, n:n + 1, :] for n in range(4)])
                    both = row[:, COLS["mq"][0]:COLS["mkv"][1]]
                    ch(dve.tensor_tensor(lsq[:, :], both, both, ALU.mult))
                    ch.wait()
                    ch(dve.reduce_sum(ms[:, 0:1], lsq[:, 0:MQR], axis=AX.X))
                    ch(dve.reduce_sum(ms[:, 1:2], lsq[:, MQR:], axis=AX.X))
                    ch.wait()
                    ch(dve.tensor_scalar(ms[:, 0:1], ms[:, 0:1], 1.0 / MQR, RMS_EPS, ALU.mult, ALU.add))
                    dve.tensor_scalar(ms[:, 1:2], ms[:, 1:2], 1.0 / MKVR, RMS_EPS, ALU.mult, ALU.add).then_inc(ms_ready, 1)
                    assert ch.n == N1
                    ch.wait()
                    dve.wait_ge(lr_ready, i + 1)
                    dve.wait_ge(small_in, 64)
                    if not isinstance(i, int):
                        dve.wait_ge(lt_ready, i)
                    dve.scalar_tensor_tensor(lat[:, 0:MQR], col["mq"], lr[:, 0:1], ln[:, 0:MQR], ALU.mult, ALU.mult)
                    dve.scalar_tensor_tensor(lat[:, MQR:], col["mkv"], lr[:, 1:2], ln[:, MQR:], ALU.mult, ALU.mult).then_inc(lat_ready, 1)
                    dve.wait_ge(lat_ready, i + 1)
                    dve.sem_inc(row_done, 1)

                def second_part(i, base):
                    ch = Chain(dve, own, base)
                    dve.wait_ge(lp_copied, 4 * i + 6)
                    cos, sin = angles(i, MH, 2)
                    a, b = q_sb[:, :, NOPE:NOPE + 16], q_sb[:, :, NOPE + 16:MQ]
                    rotate(ch, a, b, a, b, cos, sin, [rt[:, n, :, 0:16] for n in range(4)])
                    ch(dve.tensor_copy(k_sb[:, :, 0:NOPE], kv_sb[:, :, 0:NOPE]))
                    ch(dve.tensor_copy(k_sb[:, :, NOPE:MQ], kpe[:, :].unsqueeze(1).to_broadcast([P, MH, ROPE_D])))
                    ch.wait()
                    ch(dve.tensor_copy(kpe[:, :], kpe_new[:, :]))
                    ch.wait()
                    assert ch.n == N2
                    dve.sem_inc(mla_done, 1)

                first_part(0, 0)
                ch = Chain(dve, own, N1)
                ch(dve.tensor_copy(kpe[:, :], kpe_new[:, :]))
                ch.wait()
                with dve.Fori(1, TILES) as i:
                    first_part(i, (N1 + N2) * (i - 1) + N1 + 1)
                    second_part(i - 1, (N1 + N2) * (i - 1) + 2 * N1 + 1)
                second_part(TILES - 1, (N1 + N2) * (TILES - 1) + N1 + 1)


def mla_attention(nc, K, name, mq, mk, mkv, out):
    def tiles(ap, base, step, width):
        return lambda h: ap[:, bass.ds(h * step + base, width)].rearrange("(t p) c -> p t c", p=P)

    phase_attention(nc, K, name, tiles(mq, 0, MQ, MQ), tiles(mk, 0, MQ, MQ), tiles(mkv, NOPE, NOPE + MV, MV),
                    tiles(out, 0, MV, MV), 1, MQ, MV, K["chunked"], MQ ** -0.5)


def phase_mix_out(nc, K, name, proj, mla_o, x, w_g2, b_g2, gla_norm, w_out, mod, final_norm, out):
    final = final_norm is not None
    with Phase(nc, name) as ph:
        w = ph.sb("w", [P, KC, D])
        g2 = ph.sb("g2", [GRANK, P])
        bg = ph.sb("bg", [P, 1])
        gn = ph.sb("gn", [P, GDV])
        row = ph.sb("row", [P, IN_COLS])
        vv = ph.sb("vv", [P, 2, 256])
        mo = ph.sb("mo", [P, MH * MV])
        rT = ph.sb("rT", [P, 2, P])
        rkT = ph.sb("rkT", [P, RH, P])
        rqw = ph.sb("rqw", [P, 2, P])
        rkw = ph.sb("rkw", [P, RH * RD])
        gT = ph.sb("gT", [P, 2, P])
        ggT = ph.sb("ggT", [GRANK, P])
        z, ab, mn, sg, la, cum = (ph.sb(n, [P, P]) for n in ("z", "ab", "mn", "sg", "la", "cum"))
        last2, elast = ph.sb("last2", [P, 2]), ph.sb("elast", [P, 2])
        epos, eneg, el = (ph.sb(n, [P, P]) for n in ("epos", "eneg", "el"))
        qpos, qneg, kpos, kneg, kwT, kw = (ph.sb(n, [P, P]) for n in ("qpos", "qneg", "kpos", "kneg", "kwT", "kw"))
        kposm, knegm = ph.sb("kposm", [P, GH, P]), ph.sb("knegm", [P, GH, P])
        a_r, a_g = ph.sb("a_r", [P, RH, CH]), ph.sb("a_g", [P, GH, CH])
        past = ph.sb("past", [P, GH, CH], I32)
        um_r, um_g = ph.sb("um_r", [P, 2, 2, P]), ph.sb("um_g", [P, 2, 256])
        s_r, s_g = ph.sb("s_r", [P, 3, 2, P]), ph.sb("s_g", [P, 3, 256])
        o, osq = ph.sb("o", [P, 8, 64]), ph.sb("osq", [P, 8, 64])
        ms, rs, half = ph.sb("ms", [P, 8]), ph.sb("rs", [P, 8]), ph.sb("half", [P, 8])
        zs = ph.sb("zs", [P, D])
        mixed = ph.sb("mixed", [P, D])
        mT = ph.sb("mT", [P, KC, P])
        xr, xn = ph.sb("xr", [P, D]), ph.sb("xn", [P, D])
        if final:
            fn, junk = ph.sb("fn", [P, D]), ph.sb("junk", [P, D])
            fs, fr = ph.sb("fs", [P, 2]), ph.sb("fr", [P, 1])
        tA, tB, sc, pf = (ph.ps(n, [P, 4, P]) for n in ("tA", "tB", "sc", "pf"))
        u0, u1, op, acc = (ph.ps(n, [P, HALF]) for n in ("u0", "u1", "op", "acc"))
        S = {n: ph.sem(n) for n in (
            "w_in", "small_in", "row_in", "v_in", "x_in", "t_ready", "t_copied", "z_ready", "z_done", "mt_ready", "mt_copied",
            "acc_ready", "x_part", "kwt_ready", "kw_ready", "rs_ready", "gs_ready", "ar_ready", "ag_ready", "u_ready",
            "s_ready", "o_ready", "rk_ready", "ab_ready", "sg_ready", "cum_ready", "exps_ready", "q_ready", "silu_done",
            "zg_ready", "ms_ready", "rms_ready", "mix_ready", "o_copied", "xn_ready", "fs_ready", "fr_ready", "stored",
            "own", "res_own", "act_own", "pool_own", "kwt_done")}
        col = {n: row[:, a:b] for n, (a, b) in COLS.items()}
        scale_g = GDK ** -0.5

        with nc.Block() as block:
            @block.sync
            def _(sp):
                def load_row(i):
                    sp.dma_start(row[:, :], rows(proj, i)).then_inc(S["row_in"], 16)

                def load_values(i):
                    r = rows(proj, i)
                    for n, c in enumerate(("rv", "gv")):
                        sp.dma_start(vv[:, n, :], r[:, COLS[c][0]:COLS[c][1]]).then_inc(S["v_in"], 16)
                    sp.dma_start(mo[:, :], rows(mla_o, i)).then_inc(S["v_in"], 16)

                def store(i):
                    sp.wait_ge(S["xn_ready"], i + 1)
                    sp.dma_start(rows(out, i), xn[:, :]).then_inc(S["stored"], 16)

                def turn(i):
                    sp.wait_ge(S["zg_ready"], i + 1)
                    sp.wait_ge(S["rs_ready"], i + 1)
                    load_row(i + 1)
                    sp.wait_ge(S["mix_ready"], i + 1)
                    load_values(i + 1)

                load_row(0)
                load_values(0)
                sp.dma_start(g2[:, :], w_g2).then_inc(S["small_in"], 16)
                with nc.allow_non_contiguous_dma(reason="one bias per partition"):
                    sp.dma_start(bg[:, :], b_g2.rearrange("o (p a) -> p (o a)", a=1)).then_inc(S["small_in"], 16)
                sp.dma_start(gn[:, :], gla_norm.partition_broadcast(P)).then_inc(S["small_in"], 16)
                if final:
                    sp.dma_start(fn[:, :], final_norm.partition_broadcast(P)).then_inc(S["small_in"], 16)
                for k in range(KC):
                    sp.dma_start(w[:, k, :], w_out[k * P:(k + 1) * P, :]).then_inc(S["w_in"], 16)
                sp.dma_start(xr[:, :], rows(x, 0)).then_inc(S["x_in"], 16)
                turn(0)
                with sp.Fori(1, TILES - 1) as i:
                    store(i - 1)
                    sp.dma_start(xr[:, :], rows(x, i)).then_inc(S["x_in"], 16)
                    turn(i)
                store(TILES - 2)
                sp.dma_start(xr[:, :], rows(x, TILES - 1)).then_inc(S["x_in"], 16)
                store(TILES - 1)
                sp.wait_ge(S["stored"], 16 * (TILES + 1))

            @block.gpsimd
            def _(pool):
                pool.memset(half[:, :], -0.5).then_inc(S["pool_own"], 1)
                pool.memset(s_r[:, 2, :, :], 0.0).then_inc(S["pool_own"], 1)
                pool.memset(s_g[:, 2, :], 0.0).then_inc(S["pool_own"], 1)
                pool.memset(rkT[:, :, :], 0.0).then_inc(S["pool_own"], 1)
                pool.wait_ge(S["pool_own"], 4)
                pool.wait_ge(S["small_in"], 64 if final else 48)

                def final_power(i):
                    pool.wait_ge(S["fs_ready"], i + 1)
                    pool.tensor_tensor(fr[:, :], fs[:, 1:2], half[:, 0:1], ALU.pow).then_inc(S["fr_ready"], 1)

                def tile(i):
                    pool.wait_ge(S["row_in"], 16 * i + 16)
                    pool.tensor_tensor(rkw[:, :].rearrange("p (h c) -> p h c", h=RH), col["rk"].rearrange("p (h c) -> p h c", h=RH),
                                       K["rkw"].unsqueeze(2).to_broadcast([P, RH, RD]), ALU.mult).then_inc(S["rk_ready"], 1)
                    pool.wait_ge(S["t_copied"], 3 * i + 1)
                    pool.tensor_tensor(rqw[:, :, :], rT[:, :, :], K["rqw"].rearrange("p (a c) -> p a c", a=2),
                                       ALU.mult).then_inc(S["rk_ready"], 1)
                    if final and not (isinstance(i, int) and i == 0):
                        final_power(i - 1)
                    pool.wait_ge(S["silu_done"], 3 * i + 3)
                    g = zs[:, 768:].rearrange("p (h c) -> p h c", h=GH)
                    pool.tensor_tensor(g, g, gn[:, :].unsqueeze(1).to_broadcast([P, GH, GDV]), ALU.mult).then_inc(S["zg_ready"], 1)
                    pool.wait_ge(S["ms_ready"], i + 1)
                    pool.tensor_tensor(rs[:, :], ms[:, :], half[:, :], ALU.pow).then_inc(S["rms_ready"], 1)

                tile(0)
                with pool.Fori(1, TILES) as i:
                    tile(i)
                if final:
                    final_power(TILES - 1)

            @block.tensor
            def _(pe):
                T, M = nc.tensor.transpose, nc.tensor.matmul

                def open_tile(i):
                    pe.wait_ge(S["row_in"], 16 * i + 16)
                    for n in range(4):
                        last = T(tA[:, n, :], row[:, n * P:(n + 1) * P], K["ident"])
                    last.then_inc(S["t_ready"], 1)
                    T(tB[:, 0, :], col["gq"], K["ident"])
                    T(tB[:, 1, :], col["gk"], K["ident"])
                    T(tB[0:GRANK, 2, :], col["gg"], K["ident"]).then_inc(S["t_ready"], 1)
                    pe.wait_ge(S["small_in"], 64 if final else 48)
                    pe.wait_ge(S["t_copied"], 3 * i + 3)
                    M(tB[:, 3, :], g2[:, :], ggT[:, :], start=True, stop=True).then_inc(S["z_ready"], 1)
                    for h in range(RH):
                        for c in range(2):
                            t = slice(c * CH, (c + 1) * CH)
                            last = M(sc[t, h // 2, h % 2 * CH:(h % 2 + 1) * CH], rkT[:, h, t], rT[:, h // 2, t],
                                     start=True, stop=True)
                    last.then_inc(S["rs_ready"], 1)

                def project(i):
                    pe.wait_ge(S["mix_ready"], i + 1)
                    for b, bank in enumerate((tA, tB)):
                        for k in range(4):
                            last = T(bank[:, k, :], mixed[:, (4 * b + k) * P:(4 * b + k + 1) * P], K["ident"])
                        last.then_inc(S["mt_ready"], 1)
                    pe.wait_ge(S["w_in"], 16 * KC)
                    pe.wait_ge(S["mt_copied"], 2 * i + 2)
                    for c in range(2):
                        pe.wait_ge(S["x_part"], 2 * i + c + 1)
                        for k in range(KC):
                            last = M(acc[:, :], mT[:, k, :], w[:, k, c * HALF:(c + 1) * HALF], start=(k == 0), stop=(k == KC - 1))
                        last.then_inc(S["acc_ready"], 1)

                def close_tile(i):
                    pe.wait_ge(S["q_ready"], i + 1)
                    T(sc[:, 2, :], kwT[:, :], K["ident"]).then_inc(S["kwt_ready"], 1)
                    for n, (k_, q_) in enumerate(((knegm, qpos), (kposm, qneg))):
                        for h in range(GH):
                            for c in range(2):
                                t = slice(c * CH, (c + 1) * CH)
                                last = M(pf[t, 2 * n + h // 2, h % 2 * CH:(h % 2 + 1) * CH], k_[:, h, t], q_[:, t], start=True, stop=True)
                    last.then_inc(S["gs_ready"], 1)
                    pe.wait_ge(S["v_in"], 48 * i + 48)
                    pe.wait_ge(S["rk_ready"], 2 * i + 2)
                    pe.wait_ge(S["kw_ready"], i + 1)
                    for c in range(2):
                        t = slice(c * CH, (c + 1) * CH)
                        for p in range(2):
                            M((u0, u1)[c][:, p * P:(p + 1) * P], rkw[t, p * P:(p + 1) * P], vv[t, 0, p * P:(p + 1) * P],
                              start=True, stop=True)
                        last = M((u0, u1)[c][:, 256:512], kw[t, :], vv[t, 1, :], start=True, stop=True)
                    last.then_inc(S["u_ready"], 1)
                    pe.wait_ge(S["ar_ready"], i + 1)
                    pe.wait_ge(S["ag_ready"], i + 1)
                    pe.wait_ge(S["s_ready"], i + 1)
                    for c in range(2):
                        t = slice(c * CH, (c + 1) * CH)
                        for p in range(2):
                            M(op[t, p * P:(p + 1) * P], rqw[:, p, t], s_r[:, c, p, :], start=True, stop=False)
                            for h in (2 * p, 2 * p + 1):
                                M(op[t, h * RD:(h + 1) * RD], a_r[t, h, :], vv[t, 0, h * RD:(h + 1) * RD], start=False, stop=(h % 2 == 1))
                        M(op[t, 256:512], qpos[:, t], s_g[:, c, :], start=True, stop=False)
                        for h in range(GH):
                            last = M(op[t, 256 + h * GDV:256 + (h + 1) * GDV], a_g[t, h, :], vv[t, 1, h * GDV:(h + 1) * GDV],
                                     start=False, stop=(h == GH - 1))
                    last.then_inc(S["o_ready"], 1)

                open_tile(0)
                close_tile(0)
                with pe.Fori(1, TILES) as i:
                    open_tile(i)
                    pe.wait_ge(S["z_done"], i + 1)
                    project(i - 1)
                    close_tile(i)
                project(TILES - 1)

            @block.scalar
            def _(act):
                def copies(i):
                    act.wait_ge(S["t_ready"], 2 * i + 1)
                    act.copy(rT[:, :, :], tA[:, 0:2, :])
                    for h in range(2):
                        r = slice(RD * h, RD * h + RD)
                        last = act.copy(rkT[r, h::2, :], tA[r, 2:4, :])
                    last.then_inc(S["t_copied"], 1)
                    act.wait_ge(S["t_ready"], 2 * i + 2)
                    act.copy(gT[:, :, :], tB[:, 0:2, :]).then_inc(S["t_copied"], 1)
                    act.copy(ggT[:, :], tB[0:GRANK, 2, :]).then_inc(S["t_copied"], 1)

                def mixed_copies(i):
                    for b, bank in enumerate((tA, tB)):
                        act.wait_ge(S["mt_ready"], 2 * i + b + 1)
                        act.copy(mT[:, 4 * b:4 * b + 4, :], bank[:, :, :]).then_inc(S["mt_copied"], 1)

                def gates(i):
                    ch = Chain(act, S["act_own"], i)
                    act.wait_ge(S["ab_ready"], i + 1)
                    ch(act.activation(ab[:, :], ab[:, :], ACT.Exp, scale=-1.0))
                    ch.wait()
                    act.activation(sg[:, :], ab[:, :], ACT.Ln, bias=1.0).then_inc(S["sg_ready"], 1)
                    act.wait_ge(S["cum_ready"], i + 1)
                    act.activation(epos[:, :], cum[:, :], ACT.Exp, scale=1.0 / 16).then_inc(S["exps_ready"], 1)
                    act.activation(eneg[:, :], cum[:, :], ACT.Exp, scale=-1.0 / 16).then_inc(S["exps_ready"], 1)
                    for c in range(2):
                        t = slice(c * CH, (c + 1) * CH)
                        act.activation(el[:, t], cum[:, t], ACT.Exp, scale=-1.0 / 16, bias=last2[:, c:c + 1]).then_inc(S["exps_ready"], 1)
                    act.activation(elast[:, :], last2[:, :], ACT.Exp).then_inc(S["exps_ready"], 1)

                def silus(i):
                    for n, (c, a) in enumerate((("rz", 0), ("mz", 256), ("gz", 768))):
                        width = COLS[c][1] - COLS[c][0]
                        act.activation(zs[:, a:a + width], col[c], ACT.Silu).then_inc(S["silu_done"], 1)

                act.sem_inc(S["stored"], 16)
                act.wait_ge(S["pool_own"], 4)
                copies(0)
                gates(0)
                silus(0)
                with act.Fori(1, TILES) as i:
                    copies(i)
                    mixed_copies(i - 1)
                    gates(i)
                    act.wait_ge(S["mix_ready"], i)
                    silus(i)
                mixed_copies(TILES - 1)

            @block.vector
            def _(dve):
                dve.sem_inc(S["x_part"], 1)
                n_res = 5 if final else 2
                n_tile = 31

                def residual(i):
                    ch = Chain(dve, S["res_own"], n_res * i)
                    dve.wait_ge(S["x_in"], 16 * i + 16)
                    dve.wait_ge(S["stored"], 16 * i + 16)
                    for c in range(2):
                        s = slice(c * HALF, (c + 1) * HALF)
                        dve.wait_ge(S["acc_ready"], 2 * i + c + 1)
                        dve.tensor_tensor(xn[:, s], acc[:, :], mod[:, 2, s], ALU.mult).then_inc(S["x_part"], 1)
                        dve.wait_ge(S["x_part"], 2 * i + c + 2)
                        ch(dve.tensor_tensor(xn[:, s], xn[:, s], xr[:, s], ALU.add))
                    ch.wait()
                    if final:
                        ch(dve.tensor_tensor(junk[:, :], xn[:, :], xn[:, :], ALU.mult))
                        ch.wait()
                        ch(dve.reduce_sum(fs[:, 0:1], junk[:, :], axis=AX.X))
                        ch.wait()
                        dve.tensor_scalar(fs[:, 1:2], fs[:, 0:1], 1.0 / D, RMS_EPS, ALU.mult, ALU.add).then_inc(S["fs_ready"], 1)
                        dve.wait_ge(S["fr_ready"], i + 1)
                        ch(dve.scalar_tensor_tensor(xn[:, :], xn[:, :], fr[:, 0:1], fn[:, :], ALU.mult, ALU.mult))
                        ch.wait()
                    assert ch.n == n_res
                    dve.sem_inc(S["xn_ready"], 1)

                def tile(i):
                    ch = Chain(dve, S["own"], n_tile * i + 1)
                    dve.wait_ge(S["z_ready"], i + 1)
                    ch(dve.tensor_scalar(z[:, :], tB[:, 3, :], bg[:, 0:1], None, ALU.add))
                    ch.wait()
                    dve.sem_inc(S["z_done"], 1)
                    dve.scalar_tensor_tensor(ab[:, :], z[:, :], -1.0, z[:, :], ALU.mult, ALU.max).then_inc(S["ab_ready"], 1)
                    ch(dve.tensor_scalar(mn[:, :], z[:, :], 0.0, None, ALU.min))
                    dve.wait_ge(S["rs_ready"], i + 1)
                    dve.tensor_tensor(a_r[:, :, :], sc[:, 0:2, :].rearrange("p a (b c) -> p (a b) c", c=CH),
                                      K["decay"].rearrange("p (h c) -> p h c", h=RH), ALU.mult).then_inc(S["ar_ready"], 1)
                    ch.wait()
                    dve.wait_ge(S["sg_ready"], i + 1)
                    ch(dve.tensor_tensor(la[:, :], mn[:, :], sg[:, :], ALU.subtract))
                    ch.wait()
                    ch(dve.tensor_tensor_scan(cum[:, :], K["scan"], la[:, :], 0.0, ALU.mult, ALU.add))
                    ch.wait()
                    dve.tensor_scalar(last2[:, :], cum[:, CH - 1::CH], 1.0 / 16, None, ALU.mult).then_inc(S["cum_ready"], 1)
                    dve.wait_ge(S["exps_ready"], 5 * i + 5)
                    ch(dve.tensor_tensor(qpos[:, :], gT[:, 0, :], epos[:, :], ALU.mult))
                    ch(dve.tensor_tensor(qneg[:, :], gT[:, 0, :], eneg[:, :], ALU.mult))
                    for dst, e in ((kneg, eneg), (kpos, epos), (kwT, el)):
                        ch(dve.scalar_tensor_tensor(dst[:, :], gT[:, 1, :], scale_g, e[:, :], ALU.mult, ALU.mult))
                    ch.wait()
                    hm = K["ghead"].unsqueeze(2).to_broadcast([P, GH, P])
                    ch(dve.tensor_tensor(knegm[:, :, :], kneg[:, :].unsqueeze(1).to_broadcast([P, GH, P]), hm, ALU.mult))
                    ch(dve.tensor_tensor(kposm[:, :, :], kpos[:, :].unsqueeze(1).to_broadcast([P, GH, P]), hm, ALU.mult))
                    ch.wait()
                    dve.sem_inc(S["q_ready"], 1)
                    if not isinstance(i, int):
                        residual(i - 1)
                    dve.wait_ge(S["kwt_ready"], i + 1)
                    dve.tensor_copy(kw[:, :], sc[:, 2, :]).then_inc(S["kw_ready"], 1)
                    dve.wait_ge(S["gs_ready"], i + 1)
                    ch(dve.tensor_copy(a_g[:, :, :], pf[:, 2:4, :].rearrange("p a (b c) -> p (a b) c", c=CH)))
                    ch.wait()
                    settle(dve)
                    dve.copy_predicated(a_g[:, :, :], past[:, :, :], pf[:, 0:2, :].rearrange("p a (b c) -> p (a b) c", c=CH)).then_inc(S["ag_ready"], 1)
                    dve.wait_ge(S["u_ready"], i + 1)
                    for c, bank in enumerate((u0, u1)):
                        ch(dve.tensor_tensor(um_r[:, c, :, :], bank[:, 0:256].rearrange("p (a c) -> p a c", a=2),
                                             K["rbd"].unsqueeze(1).to_broadcast([P, 2, P]), ALU.mult))
                        ch(dve.tensor_tensor(um_g[:, c, :], bank[:, 256:512], K["gbd"], ALU.mult))
                    ch(dve.tensor_copy(s_r[:, 0, :, :], s_r[:, 2, :, :]))
                    ch(dve.tensor_copy(s_g[:, 0, :], s_g[:, 2, :]))
                    ch.wait()
                    for c in range(2):
                        for p in range(2):
                            ch(dve.scalar_tensor_tensor(s_r[:, c + 1, p, :], s_r[:, c, p, :], K["ra"][:, p:p + 1], um_r[:, c, p, :], ALU.mult, ALU.add))
                        ch(dve.scalar_tensor_tensor(s_g[:, c + 1, :], s_g[:, c, :], elast[:, c:c + 1], um_g[:, c, :], ALU.mult, ALU.add))
                        ch.wait()
                    dve.sem_inc(S["s_ready"], 1)
                    dve.wait_ge(S["o_ready"], i + 1)
                    ch(dve.tensor_copy(o[:, :, :], op[:, :].rearrange("p (h c) -> p h c", h=8)))
                    ch.wait()
                    ch(dve.tensor_tensor(osq[:, :, :], o[:, :, :], o[:, :, :], ALU.mult))
                    ch.wait()
                    ch(dve.reduce_sum(ms[:, :], osq[:, :, :], axis=AX.X))
                    ch.wait()
                    dve.tensor_scalar(ms[:, :], ms[:, :], 1.0 / 64, RMS_EPS, ALU.mult, ALU.add).then_inc(S["ms_ready"], 1)
                    dve.wait_ge(S["zg_ready"], i + 1)
                    ch(dve.tensor_tensor(mixed[:, 256:768], mo[:, :], zs[:, 256:768], ALU.mult))
                    dve.wait_ge(S["rms_ready"], i + 1)
                    ch(dve.tensor_tensor(o[:, :, :], o[:, :, :], rs[:, :].unsqueeze(2).to_broadcast([P, 8, 64]), ALU.mult))
                    ch.wait()
                    o2 = o[:, :, :].rearrange("p h c -> p (h c)")
                    ch(dve.tensor_tensor(mixed[:, 0:256], o2[:, 0:256], zs[:, 0:256], ALU.mult))
                    ch(dve.tensor_tensor(mixed[:, 768:], o2[:, 256:], zs[:, 768:], ALU.mult))
                    ch.wait()
                    dve.sem_inc(S["mix_ready"], 1)
                    assert ch.n == n_tile, ch.n

                ch = Chain(dve, S["own"])
                ch(dve.tensor_copy(past[:, :, :], K["past"].unsqueeze(1).to_broadcast([P, GH, CH])))
                ch.wait()
                dve.wait_ge(S["small_in"], 64 if final else 48)
                dve.wait_ge(S["pool_own"], 4)
                tile(0)
                with dve.Fori(1, TILES) as i:
                    tile(i)
                residual(TILES - 1)


def program(nc, A, consts, out):
    def scratch(name, *shape):
        return nc.dram_tensor(f"scratch_{name}", shape, F32, kind="Internal").ap()

    qkv, mix, y = scratch("qkv", SEQ, QKV), scratch("mix", SEQ, D), scratch("y", BLOCKS * P, D)
    h = [scratch(f"h{n}", SEQ, D) for n in range(4)]
    proj, mla_o, x1 = scratch("proj", SEQ, IN_COLS), scratch("mla_o", SEQ, MH * MV), scratch("x1", SEQ, D)
    mq, mk, mkv = scratch("mq", SEQ, MH * MQ), scratch("mk", SEQ, MH * MQ), scratch("mkv", SEQ, MH * (NOPE + MV))

    with ExitStack() as stack:
        def held(name, shape, dt=F32):
            return stack.enter_context(nc.sbuf_tensor(name, shape, dt))

        logits = held("logits", [P, TILES, GROUPS + EXPERTS])
        gates, dest_i = held("gates", [P, 2, TILES]), held("dest_i", [P, 2, TILES], I32)
        tok_i, blk_i, pairs_i = held("tok_i", [P, BCOLS], I32), held("blk_i", [P, BCOLS], I32), held("pairs_i", [P, 1], I32)
        mod, tabs = held("mod", [P, 3, D]), held("tabs", [P, 2, TILES, RD // 2])

        def moe_layer(K, l, mix_w, h_in, h_mid, h_out):
            r = slice(l, l + 1)
            phase_out_norm(nc, K, f"out{l}", mix, mix_w, h_in, A["ln_g"][l, 0:1, :], A["ln_b"][l, 0:1, :],
                           A["moe_w_grp_router"][l], A["moe_b_grp_router"][r, :], A["moe_w_exp_router"][l],
                           A["moe_b_exp_router"][r, :], h_mid, logits)
            phase_route(nc, K, f"route{l}", logits, gates, dest_i, tok_i, blk_i, pairs_i)
            phase_experts(nc, K, f"experts{l}", h_mid, A["moe_w_gate"][l], A["moe_w_up"][l], A["moe_w_down"][l],
                          tok_i, blk_i, pairs_i, y)
            phase_combine(nc, K, f"combine{l}", h_mid, y, gates, dest_i, A["ln_g"][l, 1:2, :], A["ln_b"][l, 1:2, :], h_out)

        def body(K):
            x = A["x"][0]
            phase_qkv(nc, K, x, A["attn_w_qkv"][0], qkv, y)
            diff_attention(nc, K, qkv, [A[f"attn_{n}"] for n in ("lq1", "lk1", "lq2", "lk2")], A["attn_sub_g"], mix)
            moe_layer(K, 0, A["attn_w_o"][0], x, h[0], h[1])
            phase_pool(nc, K, h[1], A["pool_w_in"][0], A["pool_w_grp"][0], A["pool_scale"], mix)
            moe_layer(K, 1, A["pool_w_out"][0], h[1], h[2], h[3])
            phase_angles(nc, K, A["positions_2"], tabs)
            src = h[3]
            for l in range(2):
                r = slice(l, l + 1)
                phase_modulation(nc, K, f"mod{l}", A["c_2"], A["ada_w_2"][l], A["ada_b_2"][r, :], A["norm_w_2"][r, :], mod)
                phase_project(nc, K, f"project{l}", src, A["w_in_2"][l], A["mla_q_norm_2"][r, :], A["w_uq_2"][l],
                              A["mla_kv_norm_2"][r, :], A["w_ukv_2"][l], mod, tabs, proj, mq, mk, mkv)
                mla_attention(nc, K, f"mla{l}", mq, mk, mkv, mla_o)
                phase_mix_out(nc, K, f"mixout{l}", proj, mla_o, src, A["gla_w_g2_2"][l], A["gla_b_g2_2"][r, :],
                              A["gla_norm_2"][r, :], A["w_out_2"][l], mod,
                              A["final_norm_2"].rearrange("(a n) -> a n", a=1) if l == 1 else None, out[0] if l == 1 else x1)
                src = x1

        with_constants(nc, stack, consts, body)


_INS = ["x", "attn_w_qkv", "attn_w_o", "attn_lq1", "attn_lk1", "attn_lq2", "attn_lk2", "attn_sub_g", "pool_w_in",
        "pool_w_grp", "pool_scale", "pool_w_out", "ln_g", "ln_b", "moe_w_grp_router", "moe_b_grp_router",
        "moe_w_exp_router", "moe_b_exp_router", "moe_w_gate", "moe_w_up", "moe_w_down", "c_2", "positions_2",
        "norm_w_2", "ada_w_2", "ada_b_2", "w_in_2", "mla_q_norm_2", "w_uq_2", "mla_kv_norm_2", "w_ukv_2",
        "gla_w_g2_2", "gla_b_g2_2", "gla_norm_2", "w_out_2", "final_norm_2"]


def kernel(**inputs):
    import concourse.bacc as bacc
    from concourse.bass_utils import run_bass_kernel_spmd

    nc = bacc.Bacc("TRN2", target_bir_lowering=False, num_devices=1)
    arrays, args = {}, {}
    for name in _INS:
        a = np.ascontiguousarray(inputs[name])
        arrays[f"in_{name}_dram"] = a
        args[name] = nc.dram_tensor(f"in_{name}_dram", a.shape, mybir.dt.from_np(a.dtype), kind="ExternalInput").ap()
    packed = np.concatenate(list(constant_parts().values()), axis=1)
    arrays["consts_dram"] = packed
    consts = nc.dram_tensor("consts_dram", packed.shape, F32, kind="ExternalInput").ap()
    out = nc.dram_tensor("out_0_dram", (1, SEQ, D), F32, kind="ExternalOutput").ap()
    program(nc, args, consts, out)
    r = run_bass_kernel_spmd(nc, [arrays], core_ids=[0])
    return r.results[0]["out_0_dram"]
```

```python
import math
from contextlib import ExitStack

import numpy as np
import concourse.bass as bass
from concourse import mybir

F32 = mybir.dt.float32
I32 = mybir.dt.int32
ALU = mybir.AluOpType
ACT = mybir.ActivationFunctionType
AX = mybir.AxisListType

P = 128
SEQ = 1024
D = 1024
TILES = SEQ // P
KC = D // P
HALF = 512

HEADS = 8
HD = 64
VD = 2 * HD
QKV = 3 * D
ROT = HD // 4
LAMBDA_INIT = 0.8 - 0.6 * math.exp(0.0)
ALPHA = 4 ** 0.25
LN_EPS = 1e-5
RMS_EPS = 1e-6
NEG = -1.0e30

GROUPS, PER_GROUP = 4, 8
EXPERTS = GROUPS * PER_GROUP
DE = D // 2
OVER = 2 * SEQ // P
BLOCKS = EXPERTS + OVER
BCOLS = BLOCKS + 2
POOL_WINDOWS = (2, 4, 8, 16)
PG = D // len(POOL_WINDOWS)

RH, RD = 4, 64
MH, NOPE, ROPE_D, MV = 8, 64, 32, 64
MQ = NOPE + ROPE_D
MQR, MKVR = 256, 128
GH, GDK, GDV, GRANK = 4, 32, 64, 16
CH = 64
COLS = {}
_at = 0
for _n, _w in (("rq", 256), ("rk", 256), ("rv", 256), ("rz", 256), ("mq", 256), ("mkv", 128), ("mkr", 32),
               ("mz", 512), ("gq", 128), ("gk", 128), ("gv", 256), ("gg", 16), ("gz", 256)):
    COLS[_n] = (_at, _at + _w)
    _at += _w
IN_COLS = _at
NCHUNK = 6
CW = IN_COLS // NCHUNK


def constant_parts():
    p = np.arange(P)[:, None]
    c = np.arange(P)[None, :]
    f = np.float32
    parts = {
        "ident": (p == c).astype(f),
        "causal": np.where(c > p, f(NEG), f(0)),
        "chunked": np.where((c >= CH) & (p < CH), f(NEG), f(0)),
        "before": (p < c).astype(f),
        "iota": np.broadcast_to(np.arange(P, dtype=f), (P, P)),
        "token": (p + P * np.arange(TILES)[None, :]).astype(f),
    }
    inv = f(500000.0) ** (-np.arange(0, ROT, 2, dtype=f) / f(ROT))
    ang = np.arange(SEQ, dtype=f)[:, None] * inv[None, :].astype(f)
    for name, t in (("rcos", np.cos(ang)), ("rsin", np.sin(ang))):
        parts[name] = t.astype(f).reshape(TILES, P, ROT // 2).transpose(1, 0, 2).reshape(P, -1)
    parts["inv"] = np.broadcast_to(f(10000.0) ** (-np.arange(RD // 2, dtype=f) / f(RD // 2)), (P, RD // 2))
    lg = np.log1p(-np.exp2(-5.0 - np.arange(RH, dtype=f))).astype(np.float64)
    j, i = np.arange(P)[:, None, None] % CH, np.arange(CH)[None, None, :]
    scale = RD ** -0.5
    parts["decay"] = (np.exp(lg[None, :, None] * np.abs(i - j)) * scale).reshape(P, -1)
    head = 2 * np.arange(2)[None, :, None] + (np.arange(P) // RD)[:, None, None]
    parts["rqw"] = np.exp(lg[head] * (np.arange(P)[None, None, :] % CH + 1.0)).reshape(P, -1)
    parts["rkw"] = np.exp(lg[None, :] * (CH - 1.0 - np.arange(P)[:, None] % CH)) * scale
    parts["ra"] = np.exp(CH * lg[head[:, :, 0]])
    parts["rbd"] = (p // RD == c // RD).astype(f)
    parts["gbd"] = (p // GDK == np.arange(GH * GDV)[None, :] // GDV).astype(f)
    parts["ghead"] = (p // GDK == np.arange(GH)[None, :]).astype(f)
    parts["scan"] = np.broadcast_to((np.arange(P) % CH != 0).astype(f), (P, P))
    parts["past"] = (np.arange(CH)[None, :] >= p % CH).astype(f)
    return {n: np.ascontiguousarray(a, dtype=f) for n, a in parts.items()}


def inverse_counts():
    t = np.arange(SEQ)
    return np.stack([1.0 / np.minimum(t + 1, w) for w in POOL_WINDOWS]).astype(np.float32).reshape(1, -1)


class Phase:

    def __init__(self, nc, name):
        self.nc, self.name = nc, name

    def __enter__(self):
        self.stack = ExitStack()
        self.sems = []
        return self

    def sb(self, name, shape, dt=F32):
        return self.stack.enter_context(self.nc.sbuf_tensor(f"{self.name}_{name}", shape, dt))

    def ps(self, name, shape):
        return self.stack.enter_context(self.nc.psum_tensor(f"{self.name}_{name}", shape, F32))

    def sem(self, name):
        s = self.nc.alloc_semaphore(f"{self.name}_{name}")
        self.sems.append(s)
        return s

    def __exit__(self, *exc):
        self.stack.close()
        if exc[0] is None:
            self.nc.clear_and_free_semaphores(self.sems)
            self.nc.all_engine_barrier()


class Chain:

    def __init__(self, eng, sem, base=0):
        self.eng, self.sem, self.base, self.n = eng, sem, base, 0

    def __call__(self, ins):
        self.n += 1
        ins.then_inc(self.sem, 1)
        return ins

    def wait(self):
        self.eng.wait_ge(self.sem, self.base + self.n)


def rows(ap, i):
    return ap[i * P:(i + 1) * P, :] if isinstance(i, int) else ap[bass.ds(i * P, P), :]


def load_columns(eng, w, src, c, width, ready):
    s = slice(c * width, (c + 1) * width)
    eng.dma_start(w[:, :, s], src[:, s].rearrange("(k p) n -> p k n", p=P)).then_inc(ready, 16)


SETTLED = []


def settle(eng):
    eng.sem_inc(SETTLED[-1], 1)


class Angles:

    def __init__(self, ph, K, positions, tabs):
        self.K, self.positions, self.tabs = K, positions, tabs
        n = RD // 2
        self.pi, self.pf = ph.sb("pos_i", [P, TILES], I32), ph.sb("pos_f", [P, TILES])
        self.ang, self.kf = ph.sb("ang", [P, TILES, n]), ph.sb("kf", [P, TILES, n])
        self.r = ph.sb("rest", [P, 2, TILES, n])
        self.ki = ph.sb("ki", [P, TILES, n], I32)
        self.p_in, self.own, self.r_ready, self.t_ready = (ph.sem(n) for n in ("p_in", "ang_own", "rest_ready", "tabs_ready"))

    def load(self, nc, sp):
        with nc.allow_non_contiguous_dma(reason="1024 positions"):
            sp.dma_start(self.pi[:, :], self.positions.rearrange("o (t p) -> p (o t)", p=P)).then_inc(self.p_in, 16)

    def reduce(self, dve):
        two_pi = 2 * math.pi
        c1 = 6.28125
        c2 = float(np.float32(np.round((two_pi - c1) * 2 ** 22) / 2 ** 22))
        c3 = two_pi - c1 - c2
        ch = Chain(dve, self.own)
        pf, ang, kf, ki = self.pf, self.ang, self.kf, self.ki
        shape = [P, TILES, RD // 2]

        def step(ins):
            ch(ins)
            ch.wait()

        dve.wait_ge(self.p_in, 16)
        step(dve.tensor_copy(pf[:, :], self.pi[:, :]))
        step(dve.tensor_tensor(ang[:, :, :], pf[:, :].unsqueeze(2).to_broadcast(shape),
                               self.K["inv"].unsqueeze(1).to_broadcast(shape), ALU.mult))
        for n, turn in enumerate((0.25, 0.0)):
            r = self.r[:, n, :, :]
            step(dve.tensor_scalar(kf[:, :, :], ang[:, :, :], 1.0 / two_pi, turn, ALU.mult, ALU.add))
            step(dve.tensor_copy(ki[:, :, :], kf[:, :, :]))
            step(dve.tensor_copy(kf[:, :, :], ki[:, :, :]))
            step(dve.scalar_tensor_tensor(r, kf[:, :, :], -c1, ang[:, :, :], ALU.mult, ALU.add))
            step(dve.scalar_tensor_tensor(r, kf[:, :, :], -c2, r, ALU.mult, ALU.add))
            step(dve.scalar_tensor_tensor(r, kf[:, :, :], -c3, r, ALU.mult, ALU.add))
            step(dve.tensor_scalar(r, r, turn * two_pi, None, ALU.add))
            for op, whole in ((ALU.is_gt, -1), (ALU.is_lt, 1)):
                step(dve.tensor_scalar(kf[:, :, :], r, -whole * math.pi, whole * two_pi, op, ALU.mult))
                step(dve.tensor_tensor(r, r, kf[:, :, :], ALU.add))
            dve.tensor_scalar(r, r, 3.1415925, -3.1415925, ALU.min, ALU.max).then_inc(self.r_ready, 1)

    def sines(self, act):
        act.wait_ge(self.r_ready, 2)
        act.activation(self.tabs[:, :, :, :], self.r[:, :, :, :], ACT.Sin).then_inc(self.t_ready, 1)


class Modulation:

    def __init__(self, ph, c, ada_w, ada_b, norm_w, mods):
        assert KC == HEADS
        self.c, self.ada_w, self.ada_b, self.norm_w, self.mods = c, ada_w, ada_b, norm_w, mods
        self.cs, self.ck = ph.sb("c", [P, KC]), ph.sb("ck", [P, 2])
        self.w = ph.sb("ada", [P, 2, 3 * D])
        self.acc = ph.sb("ada_sum", [P, 2, 3 * D])
        self.nw = ph.sb("nw", [P, 2, D])
        self.ones = ph.sb("ones", [P, P])
        self.w_in = [ph.sem(f"ada_in{l}") for l in range(2)]
        self.c_in, self.b_in, self.nw_in, self.cleared, self.c_act, self.taken, self.scaled, self.step, self.m_ready, self.m_done = (
            ph.sem(n) for n in ("c_in", "b_in", "nw_in", "cleared", "c_act", "ada_taken", "ada_scaled", "ada_step", "mod_ready", "mod_done"))

    def load_small(self, nc, sp):
        with nc.allow_non_contiguous_dma(reason="one column of c"):
            sp.dma_start(self.cs[:, :], self.c.rearrange("o (k p) -> p (o k)", p=P)).then_inc(self.c_in, 16)
        for l in range(2):
            sp.dma_start(self.nw[:, l, :], self.norm_w[l:l + 1, :].partition_broadcast(P)).then_inc(self.nw_in, 16)
        sp.wait_ge(self.cleared, 2)
        sp.dma_start(self.acc[0:1, :, :], self.ada_b.rearrange("(o l) n -> o l n", o=1)).then_inc(self.b_in, 16)

    def load(self, sp, h):
        for l in range(2):
            sp.wait_ge(self.step, 2 * h + l + 1)
            settle(sp)
            sp.dma_start(self.w[:, l, :], rows(self.ada_w[l], h)).then_inc(self.w_in[l], 16)

    def silu(self, act):
        act.wait_ge(self.c_in, 16)
        act.activation(self.cs[:, :], self.cs[:, :], ACT.Silu).then_inc(self.c_act, 1)

    def clear(self, pool):
        pool.memset(self.acc[:, :, :], 0.0).then_inc(self.cleared, 1)
        pool.memset(self.ones[:, :], 1.0).then_inc(self.cleared, 1)
        pool.sem_inc(self.step, 2)
        pool.wait_ge(self.b_in, 16)
        pool.wait_ge(self.c_act, 1)

    def add(self, pool, h, l):
        pool.tensor_copy(self.ck[:, l:l + 1], self.cs[:, bass.ds(h, 1)] if not isinstance(h, int) else self.cs[:, h:h + 1]).then_inc(self.taken, 1)
        pool.wait_ge(self.taken, 2 * h + l + 1)
        pool.wait_ge(self.w_in[l], 16 * h + 16)
        pool.wait_ge(self.step, 2 * h + l + 1)
        settle(pool)
        pool.tensor_scalar(self.w[:, l, :], self.w[:, l, :], self.ck[:, l:l + 1], None, ALU.mult).then_inc(self.scaled, 1)
        pool.wait_ge(self.scaled, 2 * h + l + 1)
        pool.tensor_tensor(self.acc[:, l, :], self.acc[:, l, :], self.w[:, l, :], ALU.add).then_inc(self.step, 1)

    def total(self, nc, pe, banks):
        pe.wait_ge(self.step, 2 * HEADS + 2)
        pe.wait_ge(self.cleared, 2)
        for l in range(2):
            for n in range(NCHUNK):
                g = NCHUNK * l + n
                if g >= len(banks):
                    pe.wait_ge(self.m_done, g - len(banks) + 1)
                nc.tensor.matmul(banks[g % len(banks)], self.ones[:, :], self.acc[:, l, n * HALF:(n + 1) * HALF],
                                 start=True, stop=True).then_inc(self.m_ready, 1)

    def put(self, dve, banks):
        dve.wait_ge(self.nw_in, 32)
        for l in range(2):
            for n in range(NCHUNK):
                g = NCHUNK * l + n
                part, s = n // 2, slice(n % 2 * HALF, (n % 2 + 1) * HALF)
                dve.wait_ge(self.m_ready, g + 1)
                src = banks[g % len(banks)]
                if part == 1:
                    dve.scalar_tensor_tensor(self.mods[:, l, 0, s], src, 1.0, self.nw[:, l, s], ALU.add, ALU.mult).then_inc(self.m_done, 1)
                else:
                    dve.tensor_copy(self.mods[:, l, 1 if part == 0 else 2, s], src).then_inc(self.m_done, 1)
        dve.wait_ge(self.m_done, 2 * NCHUNK)


def phase_qkv(nc, K, x, w_qkv, qkv, y=None, positions=None, tabs=None):
    with Phase(nc, "qkv") as ph:
        w = ph.sb("w", [P, KC, QKV])
        xin = ph.sb("x", [P, D])
        xT = ph.sb("xT", [P, KC, P])
        row = ph.sb("row", [P, QKV])
        t1 = ph.sb("t1", [P, 4, 32, ROT // 2])
        tp = ph.ps("tp", [P, 2, 4, P])
        acc = ph.ps("acc", [P, NCHUNK, HALF])
        w_in = [ph.sem(f"w_in{c}") for c in range(NCHUNK)]
        x_in, tp_ready, xT_ready = (ph.sem(n) for n in ("x_in", "tp_ready", "xT_ready"))
        acc_ready, row_ready, stored, rope = (ph.sem(n) for n in ("acc_ready", "row_ready", "stored", "rope"))
        rot_done, zero_set, zeroed = ph.sem("rot_done"), ph.sem("zero_set"), ph.sem("zeroed")
        zero = ph.sb("zero", [P, D])
        angles = Angles(ph, K, positions, tabs) if tabs is not None else None

        with nc.Block() as block:
            @block.sync
            def _(sp):
                sp.dma_start(xin[:, :], x[0:P, :]).then_inc(x_in, 16)
                for c in range(NCHUNK):
                    load_columns(sp, w, w_qkv, c, HALF, w_in[c])

                if angles:
                    angles.load(nc, sp)
                sp.wait_ge(zero_set, 1)
                if y is not None:
                    for b in range(EXPERTS, BLOCKS):
                        sp.dma_start(y[b * P:(b + 1) * P, :], zero[:, :]).then_inc(zeroed, 16)

                def store(i):
                    sp.wait_ge(rot_done, i + 1)
                    sp.dma_start(rows(qkv, i), row[:, :]).then_inc(stored, 16)

                with sp.Fori(0, TILES - 1) as i:
                    sp.wait_ge(tp_ready, 2 * i + 2)
                    sp.dma_start(xin[:, :], rows(x, i + 1)).then_inc(x_in, 16)
                    store(i)
                store(TILES - 1)
                sp.wait_ge(stored, 16 * (TILES + 1))
                if y is not None:
                    sp.wait_ge(zeroed, 16 * OVER)

            @block.gpsimd
            def _(pool):
                pool.memset(zero[:, :], 0.0).then_inc(zero_set, 1)

            @block.tensor
            def _(pe):
                with pe.Fori(0, TILES) as i:
                    pe.wait_ge(x_in, 16 * i + 16)
                    for b in range(2):
                        for k in range(4):
                            last = nc.tensor.transpose(tp[:, b, k, :], xin[:, (4 * b + k) * P:(4 * b + k + 1) * P],
                                                       K["ident"])
                        last.then_inc(tp_ready, 1)
                    pe.wait_ge(xT_ready, 2 * i + 2)
                    for c in range(NCHUNK):
                        pe.wait_ge(w_in[c], 16)
                        pe.wait_ge(row_ready, NCHUNK * i + c + 1)
                        for k in range(KC):
                            last = nc.tensor.matmul(acc[:, c, :], xT[:, k, :], w[:, k, c * HALF:(c + 1) * HALF],
                                                    start=(k == 0), stop=(k == KC - 1))
                        last.then_inc(acc_ready, 1)

            @block.scalar
            def _(act):
                for _ in range(NCHUNK):
                    act.sem_inc(row_ready, 1)
                act.sem_inc(stored, 16)
                with act.Fori(0, TILES) as i:
                    for b in range(2):
                        act.wait_ge(tp_ready, 2 * i + b + 1)
                        act.copy(xT[:, 4 * b:4 * b + 4, :], tp[:, b, :, :]).then_inc(xT_ready, 1)
                    for c in range(NCHUNK):
                        act.wait_ge(acc_ready, NCHUNK * i + c + 1)
                        if c == 0:
                            act.wait_ge(stored, 16 * i + 16)
                        act.copy(row[:, c * HALF:(c + 1) * HALF], acc[:, c, :]).then_inc(row_ready, 1)
                if angles:
                    angles.sines(act)

            @block.vector
            def _(dve):
                g = row[:, 0:2 * D].rearrange("p (h d) -> p h d", d=HD)
                r1, r2 = g[:, :, 0:ROT // 2], g[:, :, ROT // 2:ROT]
                if angles:
                    angles.reduce(dve)
                with dve.Fori(0, TILES) as i:
                    ch = Chain(dve, rope, 5 * i)
                    cos = K["rcos"].rearrange("p (t c) -> p t c", t=TILES)[:, bass.ds(i, 1), :].to_broadcast([P, 32, ROT // 2])
                    sin = K["rsin"].rearrange("p (t c) -> p t c", t=TILES)[:, bass.ds(i, 1), :].to_broadcast([P, 32, ROT // 2])
                    dve.wait_ge(row_ready, NCHUNK * (i + 1) + 4)
                    ch(dve.tensor_tensor(t1[:, 0], r1, cos, ALU.mult))
                    ch(dve.tensor_tensor(t1[:, 1], r2, sin, ALU.mult))
                    ch(dve.tensor_tensor(t1[:, 2], r1, sin, ALU.mult))
                    ch(dve.tensor_tensor(t1[:, 3], r2, cos, ALU.mult))
                    ch.wait()
                    ch(dve.tensor_tensor(r1, t1[:, 0], t1[:, 1], ALU.subtract))
                    dve.wait_ge(row_ready, NCHUNK * (i + 2))
                    dve.tensor_tensor(r2, t1[:, 2], t1[:, 3], ALU.add).then_inc(rot_done, 1)


def transpose_banks(n):
    return (n + 3) // 4


def phase_attention(nc, K, name, q, k, v, out, maps, dk, dv, mask, scale, lam_parts=None, sub_g=None, modulation=None):
    dq = maps * dk
    U = TILES * maps
    groups = [transpose_banks(i + 1) for i in range(TILES)]
    QK_AT = (2, 3, 4, 5)
    G = len(QK_AT) + sum(groups)
    QK_LAST = sum(groups[:QK_AT[-1] + 1]) + len(QK_AT)
    PSLOTS = 4
    diff = maps == 2
    NORM_AT = 3

    def score_banks(u):
        if u // maps < TILES // 2:
            return [u % 4], u - 4 if u >= 4 else u // 2 - 2
        return [2 * (u % 2), 2 * (u % 2) + 1], u - 2 if u - 2 >= U // 2 else U // 2 - 4 + 2 * (u % 2) + 1

    def each_head(eng, body):
        body(0, 0, 0, first=True, last=False)
        with eng.Fori(0, HEADS // 2 - 1) as p:
            body(2 * p + 1, 1, p, first=False, last=False)
            body(2 * p + 2, 0, p + 1, first=False, last=False)
        body(HEADS - 1, 1, HEADS // 2 - 1, first=False, last=True)

    with Phase(nc, name) as ph:
        qs, ks, vs = ph.sb("q", [P, TILES, dq]), ph.sb("k", [P, TILES, dq]), ph.sb("v", [P, 2, TILES, dv])
        qT, kT = ph.sb("qT", [dq, 2, SEQ]), ph.sb("kT", [dq, 2, SEQ])
        prob = ph.sb("prob", [P, PSLOTS, maps, SEQ])
        aT = ph.sb("aT", [P, TILES, P])
        o_sb = ph.sb("o", [P, 2, TILES, dv])
        mx, bias, total, inv = (ph.sb(n, [P, U]) for n in ("mx", "bias", "total", "inv"))
        s_ps = ph.ps("s", [P, 2 * SEQ])
        tp = ph.ps("tp", [P, 2, 4, P])
        o_ps = ph.ps("o_ps", [P, 2, HALF])
        qk_in, tp_ready, tp_copied, s_ready, exp_done, bias_ready, a_ready, o_ready, o_done, own = (
            ph.sem(n) for n in ("qk_in", "tp_ready", "tp_copied", "s_ready", "exp_done", "bias_ready",
                                "a_ready", "o_ready", "o_done", "own"))
        v_in, stored = ([ph.sem(f"{n}{b}") for b in range(2)] for n in ("v_in", "stored"))
        m = Modulation(ph, *modulation) if modulation else None
        if diff:
            lq = ph.sb("lq", [P, 4, HD])
            lt = ph.sb("lt", [P, 2, HD])
            ls = ph.sb("ls", [P, 4])
            lam = ph.sb("lam", [P, 1])
            gsub = ph.sb("gsub", [P, dv])
            sq = ph.sb("sq", [P, TILES, dv])
            ms, rstd, half = (ph.sb(n, [P, TILES]) for n in ("ms", "rstd", "half"))
            l_in, l_sum, l_exp, ms_ready, norm_own, pool_own, normed = (
                ph.sem(n) for n in ("l_in", "l_sum", "l_exp", "ms_ready", "norm_own", "pool_own", "normed"))

        def scores_of(u):
            first_bank = score_banks(u)[0][0]
            return s_ps[:, first_bank * HALF:first_bank * HALF + (u // maps + 1) * P]

        banks = [s_ps[:, n * HALF:(n + 1) * HALF] for n in range(4)]
        with nc.Block() as block:
            @block.sync
            def _(sp):
                def load_qk(h):
                    sp.dma_start(qs[:, :, :], q(h)).then_inc(qk_in, 16)
                    sp.dma_start(ks[:, :, :], k(h)).then_inc(qk_in, 16)

                def load_v(h, b):
                    sp.dma_start(vs[:, b, :, :], v(h)).then_inc(v_in[b], 16)

                def store(h, b):
                    if diff:
                        sp.wait_ge(normed, h + 1)
                    else:
                        sp.wait_ge(o_done, TILES * h + TILES + 2)
                    settle(sp)
                    sp.dma_start(out(h), o_sb[:, b, :, :]).then_inc(stored[b], 16)

                if diff:
                    for n, part in enumerate(lam_parts):
                        sp.dma_start(lq[:, n, :], part.partition_broadcast(P)).then_inc(l_in, 16)
                    sp.dma_start(gsub[:, :], sub_g.partition_broadcast(P)).then_inc(l_in, 16)
                load_qk(0)
                load_v(0, 0)
                load_v(1, 1)
                if m:
                    m.load_small(nc, sp)
                    m.load(sp, 0)
                sp.wait_ge(tp_ready, 4)
                load_qk(1)

                def turn(h, b):
                    sp.wait_ge(tp_ready, 4 + G * h + QK_LAST)
                    load_qk(h + 2)
                    if m:
                        m.load(sp, h + 1)
                    sp.wait_ge(o_ready, TILES * h + TILES)
                    load_v(h + 2, b)
                    store(h, b)

                with sp.Fori(0, HEADS // 2 - 1) as p:
                    for b in range(2):
                        turn(2 * p + b, b)
                if m:
                    m.load(sp, HEADS - 1)
                store(HEADS - 2, 0)
                store(HEADS - 1, 1)
                for b in range(2):
                    sp.wait_ge(stored[b], 16 * (HEADS // 2 + 1))

            @block.tensor
            def _(pe):
                def transpose_qk(at, parity, n):
                    src = (qs, ks)[n // 2]
                    bank_group(at, parity, [src[:, 4 * (n % 2) + t, :] for t in range(4)])

                def bank_group(at, parity, pieces):
                    pe.wait_ge(tp_copied, at + 1)
                    for n, piece in enumerate(pieces):
                        last = nc.tensor.transpose(tp[0:piece.shape[-1], parity, n, :], piece, K["ident"])
                    last.then_inc(tp_ready, 1)

                def scores(h, b, i):
                    n = (i + 1) * P
                    for mp in range(maps):
                        u = i * maps + mp
                        pe.wait_ge(exp_done, U * h + score_banks(u)[1] + 3)
                        dst = scores_of(u)
                        for c in range(0, n, HALF):
                            w = min(HALF, n - c)
                            last = nc.tensor.matmul(dst[:, c:c + w], qT[mp * dk:(mp + 1) * dk, b, i * P:(i + 1) * P],
                                                    kT[mp * dk:(mp + 1) * dk, b, c:c + w], start=True, stop=True)
                        last.then_inc(s_ready, 1)

                def head(h, b, turn, first, last):
                    g = 0
                    for i in range(TILES):
                        if diff:
                            pe.wait_ge(a_ready, TILES * h + i + 1)
                        else:
                            pe.wait_ge(exp_done, U * h + i + 3)
                        for j in range(0, i + 1, 4):
                            bank_group(4 + G * h + g, g % 2, [prob[:, i % PSLOTS, 0, t * P:(t + 1) * P] for t in range(j, min(j + 4, i + 1))])
                            g += 1
                        mine = g - groups[i]
                        if i in QK_AT and not last:
                            if i == QK_AT[0]:
                                pe.wait_ge(qk_in, 32 * h + 64)
                            transpose_qk(4 + G * h + g, g % 2, i - QK_AT[0])
                            g += 1
                        if i + 2 < TILES:
                            scores(h, b, i + 2)
                        elif not last:
                            if i + 2 == TILES:
                                pe.wait_ge(tp_copied, 4 + G * h + QK_LAST + 2)
                            scores(h + 1, 1 - b, i + 2 - TILES)
                        if i == 0:
                            pe.wait_ge(v_in[b], 16 * turn + 16)
                        pe.wait_ge(o_done, TILES * h + i + 1)
                        for j in range(i + 1):
                            if j % 4 == 0:
                                pe.wait_ge(tp_copied, 4 + G * h + mine + j // 4 + 3)
                            last_mm = nc.tensor.matmul(o_ps[:, i % 2, 0:dv], aT[:, j, :], vs[:, b, j, :],
                                                       start=(j == 0), stop=(j == i))
                        last_mm.then_inc(o_ready, 1)
                    assert last or g == G

                pe.wait_ge(qk_in, 32)
                for n in range(4):
                    transpose_qk(n, n % 2, n)
                pe.wait_ge(tp_copied, 6)
                scores(0, 0, 0)
                scores(0, 0, 1)
                each_head(pe, head)
                if m:
                    pe.wait_ge(exp_done, U * HEADS + 2)
                    m.total(nc, pe, banks)

            @block.scalar
            def _(act):
                if m:
                    m.silu(act)
                for _ in range(2):
                    act.sem_inc(tp_copied, 1)
                    act.sem_inc(exp_done, 1)
                if diff:
                    act.wait_ge(l_sum, 1)
                    act.activation(ls[:, 2:4], ls[:, 0:2], ACT.Exp).then_inc(l_exp, 1)

                def copy_group(at, parity, dst, n, rows_):
                    act.wait_ge(tp_ready, at + 1)
                    act.copy(dst, tp[0:rows_, parity, 0:n, :]).then_inc(tp_copied, 1)

                def copy_qk(at, parity, b, n):
                    dst = (qT, kT)[n // 2][:, b, n % 2 * HALF:(n % 2 + 1) * HALF]
                    copy_group(at, parity, dst.rearrange("p (n c) -> p n c", n=4), 4, dq)

                def exps(h, i):
                    n = (i + 1) * P
                    for mp in range(maps):
                        u = i * maps + mp
                        act.wait_ge(bias_ready, U * h + u + 1)
                        act.activation(prob[:, i % PSLOTS, mp, 0:n], scores_of(u), ACT.Exp, bias=bias[:, u:u + 1],
                                       scale=scale, accum_out=total[:, u:u + 1]).then_inc(exp_done, 1)

                def head(h, b, turn, first, last):
                    g = 0
                    for i in range(TILES):
                        for j in range(0, i + 1, 4):
                            n = min(4, i + 1 - j)
                            copy_group(4 + G * h + g, g % 2, aT[:, j:j + n, :], n, P)
                            g += 1
                        if i in QK_AT and not last:
                            copy_qk(4 + G * h + g, g % 2, 1 - b, i - QK_AT[0])
                            g += 1
                        if i + 2 < TILES:
                            exps(h, i + 2)
                        elif not last:
                            exps(h + 1, i + 2 - TILES)

                for n in range(4):
                    copy_qk(n, n % 2, 0, n)
                exps(0, 0)
                exps(0, 1)
                each_head(act, head)

            @block.vector
            def _(dve):
                dve.sem_inc(o_done, 2)
                for b in range(2):
                    dve.sem_inc(stored[b], 16)
                ch = Chain(dve, own)
                if diff:
                    dve.wait_ge(l_in, 16 * 5)
                    ch(dve.tensor_tensor(lt[:, 0], lq[:, 0], lq[:, 1], ALU.mult))
                    ch(dve.tensor_tensor(lt[:, 1], lq[:, 2], lq[:, 3], ALU.mult))
                    ch(dve.tensor_scalar(gsub[:, :], gsub[:, :], 1.0 - LAMBDA_INIT, None, ALU.mult))
                    ch.wait()
                    dve.reduce_sum(ls[:, 0:2], lt[:, :, :], axis=AX.X).then_inc(l_sum, 1)
                    dve.wait_ge(l_exp, 1)
                    ch(dve.tensor_tensor(lam[:, :], ls[:, 2:3], ls[:, 3:4], ALU.subtract))
                    ch.wait()
                    ch(dve.tensor_scalar(lam[:, :], lam[:, :], LAMBDA_INIT, None, ALU.add))
                    ch.wait()

                def biases(ch, h, i):
                    n = (i + 1) * P
                    for mp in range(maps):
                        u = i * maps + mp
                        s = scores_of(u)
                        dve.wait_ge(s_ready, U * h + u + 1)
                        ch(dve.tensor_tensor(s[:, n - P:n], s[:, n - P:n], mask, ALU.add))
                        ch.wait()
                        ch(dve.reduce_max(mx[:, u:u + 1], s[:, 0:n], axis=AX.X))
                        ch.wait()
                        dve.tensor_scalar(bias[:, u:u + 1], mx[:, u:u + 1], -scale, None, ALU.mult).then_inc(bias_ready, 1)

                def combine(ch, h, i):
                    n = (i + 1) * P
                    u = i * maps
                    dve.wait_ge(exp_done, U * h + u + maps + 2)
                    ch(dve.reciprocal(inv[:, u:u + maps], total[:, u:u + maps]))
                    if diff:
                        p0, p1 = (prob[:, i % PSLOTS, mp, 0:n] for mp in range(2))
                        ch.wait()
                        ch(dve.tensor_tensor(inv[:, u + 1:u + 2], inv[:, u + 1:u + 2], lam[:, :], ALU.mult))
                        ch.wait()
                        ch(dve.tensor_scalar(p1, p1, inv[:, u + 1:u + 2], None, ALU.mult))
                        ch.wait()
                        dve.scalar_tensor_tensor(p0, p0, inv[:, u:u + 1], p1, ALU.mult, ALU.subtract).then_inc(a_ready, 1)

                def evacuate(ch, h, b, turn, i):
                    dve.wait_ge(o_ready, TILES * h + i + 1)
                    if i == 0:
                        dve.wait_ge(stored[b], 16 * turn + 16)
                    if diff:
                        dve.tensor_copy(o_sb[:, b, i, :], o_ps[:, i % 2, 0:dv]).then_inc(o_done, 1)
                    else:
                        ch.wait()
                        dve.tensor_scalar(o_sb[:, b, i, :], o_ps[:, i % 2, 0:dv], inv[:, i:i + 1], None,
                                          ALU.mult).then_inc(o_done, 1)

                def norm(h, b):
                    ch = Chain(dve, norm_own, 2 * h)
                    dve.wait_ge(o_done, TILES * h + TILES + 2)
                    ch(dve.tensor_tensor(sq[:, :, :], o_sb[:, b, :, :], o_sb[:, b, :, :], ALU.mult))
                    ch.wait()
                    if not (isinstance(h, int) and h == 0):
                        dve.wait_ge(normed, h)
                    ch(dve.reduce_sum(ms[:, :], sq[:, :, :], axis=AX.X))
                    ch.wait()
                    dve.tensor_scalar(ms[:, :], ms[:, :], 1.0 / dv, LN_EPS, ALU.mult, ALU.add).then_inc(ms_ready, 1)

                biases(ch, 0, 0)
                biases(ch, 0, 1)
                combine(ch, 0, 0)
                before = ch.n
                per_head = 2 * U + (3 * TILES if diff else TILES)

                def head(h, b, turn, first, last):
                    ch = Chain(dve, own, per_head * h + before)
                    for i in range(TILES):
                        if i + 1 < TILES:
                            combine(ch, h, i + 1)
                        elif not last:
                            combine(ch, h + 1, 0)
                        if i + 2 < TILES:
                            biases(ch, h, i + 2)
                        elif not last:
                            biases(ch, h + 1, i + 2 - TILES)
                        if i > 0:
                            evacuate(ch, h, b, turn, i - 1)
                        elif not first:
                            evacuate(ch, h - 1, 1 - b, None, TILES - 1)
                        if diff and i == NORM_AT and not first:
                            norm(h - 1, 1 - b)
                    assert last or ch.n == per_head
                    if last:
                        evacuate(ch, h, b, turn, TILES - 1)
                        if diff:
                            norm(h, b)

                each_head(dve, head)
                if m:
                    m.put(dve, banks)

            if diff:
                @block.gpsimd
                def _(pool):
                    pool.memset(half[:, :], -0.5).then_inc(pool_own, 1)
                    pool.wait_ge(pool_own, 1)
                    if m:
                        m.clear(pool)

                    def head(h, b, turn, first, last):
                        if m:
                            for l in range(2):
                                m.add(pool, h, l)
                        ch = Chain(pool, pool_own, 2 * h + 1)
                        pool.wait_ge(ms_ready, h + 1)
                        ch(pool.tensor_tensor(rstd[:, :], ms[:, :], half[:, :], ALU.pow))
                        ch.wait()
                        o = o_sb[:, b, :, :]
                        ch(pool.tensor_tensor(o, o, rstd[:, :].unsqueeze(2).to_broadcast([P, TILES, dv]), ALU.mult))
                        ch.wait()
                        pool.tensor_tensor(o, o, gsub[:, :].unsqueeze(1).to_broadcast([P, TILES, dv]), ALU.mult).then_inc(normed, 1)

                    each_head(pool, head)


def with_constants(nc, stack, consts, body):
    parts = constant_parts()
    width = sum(a.shape[1] for a in parts.values())
    held = stack.enter_context(nc.sbuf_tensor("constants", [P, width], F32))
    K, at = {}, 0
    for name, a in parts.items():
        K[name] = held[:, at:at + a.shape[1]]
        at += a.shape[1]
    SETTLED.append(nc.alloc_semaphore("settled"))
    with Phase(nc, "load") as ph:
        loaded = ph.sem("loaded")
        with nc.Block() as block:
            @block.sync
            def _(sp):
                sp.dma_start(held[:, :], consts).then_inc(loaded, 16)
                sp.wait_ge(loaded, 16)
    body(K)


def diff_attention(nc, K, qkv, lam_parts, sub_g, mix, modulation=None):
    def heads(base, width, ap=None):
        return lambda h: (ap if ap is not None else qkv)[:, bass.ds(h * width + base, width)].rearrange("(t p) c -> p t c", p=P)

    phase_attention(nc, K, "diff", heads(0, VD), heads(D, VD), heads(2 * D, VD), heads(0, VD, mix), 2, HD, VD,
                    K["causal"], HD ** -0.5, lam_parts, sub_g, modulation)


def affine(dve, ch, r, mv, gb, rstd, rstd_ready, i, out, h_ready):
    ch(dve.scalar_tensor_tensor(out[:, :], r[:, :], mv[:, 0:1], gb[:, 0, :], ALU.subtract, ALU.mult))
    ch.wait()
    dve.wait_ge(rstd_ready, i + 2)
    dve.scalar_tensor_tensor(out[:, :], out[:, :], rstd[:, 0:1], gb[:, 1, :], ALU.mult, ALU.add).then_inc(h_ready, 1)


def layer_norm_steps(dve, ch, r, stats, mv, ms_ready):
    for c in range(2):
        ch(dve.bn_stats(stats[:, c, :], r[:, c * HALF:(c + 1) * HALF]))
    ch.wait()
    settle(dve)
    ch(dve.bn_aggr(mv[:, :], stats[:, :, :]))
    ch.wait()
    dve.tensor_scalar(mv[:, 1:2], mv[:, 1:2], LN_EPS, None, ALU.add).then_inc(ms_ready, 1)


def phase_out_norm(nc, K, name, mix, w_out, h_in, g, b, w_gr, b_gr, w_er, b_er, h_out, logits, weights=None):
    NL = GROUPS + EXPERTS
    with Phase(nc, name) as ph:
        w = ph.sb("w", [P, KC, D])
        wr = ph.sb("wr", [P, KC, NL])
        br = ph.sb("br", [P, NL])
        gb = ph.sb("gb", [P, 2, D])
        xin, res, r, hn = (ph.sb(n, [P, D]) for n in ("x", "res", "r", "hn"))
        xT, hT = ph.sb("xT", [P, KC, P]), ph.sb("hT", [P, KC, P])
        stats, mv = ph.sb("stats", [P, 2, 6]), ph.sb("mv", [P, 2])
        rstd, half = ph.sb("rstd", [P, 1]), ph.sb("half", [P, 1])
        tp = ph.ps("tp", [P, 2, 4, P])
        acc = ph.ps("acc", [P, 2, HALF])
        lg = ph.ps("lg", [P, 1, HALF])
        w_in = [ph.sem(f"w_in{c}") for c in range(2)]
        small_in, x_in, res_in, tp_ready, tp_copied, acc_ready, r_ready = (ph.sem(n) for n in (
            "small_in", "x_in", "res_in", "tp_ready", "tp_copied", "acc_ready", "r_ready"))
        ms_ready, rstd_ready, h_ready, lg_ready, lg_done, stored, own = (ph.sem(n) for n in (
            "ms_ready", "rstd_ready", "h_ready", "lg_ready", "lg_done", "stored", "own"))

        with nc.Block() as block:
            @block.sync
            def _(sp):
                sp.dma_start(xin[:, :], mix[0:P, :]).then_inc(x_in, 16)
                for c in range(2):
                    load_columns(sp, w, w_out, c, HALF, w_in[c])
                sp.dma_start(res[:, :], h_in[0:P, :]).then_inc(res_in, 16)
                for n, row in enumerate((g, b)):
                    sp.dma_start(gb[:, n, :], row.partition_broadcast(P)).then_inc(small_in, 16)
                sp.dma_start(wr[:, :, 0:GROUPS], w_gr.rearrange("(k p) n -> p k n", p=P)).then_inc(small_in, 16)
                sp.dma_start(wr[:, :, GROUPS:NL], w_er.rearrange("(k p) n -> p k n", p=P)).then_inc(small_in, 16)
                sp.dma_start(br[:, 0:GROUPS], b_gr.partition_broadcast(P)).then_inc(small_in, 16)
                sp.dma_start(br[:, GROUPS:NL], b_er.partition_broadcast(P)).then_inc(small_in, 16)

                def turn(i, transposed):
                    sp.wait_ge(tp_ready, transposed)
                    sp.dma_start(xin[:, :], rows(mix, i + 1)).then_inc(x_in, 16)
                    sp.wait_ge(r_ready, 2 * i + 4)
                    sp.dma_start(res[:, :], rows(h_in, i + 1)).then_inc(res_in, 16)
                    sp.wait_ge(h_ready, i + 1)
                    sp.dma_start(rows(h_out, i), hn[:, :]).then_inc(stored, 16)

                turn(0, 2)
                for part in range(3):
                    with sp.Fori(1 + 2 * part, 3 + 2 * part) as i:
                        turn(i, 4 * i)
                    if weights is not None:
                        weights.load_first(sp, part)
                sp.wait_ge(h_ready, TILES)
                sp.dma_start(rows(h_out, TILES - 1), hn[:, :]).then_inc(stored, 16)
                sp.wait_ge(stored, 16 * (TILES + 1))

            @block.tensor
            def _(pe):
                def transposes(src, n):
                    for bnk in range(2):
                        pe.wait_ge(tp_copied, 2 * n + bnk + 1)
                        for k in range(4):
                            last = nc.tensor.transpose(tp[:, bnk, k, :], src[:, (4 * bnk + k) * P:(4 * bnk + k + 1) * P], K["ident"])
                        last.then_inc(tp_ready, 1)

                def product(i, c):
                    pe.wait_ge(w_in[c], 16)
                    pe.wait_ge(r_ready, 2 * i + c + 1)
                    for k in range(KC):
                        last = nc.tensor.matmul(acc[:, c, :], xT[:, k, :], w[:, k, c * HALF:(c + 1) * HALF],
                                                start=(k == 0), stop=(k == KC - 1))
                    last.then_inc(acc_ready, 1)

                def route(i, copied):
                    pe.wait_ge(tp_copied, copied)
                    pe.wait_ge(lg_done, i + 1)
                    for k in range(KC):
                        last = nc.tensor.matmul(lg[:, 0, 0:NL], hT[:, k, :], wr[:, k, :], start=(k == 0), stop=(k == KC - 1))
                    last.then_inc(lg_ready, 1)

                def tile(i, last=False):
                    pe.wait_ge(tp_copied, 4 * i + 2)
                    product(i, 0)
                    pe.wait_ge(h_ready, i)
                    transposes(hn, 2 * i)
                    product(i, 1)
                    if not last:
                        pe.wait_ge(x_in, 16 * i + 32)
                        transposes(xin, 2 * i + 1)
                    route(i - 1, 4 * i + 4)

                pe.wait_ge(x_in, 16)
                transposes(xin, 0)
                pe.wait_ge(tp_copied, 4)
                product(0, 0)
                product(0, 1)
                pe.wait_ge(x_in, 32)
                transposes(xin, 1)
                pe.wait_ge(small_in, 16 * 6)
                with pe.Fori(1, TILES - 1) as i:
                    tile(i)
                tile(TILES - 1, last=True)
                pe.wait_ge(h_ready, TILES)
                transposes(hn, 2 * TILES - 1)
                route(TILES - 1, 4 * TILES + 2)

            @block.scalar
            def _(act):
                act.sem_inc(tp_copied, 1)
                act.sem_inc(tp_copied, 1)

                def copies(dst, n):
                    for bnk in range(2):
                        act.wait_ge(tp_ready, 2 * n + bnk + 1)
                        act.copy(dst[:, 4 * bnk:4 * bnk + 4, :], tp[:, bnk, :, :]).then_inc(tp_copied, 1)

                copies(xT, 0)
                copies(xT, 1)
                with act.Fori(1, TILES - 1) as i:
                    copies(hT, 2 * i)
                    copies(xT, 2 * i + 1)
                copies(hT, 2 * TILES - 2)
                copies(hT, 2 * TILES - 1)

            @block.vector
            def _(dve):
                dve.sem_inc(r_ready, 1)
                dve.sem_inc(r_ready, 1)
                dve.sem_inc(lg_done, 1)
                dve.sem_inc(stored, 16)

                def norm(i, ch):
                    dve.wait_ge(res_in, 16 * i + 16)
                    for c in range(2):
                        s = slice(c * HALF, (c + 1) * HALF)
                        dve.wait_ge(acc_ready, 2 * i + c + 1)
                        dve.scalar_tensor_tensor(r[:, s], res[:, s], ALPHA, acc[:, c, :], ALU.mult, ALU.add).then_inc(r_ready, 1)
                    dve.wait_ge(r_ready, 2 * i + 4)
                    layer_norm_steps(dve, ch, r, stats, mv, ms_ready)
                    dve.wait_ge(stored, 16 * i + 16)
                    if not isinstance(i, int):
                        dve.wait_ge(tp_ready, 4 * i + 2)
                    affine(dve, ch, r, mv, gb, rstd, rstd_ready, i, hn, h_ready)

                def put_logits(i):
                    dve.wait_ge(lg_ready, i + 1)
                    dve.tensor_tensor(logits[:, bass.ds(i, 1), :], lg[:, 0:1, 0:NL], br[:, :].unsqueeze(1), ALU.add).then_inc(lg_done, 1)

                dve.wait_ge(small_in, 16 * 6)
                norm(0, Chain(dve, own))
                with dve.Fori(1, TILES) as i:
                    norm(i, Chain(dve, own, 4 * i))
                    put_logits(i - 1)
                put_logits(TILES - 1)

            @block.gpsimd
            def _(pool):
                pool.memset(half[:, :], -0.5).then_inc(rstd_ready, 1)
                pool.wait_ge(rstd_ready, 1)
                with pool.Fori(0, TILES) as i:
                    pool.wait_ge(ms_ready, i + 1)
                    pool.tensor_tensor(rstd[:, :], mv[:, 1:2], half[:, :], ALU.pow).then_inc(rstd_ready, 1)


def phase_route(nc, K, name, logits, gates, dest_i, tok_i, blk_i, pairs_i):
    T = TILES
    NL = GROUPS + EXPERTS
    with Phase(nc, name) as ph:
        def t3(n, w=EXPERTS):
            return ph.sb(n, [P, T, w])

        def t2(n, w=T):
            return ph.sb(n, [P, w])

        gmax, gsum, v1, v2, ex, w1, w2, ones_c = (t2(n) for n in ("gmax", "gsum", "v1", "v2", "ex", "w1", "w2", "pr"))
        ge, G4, rank4 = t3("ge", GROUPS), t3("G4", GROUPS), t3("rank4", GROUPS)
        em, em2, M1, M2, M, S, R, Q, q1, Dst, tmp = (t3(n) for n in (
            "em", "em2", "M1", "M2", "M", "S", "R", "Q", "q1", "Dst", "tmp"))
        S8 = t2("S8", EXPERTS)
        ones = ph.sb("ones", [P, P])
        cnt, nov, cum, ob, obe, zero = (t2(n, EXPERTS) for n in ("cnt", "nov", "cum", "ob", "obe", "zero"))
        d1, d2, s1, s2, b1, b2 = (t2(n) for n in ("d1", "d2", "s1", "s2", "b1", "b2"))
        A = ph.sb("A", [P, T, 2, P])
        B = ph.sb("B", [P, T, 2, BCOLS])
        over = ph.sb("over", [P, OVER + 2, EXPERTS])
        over2 = ph.sb("over2", [P, OVER + 2, EXPERTS])
        bexp = ph.sb("bexp", [P, BCOLS])
        tot = ph.sb("tot", [P, 2])
        sevens = ph.sb("sevens", [P, 8])
        pr = ph.ps("pr_ps", [P, T, EXPERTS])
        pc = ph.ps("pc", [P, EXPERTS])
        pt = ph.ps("pt", [P, BCOLS])
        own, m_ready, ranked, exp_in, exp_out, ab_ready, tok_ready = (ph.sem(n) for n in (
            "own", "m_ready", "ranked", "exp_in", "exp_out", "ab_ready", "tok_ready"))
        with nc.Block() as block:
            @block.scalar
            def _(act):
                act.wait_ge(exp_in, 1)
                act.activation(ge[:, :, :], ge[:, :, :], ACT.Exp).then_inc(exp_out, 1)
                act.wait_ge(exp_in, 2)
                act.activation(ex[:, :], ex[:, :], ACT.Exp).then_inc(exp_out, 1)

            @block.tensor
            def _(pe):
                pe.wait_ge(m_ready, 1)
                nc.tensor.matmul(pr[:, :, :], K["before"], M[:, :, :], start=True, stop=False)
                nc.tensor.matmul(pr[:, :, :], ones[:, :], S[:, :, :], start=False, stop=True)
                nc.tensor.matmul(pc[:, :], ones[:, :], S8[:, :], start=True, stop=True).then_inc(ranked, 1)
                pe.wait_ge(ab_ready, 1)
                for t in range(T):
                    for c in range(2):
                        last = nc.tensor.matmul(pt[:, :], A[:, t, c, :], B[:, t, c, :], start=(t + c == 0),
                                                stop=(t == T - 1 and c == 1))
                last.then_inc(tok_ready, 1)

            @block.vector
            def _(dve):
                ch = Chain(dve, own)

                def step(ins):
                    ch(ins)
                    ch.wait()

                def tt(o, a, b, op):
                    step(dve.tensor_tensor(o, a, b, op))

                def ts(o, a, x, op, y=None, op2=None):
                    step(dve.tensor_scalar(o, a, x, y, op, *([op2] if op2 is not None else [])))

                def wide(a, w):
                    return a.unsqueeze(2).to_broadcast([P, T, w])

                def first_max(out, src, top, w, work, rev):
                    tt(work, src, wide(top, w), ALU.is_equal)
                    tt(work, work, rev, ALU.mult)
                    step(dve.reduce_max(w1[:, :], work, axis=AX.X))
                    tt(out, work, wide(w1[:, :], w), ALU.is_equal)

                step(dve.memset(ones[:, :], 1.0))
                step(dve.memset(zero[:, :], 0.0))
                rev = tmp[:, :, :]
                revs = ph.sb("revs", [P, EXPERTS])
                ts(revs[:, :], K["iota"][:, 0:EXPERTS], -1.0, ALU.mult, float(EXPERTS), ALU.add)
                revx = revs[:, :].unsqueeze(1).to_broadcast([P, T, EXPERTS])
                revg = revs[:, 0:GROUPS].unsqueeze(1).to_broadcast([P, T, GROUPS])
                gl, el = logits[:, :, 0:GROUPS], logits[:, :, GROUPS:NL]
                step(dve.reduce_max(gmax[:, :], gl, axis=AX.X))
                first_max(G4[:, :, :], gl, gmax[:, :], GROUPS, rank4[:, :, :], revg)
                dve.tensor_tensor(ge[:, :, :], gl, wide(gmax[:, :], GROUPS), ALU.subtract).then_inc(exp_in, 1)
                gx = G4[:, :, :].unsqueeze(3).to_broadcast([P, T, GROUPS, PER_GROUP])
                e4 = em[:, :, :].rearrange("p t (g e) -> p t g e", g=GROUPS)
                q4 = q1[:, :, :].rearrange("p t (g e) -> p t g e", g=GROUPS)
                for t in range(T):
                    step(dve.tensor_copy(q4[:, t], gx[:, t]))
                tt(em[:, :, :], el, q1[:, :, :], ALU.mult)
                ts(q1[:, :, :], q1[:, :, :], -NEG, ALU.mult, NEG, ALU.add)
                tt(em[:, :, :], em[:, :, :], q1[:, :, :], ALU.add)
                step(dve.reduce_max(v1[:, :], em[:, :, :], axis=AX.X))
                first_max(M1[:, :, :], em[:, :, :], v1[:, :], EXPERTS, tmp[:, :, :], revx)
                step(dve.scalar_tensor_tensor(em2[:, :, :], M1[:, :, :], 3 * NEG, em[:, :, :], ALU.mult, ALU.add))
                step(dve.reduce_max(v2[:, :], em2[:, :, :], axis=AX.X))
                first_max(M2[:, :, :], em2[:, :, :], v2[:, :], EXPERTS, tmp[:, :, :], revx)
                dve.tensor_tensor(ex[:, :], v2[:, :], v1[:, :], ALU.subtract).then_inc(exp_in, 1)
                tt(M[:, :, :], M1[:, :, :], M2[:, :, :], ALU.add)
                step(dve.tensor_copy(S[:, 0, :], zero[:, :]))
                for t in range(1, T):
                    tt(S[:, t, :], S[:, t - 1, :], M[:, t - 1, :], ALU.add)
                dve.tensor_tensor(S8[:, :], S[:, T - 1, :], M[:, T - 1, :], ALU.add).then_inc(m_ready, 1)
                dve.wait_ge(exp_out, 2)
                step(dve.reduce_sum(gsum[:, :], ge[:, :, :], axis=AX.X))
                ts(w1[:, :], ex[:, :], 1.0, ALU.add)
                tt(w1[:, :], w1[:, :], gsum[:, :], ALU.mult)
                step(dve.reciprocal(gates[:, 0, :], w1[:, :]))
                tt(gates[:, 1, :], gates[:, 0, :], ex[:, :], ALU.mult)
                dve.wait_ge(ranked, 1)
                step(dve.tensor_copy(R[:, :, :], pr[:, :, :]))
                step(dve.tensor_copy(cnt[:, :], pc[:, :]))
                ts(Q[:, :, :], R[:, :, :], float(P), ALU.is_ge)
                ts(nov[:, :], cnt[:, :], float(P), ALU.is_gt)
                for m in range(2, T):
                    step(dve.scalar_tensor_tensor(Q[:, :, :], R[:, :, :], float(m * P), Q[:, :, :], ALU.is_ge, ALU.add))
                    step(dve.scalar_tensor_tensor(nov[:, :], cnt[:, :], float(m * P), nov[:, :], ALU.is_gt, ALU.add))
                step(dve.tensor_tensor_scan(cum[:, :], nov[:, :], zero[:, :], 0.0, ALU.add, ALU.add))
                tt(ob[:, :], cum[:, :], nov[:, :], ALU.subtract)
                step(dve.tensor_copy(tot[:, 0:1], cum[:, EXPERTS - 1:EXPERTS]))
                ts(obe[:, :], ob[:, :], float(EXPERTS - 1), ALU.add)
                tt(obe[:, :], obe[:, :], K["iota"][:, 0:EXPERTS], ALU.subtract)
                ts(q1[:, :, :], Q[:, :, :], 1.0, ALU.min)
                tt(tmp[:, :, :], q1[:, :, :], obe[:, :].unsqueeze(1).to_broadcast([P, T, EXPERTS]), ALU.mult)
                tt(tmp[:, :, :], tmp[:, :, :], Q[:, :, :], ALU.add)
                tt(tmp[:, :, :], tmp[:, :, :], K["iota"][:, 0:EXPERTS].unsqueeze(1).to_broadcast([P, T, EXPERTS]), ALU.add)
                step(dve.scalar_tensor_tensor(R[:, :, :], Q[:, :, :], -float(P), R[:, :, :], ALU.mult, ALU.add))
                for Mk, s, b in ((M1, s1, b1), (M2, s2, b2)):
                    tt(S[:, :, :], Mk[:, :, :], R[:, :, :], ALU.mult)
                    step(dve.reduce_sum(s[:, :], S[:, :, :], axis=AX.X))
                    tt(S[:, :, :], Mk[:, :, :], tmp[:, :, :], ALU.mult)
                    step(dve.reduce_sum(b[:, :], S[:, :, :], axis=AX.X))
                for n, (s, b, d) in enumerate(((s1, b1, d1), (s2, b2, d2))):
                    step(dve.scalar_tensor_tensor(d[:, :], b[:, :], float(P), s[:, :], ALU.mult, ALU.add))
                    step(dve.tensor_copy(dest_i[:, n, :], d[:, :]))
                for t in range(T):
                    for c, (s, b) in enumerate(((s1, b1), (s2, b2))):
                        ch(dve.tensor_scalar(A[:, t, c, :], K["iota"], s[:, t:t + 1], None, ALU.is_equal))
                        ch(dve.tensor_scalar(B[:, t, c, :], K["iota"][:, 0:BCOLS], b[:, t:t + 1], K["token"][:, t:t + 1],
                                             ALU.is_equal, ALU.mult))
                ch.wait()
                step(dve.tensor_copy(sevens[:, :], K["iota"][:, 0:8]))
                dve.sem_inc(ab_ready, 1)
                bi = K["iota"][:, 0:OVER + 2].unsqueeze(2).to_broadcast([P, OVER + 2, EXPERTS])

                def over_b(a):
                    return a.unsqueeze(1).to_broadcast([P, OVER + 2, EXPERTS])

                tt(over[:, :, :], bi, over_b(ob[:, :]), ALU.is_ge)
                tt(over2[:, :, :], bi, over_b(cum[:, :]), ALU.is_lt)
                tt(over[:, :, :], over[:, :, :], over2[:, :, :], ALU.mult)
                tt(over[:, :, :], over[:, :, :], over_b(K["iota"][:, 0:EXPERTS]), ALU.mult)
                step(dve.reduce_sum(bexp[:, EXPERTS:BCOLS], over[:, :, :], axis=AX.X))
                step(dve.tensor_copy(bexp[:, 0:EXPERTS], K["iota"][:, 0:EXPERTS]))
                step(dve.tensor_copy(blk_i[:, :], bexp[:, :]))
                ts(sevens[:, :], sevens[:, :], 2.0, ALU.mult)
                ts(sevens[:, :], sevens[:, :], tot[:, 0:1], ALU.is_lt)
                step(dve.reduce_sum(tot[:, 1:2], sevens[:, :], axis=AX.X))
                ts(tot[:, 1:2], tot[:, 1:2], float(EXPERTS // 2), ALU.add)
                step(dve.tensor_copy(pairs_i[:, :], tot[:, 1:2]))
                dve.wait_ge(tok_ready, 1)
                step(dve.tensor_copy(tok_i[:, :], pt[:, :]))


class ExpertWeights(Phase):

    def __init__(self, nc, name, w_gate, w_up, w_down):
        super().__init__(nc, name)
        self.sources = (w_gate, w_up), w_down

    def __enter__(self):
        super().__enter__()
        self.wg, self.wu = self.sb("wg", [P, 2, KC, DE]), self.sb("wu", [P, 2, KC, DE])
        self.wd = self.sb("wd", [P, 2, DE // P, D])
        self.gu_in, self.d_in = ([self.sem(f"{n}{u}") for u in range(2)] for n in ("gu_in", "d_in"))
        return self

    def load_gate_up(self, sp, e, u):
        for src, dst in zip(self.sources[0], (self.wg, self.wu)):
            sp.dma_start(dst[:, u, :, :], src[bass.ds(e, 1), :, :].rearrange("o (k p) n -> p (o k) n", p=P)).then_inc(self.gu_in[u], 16)

    def load_down(self, sp, e, u):
        sp.dma_start(self.wd[:, u, :, :], self.sources[1][bass.ds(e, 1), :, :].rearrange("o (k p) n -> p (o k) n", p=P)).then_inc(self.d_in[u], 16)

    def load_first(self, sp, part):
        if part < 2:
            self.load_gate_up(sp, part, part)
        else:
            for u in range(2):
                self.load_down(sp, u, u)


def phase_experts(nc, K, name, h, weights, tok_i, blk_i, pairs_i, y):
    FC = DE // P
    with Phase(nc, name) as ph:
        wg, wu, wd, gu_in, d_in = weights.wg, weights.wu, weights.wd, weights.gu_in, weights.d_in
        idx = ph.sb("idx", [P, 2, 1], I32)
        xg = ph.sb("xg", [P, 2, D])
        xT = ph.sb("xT", [P, KC, P])
        sg, hh = ph.sb("sg", [P, DE]), ph.sb("hh", [P, DE])
        hT = ph.sb("hT", [P, FC, P])
        ysb = ph.sb("y", [P, 2, D])
        tp = ph.ps("tp", [P, 2, 4, P])
        gp, up = ph.ps("gp", [P, HALF]), ph.ps("up", [P, HALF])
        hp = ph.ps("hp", [P, FC, P])
        yp = ph.ps("yp", [P, 2, HALF])
        x_in, idx_ready, tp_ready, xT_ready, g_ready, gu_ready, silu_done, h_ready, hp_ready, hT_ready = (
            ph.sem(n) for n in ("x_in", "idx_ready", "tp_ready", "xT_ready", "g_ready", "gu_ready", "silu_done",
                                "h_ready", "hp_ready", "hT_ready"))
        y_ready, y_done = ph.sem("y_ready"), ph.sem("y_done")
        stored = [ph.sem(f"stored{u}") for u in range(2)]

        def pairs(eng):
            return eng.value_load(pairs_i[0:1, 0:1], min_val=EXPERTS // 2, max_val=BLOCKS // 2)

        with nc.Block() as block:
            @block.sync
            def _(sp):
                n = pairs(sp)
                with sp.Fori(1, n) as p:
                    for u in range(2):
                        b = 2 * p + u
                        e = sp.value_load(blk_i[0:1, bass.ds(b, 1)], min_val=0, max_val=EXPERTS - 1)
                        sp.wait_ge(gu_ready, b + 1)
                        weights.load_gate_up(sp, e, u)
                        sp.wait_ge(y_ready, 2 * b + 2)
                        weights.load_down(sp, e, u)

            @block.gpsimd
            def _(pool):
                n = pairs(pool)

                def gather(b, u):
                    pool.tensor_copy(idx[:, u, :], tok_i[:, bass.ds(b, 1)] if not isinstance(b, int) else tok_i[:, b:b + 1]).then_inc(idx_ready, 1)
                    pool.wait_ge(idx_ready, b + 1)
                    settle(pool)
                    pool.indirect_dma_start(out=xg[:, u, :], out_offset=None, in_=h,
                                            in_offset=bass.IndirectOffsetOnAxis(ap=idx[:, u, :], axis=0)).then_inc(x_in, 16)

                gather(0, 0)
                with pool.Fori(0, n) as p:
                    for u in range(2):
                        b = 2 * p + u
                        pool.wait_ge(tp_ready, 2 * b + 2)
                        gather(b + 1, 1 - u)
                pool.wait_ge(x_in, n * 32 + 16)
                settle(pool)

            @block.tensor
            def _(pe):
                n = pairs(pe)

                def transposes(b, u):
                    pe.wait_ge(x_in, 16 * b + 16)
                    for bnk in range(2):
                        for k in range(4):
                            last = nc.tensor.transpose(tp[:, bnk, k, :], xg[:, u, (4 * bnk + k) * P:(4 * bnk + k + 1) * P], K["ident"])
                        last.then_inc(tp_ready, 1)

                for _ in range(2):
                    pe.sem_inc(gu_ready, 1)
                    pe.sem_inc(y_ready, 2)
                transposes(0, 0)
                with pe.Fori(0, n) as p:
                    for u in range(2):
                        b = 2 * p + u
                        pe.wait_ge(gu_in[u], 32 * p + 32)
                        pe.wait_ge(xT_ready, 2 * b + 2)
                        pe.wait_ge(h_ready, b + 1)
                        for k in range(KC):
                            last = nc.tensor.matmul(gp[:, :], xT[:, k, :], wg[:, u, k, :], start=(k == 0), stop=(k == KC - 1))
                        last.then_inc(g_ready, 1)
                        for k in range(KC):
                            last = nc.tensor.matmul(up[:, :], xT[:, k, :], wu[:, u, k, :], start=(k == 0), stop=(k == KC - 1))
                        last.then_inc(gu_ready, 1)
                        transposes(b + 1, 1 - u)
                        pe.wait_ge(h_ready, b + 2)
                        for k in range(FC):
                            last = nc.tensor.transpose(hp[:, k, :], hh[:, k * P:(k + 1) * P], K["ident"])
                        last.then_inc(hp_ready, 1)
                        pe.wait_ge(d_in[u], 16 * p + 16)
                        pe.wait_ge(hT_ready, b + 1)
                        for c in range(2):
                            pe.wait_ge(y_done, 2 * b + c + 1)
                            for k in range(FC):
                                last = nc.tensor.matmul(yp[:, c, :], hT[:, k, :], wd[:, u, k, c * HALF:(c + 1) * HALF],
                                                        start=(k == 0), stop=(k == FC - 1))
                            last.then_inc(y_ready, 1)

            @block.scalar
            def _(act):
                n = pairs(act)
                for u in range(2):
                    act.sem_inc(stored[u], 16)

                def copies(b):
                    for bnk in range(2):
                        act.wait_ge(tp_ready, 2 * b + bnk + 1)
                        act.copy(xT[:, 4 * bnk:4 * bnk + 4, :], tp[:, bnk, :, :]).then_inc(xT_ready, 1)

                copies(0)
                with act.Fori(0, n) as p:
                    for u in range(2):
                        b = 2 * p + u
                        act.wait_ge(g_ready, b + 1)
                        act.wait_ge(h_ready, b + 1)
                        act.activation(sg[:, :], gp[:, :], ACT.Silu).then_inc(silu_done, 1)
                        copies(b + 1)
                        act.wait_ge(y_done, 2 * b + 4)
                        act.dma_start(y[bass.ds(b * P, P), :], ysb[:, u, :]).then_inc(stored[u], 16)
                for u in range(2):
                    act.wait_ge(stored[u], n * 16 + 16)
                    settle(act)

            @block.vector
            def _(dve):
                n = pairs(dve)
                dve.sem_inc(h_ready, 1)
                dve.sem_inc(y_done, 2)
                with dve.Fori(0, n) as p:
                    for u in range(2):
                        b = 2 * p + u
                        dve.wait_ge(silu_done, b + 1)
                        dve.wait_ge(gu_ready, b + 3)
                        dve.tensor_tensor(hh[:, :], sg[:, :], up[:, :], ALU.mult).then_inc(h_ready, 1)
                        dve.wait_ge(hp_ready, b + 1)
                        dve.tensor_copy(hT[:, :, :], hp[:, :, :]).then_inc(hT_ready, 1)
                        dve.wait_ge(stored[u], 16 * p + 16)
                        for c in range(2):
                            dve.wait_ge(y_ready, 2 * b + c + 5)
                            dve.tensor_copy(ysb[:, u, c * HALF:(c + 1) * HALF], yp[:, c, :]).then_inc(y_done, 1)


def phase_combine(nc, K, name, h, y, gates, dest_i, g, b, out):
    with Phase(nc, name) as ph:
        gb = ph.sb("gb", [P, 2, D])
        idx = ph.sb("idx", [P, 2, 2, 1], I32)
        hin, r, hn = ph.sb("h", [P, 2, D]), ph.sb("r", [P, 2, D]), ph.sb("hn", [P, 2, D])
        yin = ph.sb("y", [P, 2, 2, D])
        stats, mv = ph.sb("stats", [P, 2, 2, 6]), ph.sb("mv", [P, 2, 2])
        rstd, half = ph.sb("rstd", [P, 2, 1]), ph.sb("half", [P, 1])
        small_in, idx_ready, scaled, used, ms_ready, rstd_ready, h_ready, own = (
            ph.sem(n) for n in ("small_in", "idx_ready", "scaled", "used", "ms_ready", "rstd_ready", "h_ready", "own"))
        h_in, y_in, stored = ([ph.sem(f"{n}{u}") for u in range(2)] for n in ("h_in", "y_in", "stored"))
        PAIRS = TILES // 2

        with nc.Block() as block:
            @block.sync
            def _(sp):
                def load(i, u):
                    sp.dma_start(hin[:, u, :], rows(h, i)).then_inc(h_in[u], 16)

                def store(i, u):
                    sp.wait_ge(h_ready, i + 3)
                    sp.dma_start(rows(out, i), hn[:, u, :]).then_inc(stored[u], 16)

                load(0, 0)
                load(1, 1)
                for n, row in enumerate((g, b)):
                    sp.dma_start(gb[:, n, :], row.partition_broadcast(P)).then_inc(small_in, 16)
                with sp.Fori(0, PAIRS - 1) as p:
                    for u in range(2):
                        i = 2 * p + u
                        sp.wait_ge(scaled, i + 1)
                        load(i + 2, u)
                        store(i, u)
                for u in range(2):
                    store(TILES - 2 + u, u)
                for u in range(2):
                    sp.wait_ge(stored[u], 16 * (PAIRS + 1))

            @block.gpsimd
            def _(pool):
                pool.memset(half[:, :], -0.5).then_inc(rstd_ready, 1)
                pool.wait_ge(rstd_ready, 1)

                def gather(i, u):
                    col = slice(i, i + 1) if isinstance(i, int) else bass.ds(i, 1)
                    pool.tensor_copy(idx[:, u, :, :], dest_i[:, :, col]).then_inc(idx_ready, 1)
                    pool.wait_ge(idx_ready, i + 1)
                    settle(pool)
                    for c in range(2):
                        pool.indirect_dma_start(out=yin[:, u, c, :], out_offset=None, in_=y,
                                                in_offset=bass.IndirectOffsetOnAxis(ap=idx[:, u, c, :], axis=0)).then_inc(y_in[u], 16)

                def power(i, u):
                    pool.wait_ge(ms_ready, i + 1)
                    pool.tensor_tensor(rstd[:, u, :], mv[:, u, 1:2], half[:, :], ALU.pow).then_inc(rstd_ready, 1)

                gather(0, 0)
                gather(1, 1)
                with pool.Fori(0, PAIRS - 1) as p:
                    for u in range(2):
                        i = 2 * p + u
                        power(i, u)
                        pool.wait_ge(used, i + 1)
                        gather(i + 2, u)
                for u in range(2):
                    power(TILES - 2 + u, u)

            @block.scalar
            def _(act):
                with act.Fori(0, PAIRS) as p:
                    for u in range(2):
                        i = 2 * p + u
                        act.wait_ge(h_in[u], 16 * p + 16)
                        act.wait_ge(h_ready, i + 1)
                        act.activation(r[:, u, :], hin[:, u, :], ACT.Copy, scale=ALPHA).then_inc(scaled, 1)

            @block.vector
            def _(dve):
                dve.wait_ge(small_in, 32)
                dve.sem_inc(h_ready, 2)
                for u in range(2):
                    dve.sem_inc(stored[u], 16)
                with dve.Fori(0, PAIRS) as p:
                    for u in range(2):
                        i = 2 * p + u
                        ch = Chain(dve, own, 5 * i)
                        dve.wait_ge(scaled, i + 1)
                        dve.wait_ge(y_in[u], 32 * p + 32)
                        ch(dve.scalar_tensor_tensor(r[:, u, :], yin[:, u, 0, :], gates[:, 0, bass.ds(i, 1)], r[:, u, :], ALU.mult, ALU.add))
                        ch.wait()
                        dve.scalar_tensor_tensor(r[:, u, :], yin[:, u, 1, :], gates[:, 1, bass.ds(i, 1)], r[:, u, :],
                                                 ALU.mult, ALU.add).then_inc(used, 1)
                        dve.wait_ge(used, i + 1)
                        layer_norm_steps(dve, ch, r[:, u], stats[:, u], mv[:, u], ms_ready)
                        dve.wait_ge(stored[u], 16 * p + 16)
                        affine(dve, ch, r[:, u], mv[:, u], gb, rstd[:, u], rstd_ready, i, hn[:, u], h_ready)


def phase_pool(nc, K, h, w_in, w_grp, ls, counts, mix):
    PADW = 16
    NG = len(POOL_WINDOWS)
    CG = PG // P
    with Phase(nc, "pool") as ph:
        w = ph.sb("w", [P, KC, D])
        wg = ph.sb("wg", [P, NG, CG, PG])
        lsb = ph.sb("ls", [P, D])
        xin = ph.sb("x", [P, D])
        hT = ph.sb("hT", [P, KC, SEQ])
        u = ph.sb("u", [P, PADW + SEQ])
        s = ph.sb("s", [P, 2, PADW + SEQ])
        inv_count = ph.sb("inv_count", [P, NG, SEQ])
        pT = ph.sb("pT", [P, CG, SEQ])
        ysb = ph.sb("y", [P, TILES, PG])
        tp = ph.ps("tp", [P, 2, 4, P])
        up = ph.ps("up", [P, 2, HALF])
        yp = ph.ps("yp", [P, 2, HALF])
        w_in_s, small_in, x_in, tp_ready, tp_copied, u_ready, u_copied, p_ready, y_ready, y_done, stored, own, padded = (
            ph.sem(n) for n in ("w_in", "small_in", "x_in", "tp_ready", "tp_copied", "u_ready", "u_copied", "p_ready",
                                "y_ready", "y_done", "stored", "own", "padded"))
        with nc.Block() as block:
            @block.sync
            def _(sp):
                sp.dma_start(xin[:, :], h[0:P, :]).then_inc(x_in, 16)
                for k in range(KC):
                    sp.dma_start(w[:, k, :], w_in[k * P:(k + 1) * P, :]).then_inc(w_in_s, 16)
                for g in range(NG):
                    sp.dma_start(wg[:, g, :, :], w_grp[g].rearrange("(k p) n -> p k n", p=P)).then_inc(small_in, 16)
                sp.dma_start(lsb[:, :], ls.partition_broadcast(P)).then_inc(small_in, 16)
                sp.dma_start(inv_count[:, :, :], counts.partition_broadcast(P)).then_inc(small_in, 16)
                with sp.Fori(0, TILES - 1) as i:
                    sp.wait_ge(tp_ready, 2 * i + 2)
                    sp.dma_start(xin[:, :], rows(h, i + 1)).then_inc(x_in, 16)
                for g in range(NG):
                    sp.wait_ge(y_done, 2 + TILES // 2 * (g + 1))
                    sp.dma_start(mix[:, g * PG:(g + 1) * PG].rearrange("(t p) c -> p t c", p=P), ysb[:, :, :]).then_inc(stored, 16)
                sp.wait_ge(stored, 16 * NG)

            @block.tensor
            def _(pe):
                with pe.Fori(0, TILES) as i:
                    pe.wait_ge(x_in, 16 * i + 16)
                    for b in range(2):
                        pe.wait_ge(tp_copied, 2 * i + b + 1)
                        for k in range(4):
                            last = nc.tensor.transpose(tp[:, b, k, :], xin[:, (4 * b + k) * P:(4 * b + k + 1) * P], K["ident"])
                        last.then_inc(tp_ready, 1)
                pe.wait_ge(w_in_s, 16 * KC)
                pe.wait_ge(small_in, 16 * (NG + 2))
                pe.wait_ge(tp_copied, 2 + 2 * TILES)

                def channels(ct):
                    for c in range(2):
                        pe.wait_ge(u_copied, 2 * ct + c + 1)
                        for k in range(KC):
                            last = nc.tensor.matmul(up[:, c, :], w[:, k, ct * P:(ct + 1) * P], hT[:, k, c * HALF:(c + 1) * HALF],
                                                    start=(k == 0), stop=(k == KC - 1))
                        last.then_inc(u_ready, 1)

                def outputs(g):
                    pe.wait_ge(p_ready, CG * (g + 1))
                    for t in range(TILES):
                        if t % 2 == 0:
                            pe.wait_ge(y_done, TILES // 2 * g + t // 2 + 1)
                        for k in range(CG):
                            last = nc.tensor.matmul(yp[:, t // 2 % 2, t % 2 * PG:(t % 2 + 1) * PG], pT[:, k, t * P:(t + 1) * P],
                                                    wg[:, g, k, :], start=(k == 0), stop=(k == CG - 1))
                        if t % 2:
                            last.then_inc(y_ready, 1)

                channels(0)
                channels(1)
                for g in range(NG):
                    if g + 1 < NG:
                        channels(CG * (g + 1))
                    outputs(g)
                    if g + 1 < NG:
                        channels(CG * (g + 1) + 1)

            @block.scalar
            def _(act):
                act.sem_inc(tp_copied, 2)
                act.sem_inc(u_copied, 2)
                with act.Fori(0, TILES) as i:
                    for b in range(2):
                        act.wait_ge(tp_ready, 2 * i + b + 1)
                        act.activation(hT[:, 4 * b:4 * b + 4, bass.ds(i * P, P)], tp[:, b, :, :], ACT.Copy).then_inc(tp_copied, 1)
                act.wait_ge(padded, 1)
                for ct in range(KC):
                    if ct > 0:
                        act.wait_ge(p_ready, ct)
                    for c in range(2):
                        act.wait_ge(u_ready, 2 * ct + c + 1)
                        act.copy(u[:, PADW + c * HALF:PADW + (c + 1) * HALF], up[:, c, :]).then_inc(u_copied, 1)

            @block.vector
            def _(dve):
                ch = Chain(dve, own)
                ch(dve.memset(s[:, :, 0:PADW], 0.0))
                dve.memset(u[:, 0:PADW], 0.0).then_inc(padded, 1)
                ch.wait()
                dve.wait_ge(padded, 1)
                dve.sem_inc(y_done, 2)

                def window(ct):
                    g = ct // CG
                    dve.wait_ge(u_copied, 2 * ct + 4)
                    src, step, n = u[:, :], 1, 0
                    while step < POOL_WINDOWS[g]:
                        ch(dve.tensor_tensor(s[:, n % 2, PADW:], src[:, PADW:], src[:, PADW - step:PADW + SEQ - step], ALU.add))
                        ch.wait()
                        src, step, n = s[:, n % 2, :], 2 * step, n + 1
                    ch(dve.tensor_tensor(s[:, n % 2, PADW:], src[:, PADW:], inv_count[:, g, :], ALU.mult))
                    ch.wait()
                    if ct % CG == 0 and g > 0:
                        dve.wait_ge(y_ready, TILES // 2 * g)
                    dve.tensor_tensor(pT[:, ct % CG, :], s[:, n % 2, PADW:], u[:, PADW:], ALU.subtract).then_inc(p_ready, 1)
                    dve.wait_ge(p_ready, ct + 1)

                def outputs(g):
                    if g > 0:
                        dve.wait_ge(stored, 16 * g)
                    for t in range(0, TILES, 2):
                        dve.wait_ge(y_ready, TILES // 2 * g + t // 2 + 1)
                        dve.tensor_tensor(ysb[:, t:t + 2, :], yp[:, t // 2 % 2, :].rearrange("p (a c) -> p a c", a=2),
                                          lsb[:, g * PG:(g + 1) * PG].unsqueeze(1).to_broadcast([P, 2, PG]), ALU.mult).then_inc(y_done, 1)

                dve.wait_ge(small_in, 16 * (NG + 2))
                window(0)
                window(1)
                for g in range(NG):
                    outputs(g)
                    if g + 1 < NG:
                        window(CG * (g + 1))
                        window(CG * (g + 1) + 1)


def phase_project(nc, K, name, x, w_in, q_norm, w_uq, kv_norm, w_ukv, mod, tabs, proj, mq, mk, mkv):
    AB = 3
    with Phase(nc, name) as ph:
        w = ph.sb("w", [P, KC, IN_COLS])
        wq, wkv = ph.sb("wq", [P, 2, MH * MQ]), ph.sb("wkv", [P, D])
        ln = ph.sb("ln", [P, MQR + MKVR])
        xin, h = ph.sb("x", [P, D]), ph.sb("h", [P, D])
        ss, rstd, half = ph.sb("ss", [P, 2]), ph.sb("rstd", [P, 1]), ph.sb("half", [P, 2])
        hT = ph.sb("hT", [P, KC, P])
        row = ph.sb("row", [P, IN_COLS])
        t1 = ph.sb("t1", [P, 4, 8, 32])
        ks = ph.sb("ks", [P, 4, 16])
        lsq, ms, lr, lat = ph.sb("lsq", [P, MQR + MKVR]), ph.sb("ms", [P, 2]), ph.sb("lr", [P, 2]), ph.sb("lat", [P, MQR + MKVR])
        latT = ph.sb("latT", [P, 3, P])
        kpe_new, kpe = ph.sb("kpe_new", [P, ROPE_D]), ph.sb("kpe", [P, ROPE_D])
        q_sb, k_sb, kv_sb = ph.sb("q", [P, MH, MQ]), ph.sb("k", [P, MH, MQ]), ph.sb("kv", [P, MH, NOPE + MV])
        tp = ph.ps("tp", [P, 2, 4, P])
        acc = ph.ps("acc", [P, AB, HALF])
        lt = ph.ps("lt", [P, 4, P])
        lp = ph.ps("lp", [P, 2, HALF])
        w_ready = [ph.sem(f"w_in{c}") for c in range(NCHUNK)]
        names = ("small_in", "x_in", "x_sq", "h_step", "h_ready", "tp_ready", "tp_copied", "acc_ready", "row_copied",
                 "ms_ready", "lr_ready", "lat_ready", "lt_ready", "latT_ready", "lp_ready", "lp_copied", "row_done",
                 "row_stored", "mla_done", "mla_stored", "own")
        (small_in, x_in, x_sq, h_step, h_ready, tp_ready, tp_copied, acc_ready, row_copied, ms_ready, lr_ready,
         lat_ready, lt_ready, latT_ready, lp_ready, lp_copied, row_done, row_stored, mla_done, mla_stored, own) = (
            ph.sem(n) for n in names)
        col = {n: row[:, a:b] for n, (a, b) in COLS.items()}

        with nc.Block() as block:
            @block.sync
            def _(sp):
                sp.dma_start(xin[:, :], x[0:P, :]).then_inc(x_in, 16)
                for c in range(NCHUNK):
                    load_columns(sp, w, w_in, c, CW, w_ready[c])
                sp.dma_start(ln[:, 0:MQR], q_norm.partition_broadcast(P)).then_inc(small_in, 16)
                sp.dma_start(ln[:, MQR:], kv_norm.partition_broadcast(P)).then_inc(small_in, 16)
                sp.dma_start(wq[:, :, :], w_uq.rearrange("(k p) n -> p k n", p=P)).then_inc(small_in, 16)
                sp.dma_start(wkv[:, :], w_ukv).then_inc(small_in, 16)

                def load(i):
                    sp.wait_ge(h_ready, i)
                    sp.dma_start(xin[:, :], rows(x, i)).then_inc(x_in, 16)

                def store_row(i):
                    sp.wait_ge(row_done, i + 1)
                    sp.dma_start(rows(proj, i), row[:, :]).then_inc(row_stored, 16)

                def store_mla(i):
                    sp.wait_ge(mla_done, i + 1)
                    for dst, src in ((mq, q_sb), (mk, k_sb), (mkv, kv_sb)):
                        sp.dma_start(rows(dst, i), src[:, :, :].rearrange("p h c -> p (h c)")).then_inc(mla_stored, 16)

                load(1)
                load(2)
                store_row(0)
                with sp.Fori(1, TILES - 2) as i:
                    load(i + 2)
                    store_row(i)
                    store_mla(i - 1)
                for i in (TILES - 2, TILES - 1):
                    store_row(i)
                    store_mla(i - 1)
                store_mla(TILES - 1)
                sp.wait_ge(row_stored, 16 * (TILES + 1))
                sp.wait_ge(mla_stored, 48 * (TILES + 1))

            @block.gpsimd
            def _(pool):
                pool.memset(half[:, :], -0.5).then_inc(h_step, 1)
                pool.wait_ge(h_step, 1)

                def modulate(i):
                    ch = Chain(pool, h_step, 4 * i + 1)
                    pool.wait_ge(x_sq, i + 1)
                    settle(pool)
                    ch(pool.tensor_scalar(ss[:, 1:2], ss[:, 0:1], 1.0 / D, RMS_EPS, ALU.mult, ALU.add))
                    ch.wait()
                    ch(pool.tensor_tensor(rstd[:, :], ss[:, 1:2], half[:, 0:1], ALU.pow))
                    ch.wait()
                    if not (isinstance(i, int) and i == 0):
                        pool.wait_ge(tp_ready, 2 * i)
                    settle(pool)
                    ch(pool.tensor_scalar(h[:, :], xin[:, :], rstd[:, 0:1], None, ALU.mult))
                    ch.wait()
                    ch(pool.tensor_tensor(h[:, :], h[:, :], mod[:, 0, :], ALU.mult))
                    ch.wait()
                    pool.tensor_tensor(h[:, :], h[:, :], mod[:, 1, :], ALU.add).then_inc(h_ready, 1)

                def latent_power(i):
                    pool.wait_ge(ms_ready, i + 1)
                    pool.tensor_tensor(lr[:, :], ms[:, :], half[:, :], ALU.pow).then_inc(lr_ready, 1)

                modulate(0)
                with pool.Fori(0, TILES - 1) as i:
                    modulate(i + 1)
                    latent_power(i)
                latent_power(TILES - 1)

            @block.tensor
            def _(pe):
                def transposes(i):
                    pe.wait_ge(h_ready, i + 1)
                    for b in range(2):
                        pe.wait_ge(tp_copied, 2 * i + b + 1)
                        for k in range(4):
                            last = nc.tensor.transpose(tp[:, b, k, :], h[:, (4 * b + k) * P:(4 * b + k + 1) * P], K["ident"])
                        last.then_inc(tp_ready, 1)

                def chunks(i, which):
                    for c in which:
                        pe.wait_ge(w_ready[c], 16)
                        pe.wait_ge(row_copied, NCHUNK * i + c + 1)
                        for k in range(KC):
                            last = nc.tensor.matmul(acc[:, c % AB, 0:CW], hT[:, k, :], w[:, k, c * CW:(c + 1) * CW],
                                                    start=(k == 0), stop=(k == KC - 1))
                        last.then_inc(acc_ready, 1)

                def latent_transposes(i):
                    pe.wait_ge(lat_ready, i + 1)
                    for k in range(3):
                        last = nc.tensor.transpose(lt[:, k, :], lat[:, k * P:(k + 1) * P], K["ident"])
                    last.then_inc(lt_ready, 1)

                def latents(i):
                    pe.wait_ge(small_in, 64)
                    pe.wait_ge(latT_ready, i + 1)
                    for c in range(4):
                        pe.wait_ge(lp_copied, 4 * i + c + 1)
                        if c < 2:
                            n = MH * MQ // 2
                            for k in range(2):
                                last = nc.tensor.matmul(lp[:, c % 2, 0:n], latT[:, k, :], wq[:, k, c * n:(c + 1) * n],
                                                        start=(k == 0), stop=(k == 1))
                        else:
                            last = nc.tensor.matmul(lp[:, c % 2, :], latT[:, 2, :], wkv[:, (c - 2) * HALF:(c - 1) * HALF],
                                                    start=True, stop=True)
                        last.then_inc(lp_ready, 1)

                def tile(i, first=False, last=False):
                    pe.wait_ge(tp_copied, 2 * i + 4)
                    chunks(i, range(NCHUNK - 1))
                    if not last:
                        transposes(i + 1)
                    if not first:
                        latent_transposes(i - 1)
                    chunks(i, [NCHUNK - 1])
                    if not first:
                        latents(i - 1)

                transposes(0)
                tile(0, first=True)
                with pe.Fori(1, TILES - 1) as i:
                    tile(i)
                tile(TILES - 1, last=True)
                latent_transposes(TILES - 1)
                latents(TILES - 1)

            @block.scalar
            def _(act):
                act.sem_inc(tp_copied, 2)
                act.sem_inc(row_copied, AB)
                act.sem_inc(lp_copied, 2)
                act.sem_inc(row_stored, 16)
                act.sem_inc(mla_stored, 48)

                def square(i):
                    act.wait_ge(x_in, 16 * i + 16)
                    act.activation(t1[:, :, :, :].rearrange("p a b c -> p (a b c)"), xin[:, :], ACT.Square,
                                   accum_out=ss[:, 0:1]).then_inc(x_sq, 1)

                def transposed(i):
                    for b in range(2):
                        act.wait_ge(tp_ready, 2 * i + b + 1)
                        act.copy(hT[:, 4 * b:4 * b + 4, :], tp[:, b, :, :]).then_inc(tp_copied, 1)

                def row_chunks(i, which):
                    for c in which:
                        act.wait_ge(acc_ready, NCHUNK * i + c + 1)
                        act.copy(row[:, c * CW:(c + 1) * CW], acc[:, c % AB, 0:CW]).then_inc(row_copied, 1)

                def latents_transposed(i):
                    act.wait_ge(lt_ready, i + 1)
                    act.copy(latT[:, :, :], lt[:, 0:3, :]).then_inc(latT_ready, 1)

                def latent_chunks(i):
                    act.wait_ge(mla_stored, 48 * i + 48)
                    for c in range(4):
                        act.wait_ge(lp_ready, 4 * i + c + 1)
                        dst = q_sb if c < 2 else kv_sb
                        n = MH // 2
                        act.copy(dst[:, c % 2 * n:(c % 2 + 1) * n, :],
                                 lp[:, c % 2, 0:n * dst.shape[-1]].rearrange("p (h c) -> p h c", h=n)).then_inc(lp_copied, 1)

                def tile(i, first=False, last=False, squares=True):
                    act.wait_ge(row_stored, 16 * i + 16)
                    row_chunks(i, range(NCHUNK - 1))
                    if not first:
                        latents_transposed(i - 1)
                    row_chunks(i, [NCHUNK - 1])
                    if not last:
                        transposed(i + 1)
                    if squares:
                        square(i + 2)
                    if not first:
                        latent_chunks(i - 1)

                square(0)
                transposed(0)
                square(1)
                tile(0, first=True)
                with act.Fori(1, TILES - 2) as i:
                    tile(i)
                tile(TILES - 2, squares=False)
                tile(TILES - 1, last=True, squares=False)
                latents_transposed(TILES - 1)
                latent_chunks(TILES - 1)

            @block.vector
            def _(dve):
                def rotate(ch, r1, r2, o1, o2, cos, sin, t):
                    ch(dve.tensor_tensor(t[0], r1, cos, ALU.mult))
                    ch(dve.tensor_tensor(t[1], r2, sin, ALU.mult))
                    ch(dve.tensor_tensor(t[2], r2, cos, ALU.mult))
                    ch(dve.tensor_tensor(t[3], r1, sin, ALU.mult))
                    ch.wait()
                    ch(dve.tensor_tensor(o1, t[0], t[1], ALU.subtract))
                    ch(dve.tensor_tensor(o2, t[2], t[3], ALU.add))
                    ch.wait()

                rt = ph.sb("rt", [P, 4, 8, 32])

                def angles(i, heads, step):
                    a = slice(i, i + 1) if isinstance(i, int) else bass.ds(i, 1)
                    n = RD // 2 // step
                    return [tabs[:, k, a, ::step].to_broadcast([P, heads, n]) for k in range(2)]

                N1, N2 = 6 + 6 + 4, 6 + 3

                def first_part(i, base):
                    ch = Chain(dve, own, base)
                    dve.wait_ge(row_copied, NCHUNK * i + AB + NCHUNK)
                    g = row[:, 0:2 * RH * RD].rearrange("p (h c) -> p h c", c=RD)
                    cos, sin = angles(i, 2 * RH, 1)
                    rotate(ch, g[:, :, 0:32], g[:, :, 32:64], g[:, :, 0:32], g[:, :, 32:64], cos, sin, [rt[:, n] for n in range(4)])
                    kr = col["mkr"].unsqueeze(1)
                    cos, sin = angles(i, 1, 2)
                    rotate(ch, kr[:, :, 0:16], kr[:, :, 16:32], kpe_new[:, 0:16].unsqueeze(1), kpe_new[:, 16:32].unsqueeze(1),
                           cos, sin, [ks[:, n:n + 1, :] for n in range(4)])
                    both = row[:, COLS["mq"][0]:COLS["mkv"][1]]
                    ch(dve.tensor_tensor(lsq[:, :], both, both, ALU.mult))
                    ch.wait()
                    ch(dve.reduce_sum(ms[:, 0:1], lsq[:, 0:MQR], axis=AX.X))
                    ch(dve.reduce_sum(ms[:, 1:2], lsq[:, MQR:], axis=AX.X))
                    ch.wait()
                    ch(dve.tensor_scalar(ms[:, 0:1], ms[:, 0:1], 1.0 / MQR, RMS_EPS, ALU.mult, ALU.add))
                    dve.tensor_scalar(ms[:, 1:2], ms[:, 1:2], 1.0 / MKVR, RMS_EPS, ALU.mult, ALU.add).then_inc(ms_ready, 1)
                    assert ch.n == N1
                    ch.wait()
                    dve.wait_ge(lr_ready, i + 1)
                    dve.wait_ge(small_in, 64)
                    if not isinstance(i, int):
                        dve.wait_ge(lt_ready, i)
                    dve.scalar_tensor_tensor(lat[:, 0:MQR], col["mq"], lr[:, 0:1], ln[:, 0:MQR], ALU.mult, ALU.mult)
                    dve.scalar_tensor_tensor(lat[:, MQR:], col["mkv"], lr[:, 1:2], ln[:, MQR:], ALU.mult, ALU.mult).then_inc(lat_ready, 1)
                    dve.wait_ge(lat_ready, i + 1)
                    dve.sem_inc(row_done, 1)

                def second_part(i, base):
                    ch = Chain(dve, own, base)
                    dve.wait_ge(lp_copied, 4 * i + 6)
                    cos, sin = angles(i, MH, 2)
                    a, b = q_sb[:, :, NOPE:NOPE + 16], q_sb[:, :, NOPE + 16:MQ]
                    rotate(ch, a, b, a, b, cos, sin, [rt[:, n, :, 0:16] for n in range(4)])
                    ch(dve.tensor_copy(k_sb[:, :, 0:NOPE], kv_sb[:, :, 0:NOPE]))
                    ch(dve.tensor_copy(k_sb[:, :, NOPE:MQ], kpe[:, :].unsqueeze(1).to_broadcast([P, MH, ROPE_D])))
                    ch.wait()
                    ch(dve.tensor_copy(kpe[:, :], kpe_new[:, :]))
                    ch.wait()
                    assert ch.n == N2
                    dve.sem_inc(mla_done, 1)

                first_part(0, 0)
                ch = Chain(dve, own, N1)
                ch(dve.tensor_copy(kpe[:, :], kpe_new[:, :]))
                ch.wait()
                with dve.Fori(1, TILES) as i:
                    first_part(i, (N1 + N2) * (i - 1) + N1 + 1)
                    second_part(i - 1, (N1 + N2) * (i - 1) + 2 * N1 + 1)
                second_part(TILES - 1, (N1 + N2) * (TILES - 1) + N1 + 1)


def mla_attention(nc, K, name, mq, mk, mkv, out):
    def tiles(ap, base, step, width):
        return lambda h: ap[:, bass.ds(h * step + base, width)].rearrange("(t p) c -> p t c", p=P)

    phase_attention(nc, K, name, tiles(mq, 0, MQ, MQ), tiles(mk, 0, MQ, MQ), tiles(mkv, NOPE, NOPE + MV, MV),
                    tiles(out, 0, MV, MV), 1, MQ, MV, K["chunked"], MQ ** -0.5)


def phase_mix_out(nc, K, name, proj, mla_o, x, w_g2, b_g2, gla_norm, w_out, mod, final_norm, out):
    final = final_norm is not None
    with Phase(nc, name) as ph:
        w = ph.sb("w", [P, KC, D])
        g2 = ph.sb("g2", [GRANK, P])
        bg = ph.sb("bg", [P, 1])
        gn = ph.sb("gn", [P, GDV])
        row = ph.sb("row", [P, IN_COLS])
        vv = ph.sb("vv", [P, 2, 256])
        mo = ph.sb("mo", [P, MH * MV])
        rT = ph.sb("rT", [P, 2, P])
        rkT = ph.sb("rkT", [P, RH, P])
        rqw = ph.sb("rqw", [P, 2, P])
        rkw = ph.sb("rkw", [P, RH * RD])
        gT = ph.sb("gT", [P, 2, P])
        ggT = ph.sb("ggT", [GRANK, P])
        z, ab, mn, sg, la, cum = (ph.sb(n, [P, P]) for n in ("z", "ab", "mn", "sg", "la", "cum"))
        last2, elast = ph.sb("last2", [P, 2]), ph.sb("elast", [P, 2])
        epos, eneg, el = (ph.sb(n, [P, P]) for n in ("epos", "eneg", "el"))
        qpos, qneg, kpos, kneg, kwT, kw = (ph.sb(n, [P, P]) for n in ("qpos", "qneg", "kpos", "kneg", "kwT", "kw"))
        kposm, knegm = ph.sb("kposm", [P, GH, P]), ph.sb("knegm", [P, GH, P])
        a_r, a_g = ph.sb("a_r", [P, RH, CH]), ph.sb("a_g", [P, GH, CH])
        past = ph.sb("past", [P, GH, CH], I32)
        um_r, um_g = ph.sb("um_r", [P, 2, 2, P]), ph.sb("um_g", [P, 2, 256])
        s_r, s_g = ph.sb("s_r", [P, 3, 2, P]), ph.sb("s_g", [P, 3, 256])
        o, osq = ph.sb("o", [P, 8, 64]), ph.sb("osq", [P, 8, 64])
        ms, rs, half = ph.sb("ms", [P, 8]), ph.sb("rs", [P, 8]), ph.sb("half", [P, 8])
        zs = ph.sb("zs", [P, D])
        mixed = ph.sb("mixed", [P, D])
        mT = ph.sb("mT", [P, KC, P])
        xr, xn = ph.sb("xr", [P, D]), ph.sb("xn", [P, D])
        if final:
            fn, junk = ph.sb("fn", [P, D]), ph.sb("junk", [P, D])
            fs, fr = ph.sb("fs", [P, 2]), ph.sb("fr", [P, 1])
        tA, tB, sc, pf = (ph.ps(n, [P, 4, P]) for n in ("tA", "tB", "sc", "pf"))
        u0, u1, op, acc = (ph.ps(n, [P, HALF]) for n in ("u0", "u1", "op", "acc"))
        S = {n: ph.sem(n) for n in (
            "w_in", "small_in", "row_in", "v_in", "x_in", "t_ready", "t_copied", "z_ready", "z_done", "mt_ready", "mt_copied",
            "acc_ready", "x_part", "kwt_ready", "kw_ready", "rs_ready", "gs_ready", "ar_ready", "ag_ready", "u_ready",
            "s_ready", "o_ready", "rk_ready", "ab_ready", "sg_ready", "cum_ready", "exps_ready", "q_ready", "silu_done",
            "zg_ready", "ms_ready", "rms_ready", "mix_ready", "o_copied", "xn_ready", "fs_ready", "fr_ready", "stored",
            "own", "res_own", "act_own", "pool_own", "kwt_done")}
        col = {n: row[:, a:b] for n, (a, b) in COLS.items()}
        scale_g = GDK ** -0.5

        with nc.Block() as block:
            @block.sync
            def _(sp):
                def load_row(i):
                    sp.dma_start(row[:, :], rows(proj, i)).then_inc(S["row_in"], 16)

                def load_values(i):
                    r = rows(proj, i)
                    for n, c in enumerate(("rv", "gv")):
                        sp.dma_start(vv[:, n, :], r[:, COLS[c][0]:COLS[c][1]]).then_inc(S["v_in"], 16)
                    sp.dma_start(mo[:, :], rows(mla_o, i)).then_inc(S["v_in"], 16)

                def store(i):
                    sp.wait_ge(S["xn_ready"], i + 1)
                    sp.dma_start(rows(out, i), xn[:, :]).then_inc(S["stored"], 16)

                def turn(i):
                    sp.wait_ge(S["zg_ready"], i + 1)
                    sp.wait_ge(S["rs_ready"], i + 1)
                    load_row(i + 1)
                    sp.wait_ge(S["mix_ready"], i + 1)
                    load_values(i + 1)

                load_row(0)
                load_values(0)
                sp.dma_start(g2[:, :], w_g2).then_inc(S["small_in"], 16)
                with nc.allow_non_contiguous_dma(reason="one bias per partition"):
                    sp.dma_start(bg[:, :], b_g2.rearrange("o (p a) -> p (o a)", a=1)).then_inc(S["small_in"], 16)
                sp.dma_start(gn[:, :], gla_norm.partition_broadcast(P)).then_inc(S["small_in"], 16)
                if final:
                    sp.dma_start(fn[:, :], final_norm.partition_broadcast(P)).then_inc(S["small_in"], 16)
                for k in range(KC):
                    sp.dma_start(w[:, k, :], w_out[k * P:(k + 1) * P, :]).then_inc(S["w_in"], 16)
                sp.dma_start(xr[:, :], rows(x, 0)).then_inc(S["x_in"], 16)
                turn(0)
                with sp.Fori(1, TILES - 1) as i:
                    turn(i)
                    store(i - 1)
                    sp.dma_start(xr[:, :], rows(x, i)).then_inc(S["x_in"], 16)
                store(TILES - 2)
                sp.dma_start(xr[:, :], rows(x, TILES - 1)).then_inc(S["x_in"], 16)
                store(TILES - 1)
                sp.wait_ge(S["stored"], 16 * (TILES + 1))

            @block.gpsimd
            def _(pool):
                pool.memset(half[:, :], -0.5).then_inc(S["pool_own"], 1)
                pool.memset(s_r[:, 2, :, :], 0.0).then_inc(S["pool_own"], 1)
                pool.memset(s_g[:, 2, :], 0.0).then_inc(S["pool_own"], 1)
                pool.memset(rkT[:, :, :], 0.0).then_inc(S["pool_own"], 1)
                pool.wait_ge(S["pool_own"], 4)
                pool.wait_ge(S["small_in"], 64 if final else 48)

                def final_power(i):
                    pool.wait_ge(S["fs_ready"], i + 1)
                    pool.tensor_tensor(fr[:, :], fs[:, 1:2], half[:, 0:1], ALU.pow).then_inc(S["fr_ready"], 1)

                def tile(i):
                    pool.wait_ge(S["row_in"], 16 * i + 16)
                    pool.tensor_tensor(rkw[:, :].rearrange("p (h c) -> p h c", h=RH), col["rk"].rearrange("p (h c) -> p h c", h=RH),
                                       K["rkw"].unsqueeze(2).to_broadcast([P, RH, RD]), ALU.mult).then_inc(S["rk_ready"], 1)
                    pool.wait_ge(S["t_copied"], 3 * i + 1)
                    pool.tensor_tensor(rqw[:, :, :], rT[:, :, :], K["rqw"].rearrange("p (a c) -> p a c", a=2),
                                       ALU.mult).then_inc(S["rk_ready"], 1)
                    pool.wait_ge(S["silu_done"], 3 * i + 3)
                    g = zs[:, 768:].rearrange("p (h c) -> p h c", h=GH)
                    pool.tensor_tensor(g, g, gn[:, :].unsqueeze(1).to_broadcast([P, GH, GDV]), ALU.mult).then_inc(S["zg_ready"], 1)
                    if final and not (isinstance(i, int) and i == 0):
                        final_power(i - 1)
                    pool.wait_ge(S["ms_ready"], i + 1)
                    pool.tensor_tensor(rs[:, :], ms[:, :], half[:, :], ALU.pow).then_inc(S["rms_ready"], 1)

                tile(0)
                with pool.Fori(1, TILES) as i:
                    tile(i)
                if final:
                    final_power(TILES - 1)

            @block.tensor
            def _(pe):
                T, M = nc.tensor.transpose, nc.tensor.matmul

                def open_tile(i):
                    pe.wait_ge(S["row_in"], 16 * i + 16)
                    for n in range(4):
                        last = T(tA[:, n, :], row[:, n * P:(n + 1) * P], K["ident"])
                    last.then_inc(S["t_ready"], 1)
                    T(tB[:, 0, :], col["gq"], K["ident"])
                    T(tB[:, 1, :], col["gk"], K["ident"])
                    T(tB[0:GRANK, 2, :], col["gg"], K["ident"]).then_inc(S["t_ready"], 1)
                    pe.wait_ge(S["small_in"], 64 if final else 48)
                    pe.wait_ge(S["t_copied"], 3 * i + 3)
                    M(tB[:, 3, :], g2[:, :], ggT[:, :], start=True, stop=True).then_inc(S["z_ready"], 1)
                    for h in range(RH):
                        for c in range(2):
                            t = slice(c * CH, (c + 1) * CH)
                            last = M(sc[t, h // 2, h % 2 * CH:(h % 2 + 1) * CH], rkT[:, h, t], rT[:, h // 2, t],
                                     start=True, stop=True)
                    last.then_inc(S["rs_ready"], 1)

                def mixed_transposes(i):
                    pe.wait_ge(S["mix_ready"], i + 1)
                    for b, bank in enumerate((tA, tB)):
                        for k in range(4):
                            last = T(bank[:, k, :], mixed[:, (4 * b + k) * P:(4 * b + k + 1) * P], K["ident"])
                        last.then_inc(S["mt_ready"], 1)
                    pe.wait_ge(S["w_in"], 16 * KC)
                    pe.wait_ge(S["mt_copied"], 2 * i + 2)

                def project(i, c):
                    pe.wait_ge(S["x_part"], 2 * i + c + 1)
                    for k in range(KC):
                        last = M(acc[:, :], mT[:, k, :], w[:, k, c * HALF:(c + 1) * HALF], start=(k == 0), stop=(k == KC - 1))
                    last.then_inc(S["acc_ready"], 1)

                def scores_and_updates(i):
                    pe.wait_ge(S["q_ready"], i + 1)
                    T(sc[:, 2, :], kwT[:, :], K["ident"]).then_inc(S["kwt_ready"], 1)
                    for n, (k_, q_) in enumerate(((knegm, qpos), (kposm, qneg))):
                        for h in range(GH):
                            for c in range(2):
                                t = slice(c * CH, (c + 1) * CH)
                                last = M(pf[t, 2 * n + h // 2, h % 2 * CH:(h % 2 + 1) * CH], k_[:, h, t], q_[:, t], start=True, stop=True)
                    last.then_inc(S["gs_ready"], 1)
                    pe.wait_ge(S["v_in"], 48 * i + 48)
                    pe.wait_ge(S["rk_ready"], 2 * i + 2)
                    pe.wait_ge(S["kw_ready"], i + 1)
                    for c in range(2):
                        t = slice(c * CH, (c + 1) * CH)
                        for p in range(2):
                            M((u0, u1)[c][:, p * P:(p + 1) * P], rkw[t, p * P:(p + 1) * P], vv[t, 0, p * P:(p + 1) * P],
                              start=True, stop=True)
                        last = M((u0, u1)[c][:, 256:512], kw[t, :], vv[t, 1, :], start=True, stop=True)
                    last.then_inc(S["u_ready"], 1)

                def outputs(i):
                    pe.wait_ge(S["ar_ready"], i + 1)
                    pe.wait_ge(S["ag_ready"], i + 1)
                    pe.wait_ge(S["s_ready"], i + 1)
                    for c in range(2):
                        t = slice(c * CH, (c + 1) * CH)
                        for p in range(2):
                            M(op[t, p * P:(p + 1) * P], rqw[:, p, t], s_r[:, c, p, :], start=True, stop=False)
                            for h in (2 * p, 2 * p + 1):
                                M(op[t, h * RD:(h + 1) * RD], a_r[t, h, :], vv[t, 0, h * RD:(h + 1) * RD], start=False, stop=(h % 2 == 1))
                        M(op[t, 256:512], qpos[:, t], s_g[:, c, :], start=True, stop=False)
                        for h in range(GH):
                            last = M(op[t, 256 + h * GDV:256 + (h + 1) * GDV], a_g[t, h, :], vv[t, 1, h * GDV:(h + 1) * GDV],
                                     start=False, stop=(h == GH - 1))
                    last.then_inc(S["o_ready"], 1)

                open_tile(0)
                scores_and_updates(0)
                outputs(0)
                with pe.Fori(1, TILES) as i:
                    open_tile(i)
                    pe.wait_ge(S["z_done"], i + 1)
                    mixed_transposes(i - 1)
                    project(i - 1, 0)
                    scores_and_updates(i)
                    project(i - 1, 1)
                    outputs(i)
                mixed_transposes(TILES - 1)
                project(TILES - 1, 0)
                project(TILES - 1, 1)

            @block.scalar
            def _(act):
                def copies(i):
                    act.wait_ge(S["t_ready"], 2 * i + 1)
                    act.copy(rT[:, :, :], tA[:, 0:2, :])
                    for h in range(2):
                        r = slice(RD * h, RD * h + RD)
                        last = act.copy(rkT[r, h::2, :], tA[r, 2:4, :])
                    last.then_inc(S["t_copied"], 1)
                    act.wait_ge(S["t_ready"], 2 * i + 2)
                    act.copy(gT[:, :, :], tB[:, 0:2, :]).then_inc(S["t_copied"], 1)
                    act.copy(ggT[:, :], tB[0:GRANK, 2, :]).then_inc(S["t_copied"], 1)

                def mixed_copies(i):
                    for b, bank in enumerate((tA, tB)):
                        act.wait_ge(S["mt_ready"], 2 * i + b + 1)
                        act.copy(mT[:, 4 * b:4 * b + 4, :], bank[:, :, :]).then_inc(S["mt_copied"], 1)

                def gates(i):
                    ch = Chain(act, S["act_own"], i)
                    act.wait_ge(S["ab_ready"], i + 1)
                    ch(act.activation(ab[:, :], ab[:, :], ACT.Exp, scale=-1.0))
                    ch.wait()
                    act.activation(sg[:, :], ab[:, :], ACT.Ln, bias=1.0).then_inc(S["sg_ready"], 1)
                    act.wait_ge(S["cum_ready"], i + 1)
                    act.activation(epos[:, :], cum[:, :], ACT.Exp, scale=1.0 / 16).then_inc(S["exps_ready"], 1)
                    act.activation(eneg[:, :], cum[:, :], ACT.Exp, scale=-1.0 / 16).then_inc(S["exps_ready"], 1)
                    for c in range(2):
                        t = slice(c * CH, (c + 1) * CH)
                        act.activation(el[:, t], cum[:, t], ACT.Exp, scale=-1.0 / 16, bias=last2[:, c:c + 1]).then_inc(S["exps_ready"], 1)
                    act.activation(elast[:, :], last2[:, :], ACT.Exp).then_inc(S["exps_ready"], 1)

                def silus(i):
                    for n, (c, a) in enumerate((("rz", 0), ("mz", 256), ("gz", 768))):
                        width = COLS[c][1] - COLS[c][0]
                        act.activation(zs[:, a:a + width], col[c], ACT.Silu).then_inc(S["silu_done"], 1)

                act.sem_inc(S["stored"], 16)
                act.wait_ge(S["pool_own"], 4)
                copies(0)
                gates(0)
                silus(0)
                with act.Fori(1, TILES) as i:
                    copies(i)
                    mixed_copies(i - 1)
                    gates(i)
                    act.wait_ge(S["mix_ready"], i)
                    silus(i)
                mixed_copies(TILES - 1)

            @block.vector
            def _(dve):
                dve.sem_inc(S["x_part"], 1)
                n_res = 5 if final else 2
                n_tile = 31

                def residual(i, c):
                    ch = Chain(dve, S["res_own"], n_res * i + c)
                    if c == 0:
                        dve.wait_ge(S["x_in"], 16 * i + 16)
                        dve.wait_ge(S["stored"], 16 * i + 16)
                    s = slice(c * HALF, (c + 1) * HALF)
                    dve.wait_ge(S["acc_ready"], 2 * i + c + 1)
                    dve.tensor_tensor(xn[:, s], acc[:, :], mod[:, 2, s], ALU.mult).then_inc(S["x_part"], 1)
                    dve.wait_ge(S["x_part"], 2 * i + c + 2)
                    ch(dve.tensor_tensor(xn[:, s], xn[:, s], xr[:, s], ALU.add))
                    if c == 1:
                        ch.wait()
                        if final:
                            ch(dve.tensor_tensor(junk[:, :], xn[:, :], xn[:, :], ALU.mult))
                            ch.wait()
                            ch(dve.reduce_sum(fs[:, 0:1], junk[:, :], axis=AX.X))
                            ch.wait()
                            dve.tensor_scalar(fs[:, 1:2], fs[:, 0:1], 1.0 / D, RMS_EPS, ALU.mult, ALU.add).then_inc(S["fs_ready"], 1)
                        else:
                            dve.sem_inc(S["xn_ready"], 1)

                def finish(i):
                    if final:
                        ch = Chain(dve, S["res_own"], n_res * i + 4)
                        dve.wait_ge(S["fr_ready"], i + 1)
                        ch(dve.scalar_tensor_tensor(xn[:, :], xn[:, :], fr[:, 0:1], fn[:, :], ALU.mult, ALU.mult))
                        ch.wait()
                        dve.sem_inc(S["xn_ready"], 1)

                def tile(i):
                    ch = Chain(dve, S["own"], n_tile * i + 1)
                    dve.wait_ge(S["z_ready"], i + 1)
                    ch(dve.tensor_scalar(z[:, :], tB[:, 3, :], bg[:, 0:1], None, ALU.add))
                    ch.wait()
                    dve.sem_inc(S["z_done"], 1)
                    dve.scalar_tensor_tensor(ab[:, :], z[:, :], -1.0, z[:, :], ALU.mult, ALU.max).then_inc(S["ab_ready"], 1)
                    ch(dve.tensor_scalar(mn[:, :], z[:, :], 0.0, None, ALU.min))
                    dve.wait_ge(S["rs_ready"], i + 1)
                    dve.tensor_tensor(a_r[:, :, :], sc[:, 0:2, :].rearrange("p a (b c) -> p (a b) c", c=CH),
                                      K["decay"].rearrange("p (h c) -> p h c", h=RH), ALU.mult).then_inc(S["ar_ready"], 1)
                    ch.wait()
                    dve.wait_ge(S["sg_ready"], i + 1)
                    ch(dve.tensor_tensor(la[:, :], mn[:, :], sg[:, :], ALU.subtract))
                    ch.wait()
                    ch(dve.tensor_tensor_scan(cum[:, :], K["scan"], la[:, :], 0.0, ALU.mult, ALU.add))
                    ch.wait()
                    dve.tensor_scalar(last2[:, :], cum[:, CH - 1::CH], 1.0 / 16, None, ALU.mult).then_inc(S["cum_ready"], 1)
                    dve.wait_ge(S["exps_ready"], 5 * i + 5)
                    ch(dve.tensor_tensor(qpos[:, :], gT[:, 0, :], epos[:, :], ALU.mult))
                    ch(dve.tensor_tensor(qneg[:, :], gT[:, 0, :], eneg[:, :], ALU.mult))
                    for dst, e in ((kneg, eneg), (kpos, epos), (kwT, el)):
                        ch(dve.scalar_tensor_tensor(dst[:, :], gT[:, 1, :], scale_g, e[:, :], ALU.mult, ALU.mult))
                    ch.wait()
                    hm = K["ghead"].unsqueeze(2).to_broadcast([P, GH, P])
                    ch(dve.tensor_tensor(knegm[:, :, :], kneg[:, :].unsqueeze(1).to_broadcast([P, GH, P]), hm, ALU.mult))
                    ch(dve.tensor_tensor(kposm[:, :, :], kpos[:, :].unsqueeze(1).to_broadcast([P, GH, P]), hm, ALU.mult))
                    ch.wait()
                    dve.sem_inc(S["q_ready"], 1)
                    if not isinstance(i, int):
                        residual(i - 1, 0)
                    dve.wait_ge(S["kwt_ready"], i + 1)
                    dve.tensor_copy(kw[:, :], sc[:, 2, :]).then_inc(S["kw_ready"], 1)
                    dve.wait_ge(S["gs_ready"], i + 1)
                    ch(dve.tensor_copy(a_g[:, :, :], pf[:, 2:4, :].rearrange("p a (b c) -> p (a b) c", c=CH)))
                    ch.wait()
                    settle(dve)
                    dve.copy_predicated(a_g[:, :, :], past[:, :, :], pf[:, 0:2, :].rearrange("p a (b c) -> p (a b) c", c=CH)).then_inc(S["ag_ready"], 1)
                    dve.wait_ge(S["u_ready"], i + 1)
                    for c, bank in enumerate((u0, u1)):
                        ch(dve.tensor_tensor(um_r[:, c, :, :], bank[:, 0:256].rearrange("p (a c) -> p a c", a=2),
                                             K["rbd"].unsqueeze(1).to_broadcast([P, 2, P]), ALU.mult))
                        ch(dve.tensor_tensor(um_g[:, c, :], bank[:, 256:512], K["gbd"], ALU.mult))
                    ch(dve.tensor_copy(s_r[:, 0, :, :], s_r[:, 2, :, :]))
                    ch(dve.tensor_copy(s_g[:, 0, :], s_g[:, 2, :]))
                    ch.wait()
                    for c in range(2):
                        for p in range(2):
                            ch(dve.scalar_tensor_tensor(s_r[:, c + 1, p, :], s_r[:, c, p, :], K["ra"][:, p:p + 1], um_r[:, c, p, :], ALU.mult, ALU.add))
                        ch(dve.scalar_tensor_tensor(s_g[:, c + 1, :], s_g[:, c, :], elast[:, c:c + 1], um_g[:, c, :], ALU.mult, ALU.add))
                        ch.wait()
                    dve.sem_inc(S["s_ready"], 1)
                    if not isinstance(i, int):
                        residual(i - 1, 1)
                    dve.wait_ge(S["o_ready"], i + 1)
                    ch(dve.tensor_copy(o[:, :, :], op[:, :].rearrange("p (h c) -> p h c", h=8)))
                    ch.wait()
                    ch(dve.tensor_tensor(osq[:, :, :], o[:, :, :], o[:, :, :], ALU.mult))
                    ch.wait()
                    ch(dve.reduce_sum(ms[:, :], osq[:, :, :], axis=AX.X))
                    ch.wait()
                    dve.tensor_scalar(ms[:, :], ms[:, :], 1.0 / 64, RMS_EPS, ALU.mult, ALU.add).then_inc(S["ms_ready"], 1)
                    dve.wait_ge(S["zg_ready"], i + 1)
                    ch(dve.tensor_tensor(mixed[:, 256:768], mo[:, :], zs[:, 256:768], ALU.mult))
                    dve.wait_ge(S["rms_ready"], i + 1)
                    ch(dve.tensor_tensor(o[:, :, :], o[:, :, :], rs[:, :].unsqueeze(2).to_broadcast([P, 8, 64]), ALU.mult))
                    ch.wait()
                    o2 = o[:, :, :].rearrange("p h c -> p (h c)")
                    ch(dve.tensor_tensor(mixed[:, 0:256], o2[:, 0:256], zs[:, 0:256], ALU.mult))
                    ch(dve.tensor_tensor(mixed[:, 768:], o2[:, 256:], zs[:, 768:], ALU.mult))
                    ch.wait()
                    dve.sem_inc(S["mix_ready"], 1)
                    if not isinstance(i, int):
                        finish(i - 1)
                    assert ch.n == n_tile, ch.n

                ch = Chain(dve, S["own"])
                ch(dve.tensor_copy(past[:, :, :], K["past"].unsqueeze(1).to_broadcast([P, GH, CH])))
                ch.wait()
                dve.wait_ge(S["small_in"], 64 if final else 48)
                dve.wait_ge(S["pool_own"], 4)
                tile(0)
                with dve.Fori(1, TILES) as i:
                    tile(i)
                residual(TILES - 1, 0)
                residual(TILES - 1, 1)
                finish(TILES - 1)


def program(nc, A, consts, out):
    def scratch(name, *shape):
        return nc.dram_tensor(f"scratch_{name}", shape, F32, kind="Internal").ap()

    qkv, mix, y = scratch("qkv", SEQ, QKV), scratch("mix", SEQ, D), scratch("y", BLOCKS * P, D)
    h = [scratch(f"h{n}", SEQ, D) for n in range(4)]
    proj, mla_o, x1 = scratch("proj", SEQ, IN_COLS), scratch("mla_o", SEQ, MH * MV), scratch("x1", SEQ, D)
    mq, mk, mkv = scratch("mq", SEQ, MH * MQ), scratch("mk", SEQ, MH * MQ), scratch("mkv", SEQ, MH * (NOPE + MV))

    with ExitStack() as stack:
        def held(name, shape, dt=F32):
            return stack.enter_context(nc.sbuf_tensor(name, shape, dt))

        logits = held("logits", [P, TILES, GROUPS + EXPERTS])
        gates, dest_i = held("gates", [P, 2, TILES]), held("dest_i", [P, 2, TILES], I32)
        tok_i, blk_i, pairs_i = held("tok_i", [P, BCOLS], I32), held("blk_i", [P, BCOLS], I32), held("pairs_i", [P, 1], I32)
        mods, tabs = held("mods", [P, 2, 3, D]), held("tabs", [P, 2, TILES, RD // 2])

        def moe_layer(K, l, mix_w, h_in, h_mid, h_out):
            r = slice(l, l + 1)
            with ExpertWeights(nc, f"weights{l}", A["moe_w_gate"][l], A["moe_w_up"][l], A["moe_w_down"][l]) as weights:
                phase_out_norm(nc, K, f"out{l}", mix, mix_w, h_in, A["ln_g"][l, 0:1, :], A["ln_b"][l, 0:1, :],
                               A["moe_w_grp_router"][l], A["moe_b_grp_router"][r, :], A["moe_w_exp_router"][l],
                               A["moe_b_exp_router"][r, :], h_mid, logits, weights)
                phase_route(nc, K, f"route{l}", logits, gates, dest_i, tok_i, blk_i, pairs_i)
                phase_experts(nc, K, f"experts{l}", h_mid, weights, tok_i, blk_i, pairs_i, y)
            phase_combine(nc, K, f"combine{l}", h_mid, y, gates, dest_i, A["ln_g"][l, 1:2, :], A["ln_b"][l, 1:2, :], h_out)

        def body(K):
            x = A["x"][0]
            phase_qkv(nc, K, x, A["attn_w_qkv"][0], qkv, y, A["positions_2"], tabs)
            diff_attention(nc, K, qkv, [A[f"attn_{n}"] for n in ("lq1", "lk1", "lq2", "lk2")], A["attn_sub_g"], mix,
                           (A["c_2"], A["ada_w_2"], A["ada_b_2"], A["norm_w_2"], mods))
            moe_layer(K, 0, A["attn_w_o"][0], x, h[0], h[1])
            phase_pool(nc, K, h[1], A["pool_w_in"][0], A["pool_w_grp"][0], A["pool_scale"], A["inverse_counts"], mix)
            moe_layer(K, 1, A["pool_w_out"][0], h[1], h[2], h[3])
            src = h[3]
            for l in range(2):
                r = slice(l, l + 1)
                mod = mods[:, l]
                phase_project(nc, K, f"project{l}", src, A["w_in_2"][l], A["mla_q_norm_2"][r, :], A["w_uq_2"][l],
                              A["mla_kv_norm_2"][r, :], A["w_ukv_2"][l], mod, tabs, proj, mq, mk, mkv)
                mla_attention(nc, K, f"mla{l}", mq, mk, mkv, mla_o)
                phase_mix_out(nc, K, f"mixout{l}", proj, mla_o, src, A["gla_w_g2_2"][l], A["gla_b_g2_2"][r, :],
                              A["gla_norm_2"][r, :], A["w_out_2"][l], mod,
                              A["final_norm_2"].rearrange("(a n) -> a n", a=1) if l == 1 else None, out[0] if l == 1 else x1)
                src = x1

        with_constants(nc, stack, consts, body)


_INS = ["x", "attn_w_qkv", "attn_w_o", "attn_lq1", "attn_lk1", "attn_lq2", "attn_lk2", "attn_sub_g", "pool_w_in",
        "pool_w_grp", "pool_scale", "pool_w_out", "ln_g", "ln_b", "moe_w_grp_router", "moe_b_grp_router",
        "moe_w_exp_router", "moe_b_exp_router", "moe_w_gate", "moe_w_up", "moe_w_down", "c_2", "positions_2",
        "norm_w_2", "ada_w_2", "ada_b_2", "w_in_2", "mla_q_norm_2", "w_uq_2", "mla_kv_norm_2", "w_ukv_2",
        "gla_w_g2_2", "gla_b_g2_2", "gla_norm_2", "w_out_2", "final_norm_2"]


def kernel(**inputs):
    import concourse.bacc as bacc
    from concourse.bass_utils import run_bass_kernel_spmd

    nc = bacc.Bacc("TRN2", target_bir_lowering=False, num_devices=1)
    arrays, args = {}, {}
    for name in _INS:
        a = np.ascontiguousarray(inputs[name])
        arrays[f"in_{name}_dram"] = a
        args[name] = nc.dram_tensor(f"in_{name}_dram", a.shape, mybir.dt.from_np(a.dtype), kind="ExternalInput").ap()
    packed = np.concatenate(list(constant_parts().values()), axis=1)
    arrays["consts_dram"] = packed
    consts = nc.dram_tensor("consts_dram", packed.shape, F32, kind="ExternalInput").ap()
    arrays["counts_dram"] = inverse_counts()
    args["inverse_counts"] = nc.dram_tensor("counts_dram", arrays["counts_dram"].shape, F32, kind="ExternalInput").ap()
    out = nc.dram_tensor("out_0_dram", (1, SEQ, D), F32, kind="ExternalOutput").ap()
    program(nc, args, consts, out)
    r = run_bass_kernel_spmd(nc, [arrays], core_ids=[0])
    return r.results[0]["out_0_dram"]
```

```python
import math
from contextlib import ExitStack

import numpy as np
import concourse.bass as bass
from concourse import mybir

F32 = mybir.dt.float32
F32R = mybir.dt.float32r
I32 = mybir.dt.int32
ALU = mybir.AluOpType
ACT = mybir.ActivationFunctionType
AX = mybir.AxisListType

P = 128
SEQ = 1024
D = 1024
TILES = SEQ // P
KC = D // P
HALF = 512

HEADS = 8
HD = 64
VD = 2 * HD
QKV = 3 * D
ROT = HD // 4
LAMBDA_INIT = 0.8 - 0.6 * math.exp(0.0)
ALPHA = 4 ** 0.25
LN_EPS = 1e-5
RMS_EPS = 1e-6
NEG = -1.0e30

GROUPS, PER_GROUP = 4, 8
EXPERTS = GROUPS * PER_GROUP
DE = D // 2
OVER = 2 * SEQ // P
BLOCKS = EXPERTS + OVER
BCOLS = BLOCKS + 2
POOL_WINDOWS = (2, 4, 8, 16)
PG = D // len(POOL_WINDOWS)

RH, RD = 4, 64
MH, NOPE, ROPE_D, MV = 8, 64, 32, 64
MQ = NOPE + ROPE_D
MQR, MKVR = 256, 128
GH, GDK, GDV, GRANK = 4, 32, 64, 16
CH = 64
COLS = {}
_at = 0
for _n, _w in (("rq", 256), ("rk", 256), ("rv", 256), ("rz", 256), ("mq", 256), ("mkv", 128), ("mkr", 32),
               ("mz", 512), ("gq", 128), ("gk", 128), ("gv", 256), ("gg", 16), ("gz", 256)):
    COLS[_n] = (_at, _at + _w)
    _at += _w
IN_COLS = _at
NCHUNK = 6
CW = IN_COLS // NCHUNK


def constant_parts():
    p = np.arange(P)[:, None]
    c = np.arange(P)[None, :]
    f = np.float32
    parts = {
        "ident": (p == c).astype(f),
        "causal": np.where(c > p, f(NEG), f(0)),
        "chunked": np.where((c >= CH) & (p < CH), f(NEG), f(0)),
        "before": (p < c).astype(f),
        "iota": np.broadcast_to(np.arange(P, dtype=f), (P, P)),
        "token": (p + P * np.arange(TILES)[None, :]).astype(f),
    }
    inv = f(500000.0) ** (-np.arange(0, ROT, 2, dtype=f) / f(ROT))
    ang = np.arange(SEQ, dtype=f)[:, None] * inv[None, :].astype(f)
    for name, t in (("rcos", np.cos(ang)), ("rsin", np.sin(ang))):
        parts[name] = t.astype(f).reshape(TILES, P, ROT // 2).transpose(1, 0, 2).reshape(P, -1)
    parts["inv"] = np.broadcast_to(f(10000.0) ** (-np.arange(RD // 2, dtype=f) / f(RD // 2)), (P, RD // 2))
    lg = np.log1p(-np.exp2(-5.0 - np.arange(RH, dtype=f))).astype(np.float64)
    j, i = np.arange(P)[:, None, None] % CH, np.arange(CH)[None, None, :]
    scale = RD ** -0.5
    parts["decay"] = (np.exp(lg[None, :, None] * np.abs(i - j)) * scale).reshape(P, -1)
    head = 2 * np.arange(2)[None, :, None] + (np.arange(P) // RD)[:, None, None]
    parts["rqw"] = np.exp(lg[head] * (np.arange(P)[None, None, :] % CH + 1.0)).reshape(P, -1)
    parts["rkw"] = np.exp(lg[None, :] * (CH - 1.0 - np.arange(P)[:, None] % CH)) * scale
    parts["ra"] = np.exp(CH * lg[head[:, :, 0]])
    parts["rbd"] = (p // RD == c // RD).astype(f)
    parts["gbd"] = (p // GDK == np.arange(GH * GDV)[None, :] // GDV).astype(f)
    parts["ghead"] = (p // GDK == np.arange(GH)[None, :]).astype(f)
    parts["scan"] = np.broadcast_to((np.arange(P) % CH != 0).astype(f), (P, P))
    parts["past"] = (np.arange(CH)[None, :] >= p % CH).astype(f)
    return {n: np.ascontiguousarray(a, dtype=f) for n, a in parts.items()}


def inverse_counts():
    t = np.arange(SEQ)
    return np.stack([1.0 / np.minimum(t + 1, w) for w in POOL_WINDOWS]).astype(np.float32).reshape(1, -1)


class Phase:

    def __init__(self, nc, name):
        self.nc, self.name = nc, name

    def __enter__(self):
        self.stack = ExitStack()
        self.sems = []
        return self

    def sb(self, name, shape, dt=F32):
        return self.stack.enter_context(self.nc.sbuf_tensor(f"{self.name}_{name}", shape, dt))

    def ps(self, name, shape):
        return self.stack.enter_context(self.nc.psum_tensor(f"{self.name}_{name}", shape, F32))

    def sem(self, name):
        s = self.nc.alloc_semaphore(f"{self.name}_{name}")
        self.sems.append(s)
        return s

    def __exit__(self, *exc):
        self.stack.close()
        if exc[0] is None:
            self.nc.clear_and_free_semaphores(self.sems)
            self.nc.all_engine_barrier()


class Chain:

    def __init__(self, eng, sem, base=0):
        self.eng, self.sem, self.base, self.n = eng, sem, base, 0

    def __call__(self, ins):
        self.n += 1
        ins.then_inc(self.sem, 1)
        return ins

    def wait(self):
        self.eng.wait_ge(self.sem, self.base + self.n)


def rows(ap, i):
    return ap[i * P:(i + 1) * P, :] if isinstance(i, int) else ap[bass.ds(i * P, P), :]


SETTLED = []


def settle(eng):
    eng.sem_inc(SETTLED[-1], 1)


class Angles:

    def __init__(self, ph, K, positions, tabs):
        self.K, self.positions, self.tabs = K, positions, tabs
        n = RD // 2
        self.pi, self.pf = ph.sb("pos_i", [P, TILES], I32), ph.sb("pos_f", [P, TILES])
        self.ang, self.kf = ph.sb("ang", [P, TILES, n]), ph.sb("kf", [P, TILES, n])
        self.r, self.t = ph.sb("rest", [P, 2, TILES, n]), ph.sb("tabs", [P, 2, TILES, n])
        self.ki = ph.sb("ki", [P, TILES, n], I32)
        self.p_in, self.own, self.r_ready, self.t_ready, self.t_stored = (
            ph.sem(n) for n in ("p_in", "ang_own", "rest_ready", "tabs_ready", "tabs_stored"))

    def load(self, nc, sp):
        with nc.allow_non_contiguous_dma(reason="1024 positions"):
            sp.dma_start(self.pi[:, :], self.positions.rearrange("o (t p) -> p (o t)", p=P)).then_inc(self.p_in, 16)

    def reduce(self, dve):
        two_pi = 2 * math.pi
        c1 = 6.28125
        c2 = float(np.float32(np.round((two_pi - c1) * 2 ** 22) / 2 ** 22))
        c3 = two_pi - c1 - c2
        ch = Chain(dve, self.own)
        pf, ang, kf, ki = self.pf, self.ang, self.kf, self.ki
        shape = [P, TILES, RD // 2]

        def step(ins):
            ch(ins)
            ch.wait()

        dve.wait_ge(self.p_in, 16)
        step(dve.tensor_copy(pf[:, :], self.pi[:, :]))
        step(dve.tensor_tensor(ang[:, :, :], pf[:, :].unsqueeze(2).to_broadcast(shape),
                               self.K["inv"].unsqueeze(1).to_broadcast(shape), ALU.mult))
        for n, turn in enumerate((0.25, 0.0)):
            r = self.r[:, n, :, :]
            step(dve.tensor_scalar(kf[:, :, :], ang[:, :, :], 1.0 / two_pi, turn, ALU.mult, ALU.add))
            step(dve.tensor_copy(ki[:, :, :], kf[:, :, :]))
            step(dve.tensor_copy(kf[:, :, :], ki[:, :, :]))
            step(dve.scalar_tensor_tensor(r, kf[:, :, :], -c1, ang[:, :, :], ALU.mult, ALU.add))
            step(dve.scalar_tensor_tensor(r, kf[:, :, :], -c2, r, ALU.mult, ALU.add))
            step(dve.scalar_tensor_tensor(r, kf[:, :, :], -c3, r, ALU.mult, ALU.add))
            step(dve.tensor_scalar(r, r, turn * two_pi, None, ALU.add))
            for op, whole in ((ALU.is_gt, -1), (ALU.is_lt, 1)):
                step(dve.tensor_scalar(kf[:, :, :], r, -whole * math.pi, whole * two_pi, op, ALU.mult))
                step(dve.tensor_tensor(r, r, kf[:, :, :], ALU.add))
            dve.tensor_scalar(r, r, 3.1415925, -3.1415925, ALU.min, ALU.max).then_inc(self.r_ready, 1)

    def sines(self, act):
        act.wait_ge(self.r_ready, 2)
        act.activation(self.t[:, :, :, :], self.r[:, :, :, :], ACT.Sin).then_inc(self.t_ready, 1)

    def store(self, sp):
        sp.wait_ge(self.t_ready, 1)
        sp.dma_start(self.tabs, self.t[:, :, :, :]).then_inc(self.t_stored, 16)
        sp.wait_ge(self.t_stored, 16)


class Modulation:

    def __init__(self, ph, c, ada_w, ada_b, norm_w, mods):
        assert KC == HEADS
        self.c, self.ada_w, self.ada_b, self.norm_w, self.mods = c, ada_w, ada_b, norm_w, mods
        self.cs, self.ck = ph.sb("c", [P, KC]), ph.sb("ck", [P, 2])
        self.w = ph.sb("ada", [P, 2, 3 * D])
        self.acc = ph.sb("ada_sum", [P, 2, 3 * D])
        self.nw = ph.sb("nw", [P, 2, D])
        self.rows = ph.sb("mod_rows", [P, 2, 3, D])
        self.ones = ph.sb("ones", [P, P])
        self.w_in = [ph.sem(f"ada_in{l}") for l in range(2)]
        self.c_in, self.b_in, self.nw_in, self.cleared, self.c_act, self.taken, self.scaled, self.step, self.m_ready, self.m_done, self.m_stored = (
            ph.sem(n) for n in ("c_in", "b_in", "nw_in", "cleared", "c_act", "ada_taken", "ada_scaled", "ada_step", "mod_ready", "mod_done", "mod_stored"))

    def load_small(self, nc, sp):
        with nc.allow_non_contiguous_dma(reason="one column of c"):
            sp.dma_start(self.cs[:, :], self.c.rearrange("o (k p) -> p (o k)", p=P)).then_inc(self.c_in, 16)
        for l in range(2):
            sp.dma_start(self.nw[:, l, :], self.norm_w[l:l + 1, :].partition_broadcast(P)).then_inc(self.nw_in, 16)
        sp.wait_ge(self.cleared, 2)
        sp.dma_start(self.acc[0:1, :, :], self.ada_b.rearrange("(o l) n -> o l n", o=1)).then_inc(self.b_in, 16)

    def load(self, sp, h):
        for l in range(2):
            sp.wait_ge(self.step, 2 * h + l + 1)
            settle(sp)
            sp.dma_start(self.w[:, l, :], rows(self.ada_w[l], h)).then_inc(self.w_in[l], 16)

    def silu(self, act):
        act.wait_ge(self.c_in, 16)
        act.activation(self.cs[:, :], self.cs[:, :], ACT.Silu).then_inc(self.c_act, 1)

    def clear(self, pool):
        pool.memset(self.acc[:, :, :], 0.0).then_inc(self.cleared, 1)
        pool.memset(self.ones[:, :], 1.0).then_inc(self.cleared, 1)
        pool.sem_inc(self.step, 2)
        pool.wait_ge(self.b_in, 16)
        pool.wait_ge(self.c_act, 1)

    def add(self, pool, h, l):
        pool.tensor_copy(self.ck[:, l:l + 1], self.cs[:, bass.ds(h, 1)] if not isinstance(h, int) else self.cs[:, h:h + 1]).then_inc(self.taken, 1)
        pool.wait_ge(self.taken, 2 * h + l + 1)
        pool.wait_ge(self.w_in[l], 16 * h + 16)
        pool.wait_ge(self.step, 2 * h + l + 1)
        settle(pool)
        pool.tensor_scalar(self.w[:, l, :], self.w[:, l, :], self.ck[:, l:l + 1], None, ALU.mult).then_inc(self.scaled, 1)
        pool.wait_ge(self.scaled, 2 * h + l + 1)
        pool.tensor_tensor(self.acc[:, l, :], self.acc[:, l, :], self.w[:, l, :], ALU.add).then_inc(self.step, 1)

    def total(self, nc, pe, banks):
        pe.wait_ge(self.step, 2 * HEADS + 2)
        pe.wait_ge(self.cleared, 2)
        for l in range(2):
            for n in range(NCHUNK):
                g = NCHUNK * l + n
                if g >= len(banks):
                    pe.wait_ge(self.m_done, g - len(banks) + 1)
                nc.tensor.matmul(banks[g % len(banks)], self.ones[:, :], self.acc[:, l, n * HALF:(n + 1) * HALF],
                                 start=True, stop=True).then_inc(self.m_ready, 1)

    def put(self, dve, banks):
        dve.wait_ge(self.nw_in, 32)
        for l in range(2):
            for n in range(NCHUNK):
                g = NCHUNK * l + n
                part, s = n // 2, slice(n % 2 * HALF, (n % 2 + 1) * HALF)
                dve.wait_ge(self.m_ready, g + 1)
                src = banks[g % len(banks)]
                if part == 1:
                    dve.scalar_tensor_tensor(self.rows[:, l, 0, s], src, 1.0, self.nw[:, l, s], ALU.add, ALU.mult).then_inc(self.m_done, 1)
                else:
                    dve.tensor_copy(self.rows[:, l, 1 if part == 0 else 2, s], src).then_inc(self.m_done, 1)

    def store(self, sp):
        sp.wait_ge(self.m_done, 2 * NCHUNK)
        sp.dma_start(self.mods.rearrange("(o l) a n -> o l a n", o=1), self.rows[0:1, :, :, :]).then_inc(self.m_stored, 16)
        sp.wait_ge(self.m_stored, 16)


def part_hi(act, hi, src):
    return act.copy(hi, src)


def part_lo(dve, lo, src, hi):
    return dve.tensor_tensor(lo, src, hi.bitcast(F32), ALU.subtract)


def split_turn(t):
    return [] if t == 0 else [t - 1] if t < TILES - 1 else [t - 1, t]


class SplitRows:

    def __init__(self, ph, src, raw):
        self.src, self.raw = src, raw
        self.hi, self.lo = ph.sb("w_hi", [P, KC, D], F32R), ph.sb("w_lo", [P, KC, D], F32R)
        self.raw_in = [ph.sem(f"raw_in{u}") for u in range(len(raw))]
        self.hi_ready, self.lo_ready = ph.sem("w_hi_ready"), ph.sem("w_lo_ready")

    def load(self, sp):
        n = len(self.raw)
        for k in range(KC):
            if k >= n:
                sp.wait_ge(self.lo_ready, k - n + 1)
            sp.dma_start(self.raw[k % n][:, :], self.src[k * P:(k + 1) * P, :]).then_inc(self.raw_in[k % n], 16)

    def split_hi(self, act, ks=range(KC)):
        n = len(self.raw)
        for k in ks:
            act.wait_ge(self.raw_in[k % n], 16 * (k // n) + 16)
            part_hi(act, self.hi[:, k, :], self.raw[k % n][:, :]).then_inc(self.hi_ready, 1)

    def split_lo(self, dve, ks=range(KC)):
        for k in ks:
            dve.wait_ge(self.hi_ready, k + 1)
            part_lo(dve, self.lo[:, k, :], self.raw[k % len(self.raw)][:, :], self.hi[:, k, :]).then_inc(self.lo_ready, 1)

    def wait(self, eng):
        eng.wait_ge(self.lo_ready, KC)

    def columns(self, cols, ks=range(KC)):
        return [[p_[:, k, cols] for k in ks] for p_ in (self.hi, self.lo)]


def split_product(nc, acc, a, b, start=True, stop=True):
    n = len(a[0])
    for k in range(n):
        nc.tensor.matmul(acc, a[0][k], b[0][k], start=(start and k == 0), stop=False)
        nc.tensor.matmul(acc, a[0][k], b[1][k], start=False, stop=False)
        last = nc.tensor.matmul(acc, a[1][k], b[0][k], start=False, stop=(stop and k == n - 1))
    return last


def phase_qkv(nc, K, x, w_qkv, qkv, y=None, positions=None, tabs=None):
    SLOTS = 4
    HH = HALF // HD
    with Phase(nc, "qkv") as ph:
        raw = ph.sb("raw", [P, KC, HALF])
        wh, wl = ph.sb("wh", [P, 2, KC, HALF], F32R), ph.sb("wl", [P, 2, KC, HALF], F32R)
        xh, xl = ph.sb("xh", [P, KC, SEQ], F32R), ph.sb("xl", [P, KC, SEQ], F32R)
        xin = ph.sb("x", [P, 2, D])
        row = ph.sb("row", [P, SLOTS, HALF])
        t1 = ph.sb("t1", [P, 4, HH, ROT // 2])
        zero = ph.sb("zero", [P, D])
        tp = ph.ps("tp", [P, 2, 4, P])
        acc = ph.ps("acc", [P, SLOTS, HALF])
        raw_in, tp_ready, x_hi, x_lo, w_hi, w_lo, acc_ready, acc_done, rope, row_done, zero_set, zeroed = (
            ph.sem(n) for n in ("raw_in", "tp_ready", "x_hi", "x_lo", "w_hi", "w_lo", "acc_ready", "acc_done",
                                "rope", "row_done", "zero_set", "zeroed"))
        x_in = [ph.sem(f"x_in{u}") for u in range(2)]
        stored = [ph.sem(f"stored{u}") for u in range(SLOTS)]
        angles = Angles(ph, K, positions, tabs) if tabs is not None else None

        def each_chunk(eng, body):
            body(0, 0)
            with eng.Fori(0, 2) as p:
                body(2 * p + 1, 1)
                body(2 * p + 2, 0)
            body(NCHUNK - 1, 1)

        def columns(s):
            return (NCHUNK - 1) * HALF if isinstance(s, int) and s == 0 else (s - 1) * HALF

        with nc.Block() as block:
            @block.sync
            def _(sp):
                def load_raw(s, col):
                    if s is not None:
                        sp.wait_ge(w_lo, KC * s + KC)
                        settle(sp)
                    sp.dma_start(raw[:, :, :], w_qkv[:, bass.ds(col, HALF)].rearrange("(k p) n -> p k n", p=P)).then_inc(raw_in, 16)

                def load_x(i):
                    sp.dma_start(xin[:, i % 2, :], rows(x, i)).then_inc(x_in[i % 2], 16)

                load_x(0)
                load_raw(None, columns(0))
                load_x(1)
                if angles:
                    angles.load(nc, sp)
                load_raw(0, columns(1))
                for i in range(2, TILES):
                    sp.wait_ge(tp_ready, 2 * (i - 2) + 2)
                    load_x(i)
                sp.wait_ge(zero_set, 1)
                if y is not None:
                    for b in range(EXPERTS, BLOCKS):
                        sp.dma_start(y[b * P:(b + 1) * P, :], zero[:, :]).then_inc(zeroed, 16)

                def chunk(s, load=True):
                    for t in range(TILES):
                        sp.wait_ge(row_done, TILES * s + t + 1)
                        settle(sp)
                        sp.dma_start(qkv[t * P:(t + 1) * P, bass.ds(columns(s), HALF)], row[:, t % SLOTS, :]).then_inc(stored[t % SLOTS], 16)
                    if load:
                        load_raw(s + 1, columns(s + 2))

                chunk(0)
                with sp.Fori(1, NCHUNK - 2) as s:
                    chunk(s)
                with sp.Fori(NCHUNK - 2, NCHUNK) as s:
                    chunk(s, load=False)
                for u in range(SLOTS):
                    sp.wait_ge(stored[u], 16 * (NCHUNK * TILES // SLOTS + 1))
                if angles:
                    angles.store(sp)
                if y is not None:
                    sp.wait_ge(zeroed, 16 * OVER)

            @block.gpsimd
            def _(pool):
                pool.memset(zero[:, :], 0.0).then_inc(zero_set, 1)

            @block.tensor
            def _(pe):
                def transposes(i):
                    pe.wait_ge(x_in[i % 2], 16 * (i // 2) + 16)
                    for b in range(2):
                        pe.wait_ge(x_lo, 2 * i + b + 1)
                        for k in range(4):
                            last = nc.tensor.transpose(tp[:, b, k, :], xin[:, i % 2, (4 * b + k) * P:(4 * b + k + 1) * P], K["ident"])
                        last.then_inc(tp_ready, 1)

                def chunk(s, u):
                    pe.wait_ge(w_lo, KC * s + KC)
                    for t in range(TILES):
                        if isinstance(s, int) and s == 0:
                            if t + 1 < TILES:
                                transposes(t + 1)
                            pe.wait_ge(x_lo, 2 * t + 4)
                        pe.wait_ge(acc_done, TILES * s + t + 1)
                        cols = slice(t * P, (t + 1) * P)
                        split_product(nc, acc[:, t % SLOTS, :], [[p_[:, k, cols] for k in range(KC)] for p_ in (xh, xl)],
                                      [[p_[:, u, k, :] for k in range(KC)] for p_ in (wh, wl)]).then_inc(acc_ready, 1)

                transposes(0)
                each_chunk(pe, chunk)

            @block.scalar
            def _(act):
                act.sem_inc(acc_done, SLOTS)
                for u in range(SLOTS):
                    act.sem_inc(stored[u], 16)

                def x_his(i):
                    for b in range(2):
                        act.wait_ge(tp_ready, 2 * i + b + 1)
                        part_hi(act, xh[:, 4 * b:4 * b + 4, i * P:(i + 1) * P], tp[:, b, :, :]).then_inc(x_hi, 1)

                def w_his(s, u, k):
                    act.wait_ge(raw_in, 16 * s + 16)
                    part_hi(act, wh[:, u, k, :], raw[:, k, :]).then_inc(w_hi, 1)

                def chunk(s, u):
                    first = isinstance(s, int) and s == 0
                    for t in range(TILES):
                        if first and t + 1 < TILES:
                            x_his(t + 1)
                        act.wait_ge(acc_ready, TILES * s + t + 1)
                        act.wait_ge(stored[t % SLOTS], 16 * (TILES // SLOTS * s + t // SLOTS) + 16)
                        act.copy(row[:, t % SLOTS, :], acc[:, t % SLOTS, :]).then_inc(acc_done, 1)
                        if not (isinstance(s, int) and s == NCHUNK - 1):
                            w_his(s + 1, 1 - u, t)

                x_his(0)
                for k in range(KC):
                    w_his(0, 0, k)
                each_chunk(act, chunk)
                if angles:
                    angles.sines(act)

            @block.vector
            def _(dve):
                dve.sem_inc(x_lo, 2)
                if angles:
                    angles.reduce(dve)

                def x_los(i):
                    for b in range(2):
                        dve.wait_ge(x_hi, 2 * i + b + 1)
                        part = (slice(None), slice(4 * b, 4 * b + 4), slice(i * P, (i + 1) * P))
                        part_lo(dve, xl[part], tp[:, b, :, :], xh[part]).then_inc(x_lo, 1)

                def w_los(s, u, k):
                    dve.wait_ge(w_hi, KC * s + k + 1)
                    part_lo(dve, wl[:, u, k, :], raw[:, k, :], wh[:, u, k, :]).then_inc(w_lo, 1)

                def chunk(s, u):
                    rotated = not (isinstance(s, int) and s in (0, NCHUNK - 1))
                    for t in range(TILES):
                        if isinstance(s, int) and s == 0 and t + 1 < TILES:
                            x_los(t + 1)
                        dve.wait_ge(acc_done, TILES * s + t + 1 + SLOTS)
                        if rotated:
                            ch = Chain(dve, rope, 5 * (TILES * (s - 1) + t))
                            g = row[:, t % SLOTS, :].rearrange("p (h d) -> p h d", d=HD)
                            r1, r2 = g[:, :, 0:ROT // 2], g[:, :, ROT // 2:ROT]
                            cos, sin = (K[n].rearrange("p (t c) -> p t c", t=TILES)[:, t:t + 1, :].to_broadcast([P, HH, ROT // 2])
                                        for n in ("rcos", "rsin"))
                            if t:
                                ch.wait()
                            ch(dve.tensor_tensor(t1[:, 0], r1, cos, ALU.mult))
                            ch(dve.tensor_tensor(t1[:, 1], r2, sin, ALU.mult))
                            ch(dve.tensor_tensor(t1[:, 2], r1, sin, ALU.mult))
                            ch(dve.tensor_tensor(t1[:, 3], r2, cos, ALU.mult))
                            ch.wait()
                            ch(dve.tensor_tensor(r1, t1[:, 0], t1[:, 1], ALU.subtract))
                            dve.tensor_tensor(r2, t1[:, 2], t1[:, 3], ALU.add).then_inc(row_done, 1)
                            dve.wait_ge(row_done, TILES * s + t + 1)
                        else:
                            dve.sem_inc(row_done, 1)
                        if not (isinstance(s, int) and s == NCHUNK - 1):
                            w_los(s + 1, 1 - u, t)

                x_los(0)
                for k in range(KC):
                    w_los(0, 0, k)
                each_chunk(dve, chunk)


def transpose_banks(n):
    return (n + 3) // 4


def phase_attention(nc, K, name, q, k, v, out, maps, dk, dv, mask, scale, lam_parts=None, sub_g=None, modulation=None):
    dq = maps * dk
    U = TILES * maps
    groups = [transpose_banks(i + 1) for i in range(TILES)]
    QK_AT = (2, 3, 4, 5)
    G = len(QK_AT) + sum(groups)
    QK_LAST = sum(groups[:QK_AT[-1] + 1]) + len(QK_AT)
    PSLOTS = 4
    diff = maps == 2
    NORM_AT = 3

    def score_banks(u):
        if u // maps < TILES // 2:
            return [u % 4], u - 4 if u >= 4 else u // 2 - 2
        return [2 * (u % 2), 2 * (u % 2) + 1], u - 2 if u - 2 >= U // 2 else U // 2 - 4 + 2 * (u % 2) + 1

    def each_head(eng, body):
        body(0, 0, 0, first=True, last=False)
        with eng.Fori(0, HEADS // 2 - 1) as p:
            body(2 * p + 1, 1, p, first=False, last=False)
            body(2 * p + 2, 0, p + 1, first=False, last=False)
        body(HEADS - 1, 1, HEADS // 2 - 1, first=False, last=True)

    with Phase(nc, name) as ph:
        qs, ks, vs = ph.sb("q", [P, TILES, dq]), ph.sb("k", [P, TILES, dq]), ph.sb("v", [P, 2, TILES, dv])
        qT, kT = ph.sb("qT", [dq, 2, SEQ]), ph.sb("kT", [dq, 2, SEQ])
        prob = ph.sb("prob", [P, PSLOTS, maps, SEQ])
        aT = ph.sb("aT", [P, TILES, P])
        o_sb = ph.sb("o", [P, 2, TILES, dv])
        mx, bias, total, inv = (ph.sb(n, [P, U]) for n in ("mx", "bias", "total", "inv"))
        s_ps = ph.ps("s", [P, 2 * SEQ])
        tp = ph.ps("tp", [P, 2, 4, P])
        o_ps = ph.ps("o_ps", [P, 2, HALF])
        qk_in, tp_ready, tp_copied, s_ready, exp_done, bias_ready, a_ready, o_ready, o_done, own = (
            ph.sem(n) for n in ("qk_in", "tp_ready", "tp_copied", "s_ready", "exp_done", "bias_ready",
                                "a_ready", "o_ready", "o_done", "own"))
        v_in, stored = ([ph.sem(f"{n}{b}") for b in range(2)] for n in ("v_in", "stored"))
        m = Modulation(ph, *modulation) if modulation else None
        if diff:
            lq = ph.sb("lq", [P, 4, HD])
            lt = ph.sb("lt", [P, 2, HD])
            ls = ph.sb("ls", [P, 4])
            lam = ph.sb("lam", [P, 1])
            gsub = ph.sb("gsub", [P, dv])
            sq = ph.sb("sq", [P, TILES, dv])
            ms, rstd, half = (ph.sb(n, [P, TILES]) for n in ("ms", "rstd", "half"))
            l_in, l_sum, l_exp, ms_ready, norm_own, pool_own, normed = (
                ph.sem(n) for n in ("l_in", "l_sum", "l_exp", "ms_ready", "norm_own", "pool_own", "normed"))

        def scores_of(u):
            first_bank = score_banks(u)[0][0]
            return s_ps[:, first_bank * HALF:first_bank * HALF + (u // maps + 1) * P]

        banks = [s_ps[:, n * HALF:(n + 1) * HALF] for n in range(4)]
        with nc.Block() as block:
            @block.sync
            def _(sp):
                def load_qk(h):
                    sp.dma_start(qs[:, :, :], q(h)).then_inc(qk_in, 16)
                    sp.dma_start(ks[:, :, :], k(h)).then_inc(qk_in, 16)

                def load_v(h, b):
                    sp.dma_start(vs[:, b, :, :], v(h)).then_inc(v_in[b], 16)

                def store(h, b):
                    if diff:
                        sp.wait_ge(normed, h + 1)
                    else:
                        sp.wait_ge(o_done, TILES * h + TILES + 2)
                    settle(sp)
                    sp.dma_start(out(h), o_sb[:, b, :, :]).then_inc(stored[b], 16)

                if diff:
                    for n, part in enumerate(lam_parts):
                        sp.dma_start(lq[:, n, :], part.partition_broadcast(P)).then_inc(l_in, 16)
                    sp.dma_start(gsub[:, :], sub_g.partition_broadcast(P)).then_inc(l_in, 16)
                load_qk(0)
                load_v(0, 0)
                load_v(1, 1)
                if m:
                    m.load_small(nc, sp)
                    m.load(sp, 0)
                sp.wait_ge(tp_ready, 4)
                load_qk(1)

                def turn(h, b):
                    sp.wait_ge(tp_ready, 4 + G * h + QK_LAST)
                    load_qk(h + 2)
                    if m:
                        m.load(sp, h + 1)
                    sp.wait_ge(o_ready, TILES * h + TILES)
                    load_v(h + 2, b)
                    store(h, b)

                with sp.Fori(0, HEADS // 2 - 1) as p:
                    for b in range(2):
                        turn(2 * p + b, b)
                if m:
                    m.load(sp, HEADS - 1)
                store(HEADS - 2, 0)
                store(HEADS - 1, 1)
                for b in range(2):
                    sp.wait_ge(stored[b], 16 * (HEADS // 2 + 1))
                if m:
                    m.store(sp)

            @block.tensor
            def _(pe):
                def transpose_qk(at, parity, n):
                    src = (qs, ks)[n // 2]
                    bank_group(at, parity, [src[:, 4 * (n % 2) + t, :] for t in range(4)])

                def bank_group(at, parity, pieces):
                    pe.wait_ge(tp_copied, at + 1)
                    for n, piece in enumerate(pieces):
                        last = nc.tensor.transpose(tp[0:piece.shape[-1], parity, n, :], piece, K["ident"])
                    last.then_inc(tp_ready, 1)

                def scores(h, b, i):
                    n = (i + 1) * P
                    for mp in range(maps):
                        u = i * maps + mp
                        pe.wait_ge(exp_done, U * h + score_banks(u)[1] + 3)
                        dst = scores_of(u)
                        for c in range(0, n, HALF):
                            w = min(HALF, n - c)
                            last = nc.tensor.matmul(dst[:, c:c + w], qT[mp * dk:(mp + 1) * dk, b, i * P:(i + 1) * P],
                                                    kT[mp * dk:(mp + 1) * dk, b, c:c + w], start=True, stop=True)
                        last.then_inc(s_ready, 1)

                def head(h, b, turn, first, last):
                    g = 0
                    for i in range(TILES):
                        if diff:
                            pe.wait_ge(a_ready, TILES * h + i + 1)
                        else:
                            pe.wait_ge(exp_done, U * h + i + 3)
                        for j in range(0, i + 1, 4):
                            bank_group(4 + G * h + g, g % 2, [prob[:, i % PSLOTS, 0, t * P:(t + 1) * P] for t in range(j, min(j + 4, i + 1))])
                            g += 1
                        mine = g - groups[i]
                        if i in QK_AT and not last:
                            if i == QK_AT[0]:
                                pe.wait_ge(qk_in, 32 * h + 64)
                            transpose_qk(4 + G * h + g, g % 2, i - QK_AT[0])
                            g += 1
                        if i + 2 < TILES:
                            scores(h, b, i + 2)
                        elif not last:
                            if i + 2 == TILES:
                                pe.wait_ge(tp_copied, 4 + G * h + QK_LAST + 2)
                            scores(h + 1, 1 - b, i + 2 - TILES)
                        if i == 0:
                            pe.wait_ge(v_in[b], 16 * turn + 16)
                        pe.wait_ge(o_done, TILES * h + i + 1)
                        for j in range(i + 1):
                            if j % 4 == 0:
                                pe.wait_ge(tp_copied, 4 + G * h + mine + j // 4 + 3)
                            last_mm = nc.tensor.matmul(o_ps[:, i % 2, 0:dv], aT[:, j, :], vs[:, b, j, :],
                                                       start=(j == 0), stop=(j == i))
                        last_mm.then_inc(o_ready, 1)
                    assert last or g == G

                pe.wait_ge(qk_in, 32)
                for n in range(4):
                    transpose_qk(n, n % 2, n)
                pe.wait_ge(tp_copied, 6)
                scores(0, 0, 0)
                scores(0, 0, 1)
                each_head(pe, head)
                if m:
                    pe.wait_ge(exp_done, U * HEADS + 2)
                    m.total(nc, pe, banks)

            @block.scalar
            def _(act):
                if m:
                    m.silu(act)
                for _ in range(2):
                    act.sem_inc(tp_copied, 1)
                    act.sem_inc(exp_done, 1)
                if diff:
                    act.wait_ge(l_sum, 1)
                    act.activation(ls[:, 2:4], ls[:, 0:2], ACT.Exp).then_inc(l_exp, 1)

                def copy_group(at, parity, dst, n, rows_):
                    act.wait_ge(tp_ready, at + 1)
                    act.copy(dst, tp[0:rows_, parity, 0:n, :]).then_inc(tp_copied, 1)

                def copy_qk(at, parity, b, n):
                    dst = (qT, kT)[n // 2][:, b, n % 2 * HALF:(n % 2 + 1) * HALF]
                    copy_group(at, parity, dst.rearrange("p (n c) -> p n c", n=4), 4, dq)

                def exps(h, i):
                    n = (i + 1) * P
                    for mp in range(maps):
                        u = i * maps + mp
                        act.wait_ge(bias_ready, U * h + u + 1)
                        act.activation(prob[:, i % PSLOTS, mp, 0:n], scores_of(u), ACT.Exp, bias=bias[:, u:u + 1],
                                       scale=scale, accum_out=total[:, u:u + 1]).then_inc(exp_done, 1)

                def head(h, b, turn, first, last):
                    g = 0
                    for i in range(TILES):
                        for j in range(0, i + 1, 4):
                            n = min(4, i + 1 - j)
                            copy_group(4 + G * h + g, g % 2, aT[:, j:j + n, :], n, P)
                            g += 1
                        if i in QK_AT and not last:
                            copy_qk(4 + G * h + g, g % 2, 1 - b, i - QK_AT[0])
                            g += 1
                        if i + 2 < TILES:
                            exps(h, i + 2)
                        elif not last:
                            exps(h + 1, i + 2 - TILES)

                for n in range(4):
                    copy_qk(n, n % 2, 0, n)
                exps(0, 0)
                exps(0, 1)
                each_head(act, head)

            @block.vector
            def _(dve):
                dve.sem_inc(o_done, 2)
                for b in range(2):
                    dve.sem_inc(stored[b], 16)
                ch = Chain(dve, own)
                if diff:
                    dve.wait_ge(l_in, 16 * 5)
                    ch(dve.tensor_tensor(lt[:, 0], lq[:, 0], lq[:, 1], ALU.mult))
                    ch(dve.tensor_tensor(lt[:, 1], lq[:, 2], lq[:, 3], ALU.mult))
                    ch(dve.tensor_scalar(gsub[:, :], gsub[:, :], 1.0 - LAMBDA_INIT, None, ALU.mult))
                    ch.wait()
                    dve.reduce_sum(ls[:, 0:2], lt[:, :, :], axis=AX.X).then_inc(l_sum, 1)
                    dve.wait_ge(l_exp, 1)
                    ch(dve.tensor_tensor(lam[:, :], ls[:, 2:3], ls[:, 3:4], ALU.subtract))
                    ch.wait()
                    ch(dve.tensor_scalar(lam[:, :], lam[:, :], LAMBDA_INIT, None, ALU.add))
                    ch.wait()

                def biases(ch, h, i):
                    n = (i + 1) * P
                    for mp in range(maps):
                        u = i * maps + mp
                        s = scores_of(u)
                        dve.wait_ge(s_ready, U * h + u + 1)
                        ch(dve.tensor_tensor(s[:, n - P:n], s[:, n - P:n], mask, ALU.add))
                        ch.wait()
                        ch(dve.reduce_max(mx[:, u:u + 1], s[:, 0:n], axis=AX.X))
                        ch.wait()
                        dve.tensor_scalar(bias[:, u:u + 1], mx[:, u:u + 1], -scale, None, ALU.mult).then_inc(bias_ready, 1)

                def combine(ch, h, i):
                    n = (i + 1) * P
                    u = i * maps
                    dve.wait_ge(exp_done, U * h + u + maps + 2)
                    ch(dve.reciprocal(inv[:, u:u + maps], total[:, u:u + maps]))
                    if diff:
                        p0, p1 = (prob[:, i % PSLOTS, mp, 0:n] for mp in range(2))
                        ch.wait()
                        ch(dve.tensor_tensor(inv[:, u + 1:u + 2], inv[:, u + 1:u + 2], lam[:, :], ALU.mult))
                        ch.wait()
                        ch(dve.tensor_scalar(p1, p1, inv[:, u + 1:u + 2], None, ALU.mult))
                        ch.wait()
                        dve.scalar_tensor_tensor(p0, p0, inv[:, u:u + 1], p1, ALU.mult, ALU.subtract).then_inc(a_ready, 1)

                def evacuate(ch, h, b, turn, i):
                    dve.wait_ge(o_ready, TILES * h + i + 1)
                    if i == 0:
                        dve.wait_ge(stored[b], 16 * turn + 16)
                    if diff:
                        dve.tensor_copy(o_sb[:, b, i, :], o_ps[:, i % 2, 0:dv]).then_inc(o_done, 1)
                    else:
                        ch.wait()
                        dve.tensor_scalar(o_sb[:, b, i, :], o_ps[:, i % 2, 0:dv], inv[:, i:i + 1], None,
                                          ALU.mult).then_inc(o_done, 1)

                def norm(h, b):
                    ch = Chain(dve, norm_own, 2 * h)
                    dve.wait_ge(o_done, TILES * h + TILES + 2)
                    ch(dve.tensor_tensor(sq[:, :, :], o_sb[:, b, :, :], o_sb[:, b, :, :], ALU.mult))
                    ch.wait()
                    if not (isinstance(h, int) and h == 0):
                        dve.wait_ge(normed, h)
                    ch(dve.reduce_sum(ms[:, :], sq[:, :, :], axis=AX.X))
                    ch.wait()
                    dve.tensor_scalar(ms[:, :], ms[:, :], 1.0 / dv, LN_EPS, ALU.mult, ALU.add).then_inc(ms_ready, 1)

                biases(ch, 0, 0)
                biases(ch, 0, 1)
                combine(ch, 0, 0)
                before = ch.n
                per_head = 2 * U + (3 * TILES if diff else TILES)

                def head(h, b, turn, first, last):
                    ch = Chain(dve, own, per_head * h + before)
                    for i in range(TILES):
                        if i + 1 < TILES:
                            combine(ch, h, i + 1)
                        elif not last:
                            combine(ch, h + 1, 0)
                        if i + 2 < TILES:
                            biases(ch, h, i + 2)
                        elif not last:
                            biases(ch, h + 1, i + 2 - TILES)
                        if i > 0:
                            evacuate(ch, h, b, turn, i - 1)
                        elif not first:
                            evacuate(ch, h - 1, 1 - b, None, TILES - 1)
                        if diff and i == NORM_AT and not first:
                            norm(h - 1, 1 - b)
                    assert last or ch.n == per_head
                    if last:
                        evacuate(ch, h, b, turn, TILES - 1)
                        if diff:
                            norm(h, b)

                each_head(dve, head)
                if m:
                    m.put(dve, banks)

            if diff:
                @block.gpsimd
                def _(pool):
                    pool.memset(half[:, :], -0.5).then_inc(pool_own, 1)
                    pool.wait_ge(pool_own, 1)
                    if m:
                        m.clear(pool)

                    def head(h, b, turn, first, last):
                        if m:
                            for l in range(2):
                                m.add(pool, h, l)
                        ch = Chain(pool, pool_own, 2 * h + 1)
                        pool.wait_ge(ms_ready, h + 1)
                        ch(pool.tensor_tensor(rstd[:, :], ms[:, :], half[:, :], ALU.pow))
                        ch.wait()
                        o = o_sb[:, b, :, :]
                        ch(pool.tensor_tensor(o, o, rstd[:, :].unsqueeze(2).to_broadcast([P, TILES, dv]), ALU.mult))
                        ch.wait()
                        pool.tensor_tensor(o, o, gsub[:, :].unsqueeze(1).to_broadcast([P, TILES, dv]), ALU.mult).then_inc(normed, 1)

                    each_head(pool, head)


def with_constants(nc, stack, consts, body):
    parts = constant_parts()
    width = sum(a.shape[1] for a in parts.values())
    held = stack.enter_context(nc.sbuf_tensor("constants", [P, width], F32))
    K, at = {}, 0
    for name, a in parts.items():
        K[name] = held[:, at:at + a.shape[1]]
        at += a.shape[1]
    SETTLED.append(nc.alloc_semaphore("settled"))
    with Phase(nc, "load") as ph:
        loaded = ph.sem("loaded")
        with nc.Block() as block:
            @block.sync
            def _(sp):
                sp.dma_start(held[:, :], consts).then_inc(loaded, 16)
                sp.wait_ge(loaded, 16)
    body(K)


def diff_attention(nc, K, qkv, lam_parts, sub_g, mix, modulation=None):
    def heads(base, width, ap=None):
        return lambda h: (ap if ap is not None else qkv)[:, bass.ds(h * width + base, width)].rearrange("(t p) c -> p t c", p=P)

    phase_attention(nc, K, "diff", heads(0, VD), heads(D, VD), heads(2 * D, VD), heads(0, VD, mix), 2, HD, VD,
                    K["causal"], HD ** -0.5, lam_parts, sub_g, modulation)


def affine(dve, ch, r, mv, gb, rstd, rstd_ready, i, out, h_ready):
    ch(dve.scalar_tensor_tensor(out[:, :], r[:, :], mv[:, 0:1], gb[:, 0, :], ALU.subtract, ALU.mult))
    ch.wait()
    dve.wait_ge(rstd_ready, i + 2)
    dve.scalar_tensor_tensor(out[:, :], out[:, :], rstd[:, 0:1], gb[:, 1, :], ALU.mult, ALU.add).then_inc(h_ready, 1)


def layer_norm_steps(dve, ch, r, stats, mv, ms_ready):
    for c in range(2):
        ch(dve.bn_stats(stats[:, c, :], r[:, c * HALF:(c + 1) * HALF]))
    ch.wait()
    settle(dve)
    ch(dve.bn_aggr(mv[:, :], stats[:, :, :]))
    ch.wait()
    dve.tensor_scalar(mv[:, 1:2], mv[:, 1:2], LN_EPS, None, ALU.add).then_inc(ms_ready, 1)


def phase_out_norm(nc, K, name, mix, w_out, h_in, g, b, w_gr, b_gr, w_er, b_er, h_out, logits, weights=None):
    NL = GROUPS + EXPERTS
    with Phase(nc, name) as ph:
        wr = ph.sb("wr", [P, KC, NL])
        br = ph.sb("br", [P, NL])
        gb = ph.sb("gb", [P, 2, D])
        xin, res, r, hn = (ph.sb(n, [P, D]) for n in ("x", "res", "r", "hn"))
        w = SplitRows(ph, w_out, [r, hn, res])
        xh, xl = ph.sb("xh", [P, KC, P], F32R), ph.sb("xl", [P, KC, P], F32R)
        hT = ph.sb("hT", [P, KC, P])
        stats, mv = ph.sb("stats", [P, 2, 6]), ph.sb("mv", [P, 2])
        rstd, half = ph.sb("rstd", [P, 1]), ph.sb("half", [P, 1])
        tp = ph.ps("tp", [P, 2, 4, P])
        acc = ph.ps("acc", [P, 2, HALF])
        lg = ph.ps("lg", [P, 1, HALF])
        small_in, x_in, res_in, tp_ready, x_hi, x_lo, hT_ready, acc_ready, r_ready = (ph.sem(n) for n in (
            "small_in", "x_in", "res_in", "tp_ready", "x_hi", "x_lo", "hT_ready", "acc_ready", "r_ready"))
        ms_ready, rstd_ready, h_ready, lg_ready, lg_done, stored, own = (ph.sem(n) for n in (
            "ms_ready", "rstd_ready", "h_ready", "lg_ready", "lg_done", "stored", "own"))

        with nc.Block() as block:
            @block.sync
            def _(sp):
                sp.dma_start(xin[:, :], mix[0:P, :]).then_inc(x_in, 16)
                w.load(sp)
                w.wait(sp)
                sp.dma_start(res[:, :], h_in[0:P, :]).then_inc(res_in, 16)
                for n, row in enumerate((g, b)):
                    sp.dma_start(gb[:, n, :], row.partition_broadcast(P)).then_inc(small_in, 16)
                sp.dma_start(wr[:, :, 0:GROUPS], w_gr.rearrange("(k p) n -> p k n", p=P)).then_inc(small_in, 16)
                sp.dma_start(wr[:, :, GROUPS:NL], w_er.rearrange("(k p) n -> p k n", p=P)).then_inc(small_in, 16)
                sp.dma_start(br[:, 0:GROUPS], b_gr.partition_broadcast(P)).then_inc(small_in, 16)
                sp.dma_start(br[:, GROUPS:NL], b_er.partition_broadcast(P)).then_inc(small_in, 16)

                def turn(i, transposed):
                    sp.wait_ge(tp_ready, transposed)
                    sp.dma_start(xin[:, :], rows(mix, i + 1)).then_inc(x_in, 16)
                    sp.wait_ge(r_ready, 2 * i + 4)
                    sp.dma_start(res[:, :], rows(h_in, i + 1)).then_inc(res_in, 16)
                    sp.wait_ge(h_ready, i + 1)
                    sp.dma_start(rows(h_out, i), hn[:, :]).then_inc(stored, 16)

                turn(0, 2)
                with sp.Fori(1, TILES - 1) as i:
                    turn(i, 4 * i)
                if weights is not None:
                    for part in range(3):
                        weights.load_first(sp, part)
                sp.wait_ge(h_ready, TILES)
                sp.dma_start(rows(h_out, TILES - 1), hn[:, :]).then_inc(stored, 16)
                sp.wait_ge(stored, 16 * (TILES + 1))

            @block.tensor
            def _(pe):
                def transpose_x(i):
                    pe.wait_ge(x_in, 16 * i + 16)
                    for bnk in range(2):
                        if not (isinstance(i, int) and i < 2):
                            pe.wait_ge(hT_ready, 2 * (i - 2) + bnk + 1)
                        elif i == 1:
                            pe.wait_ge(x_lo, bnk + 1)
                        for k in range(4):
                            last = nc.tensor.transpose(tp[:, bnk, k, :], xin[:, (4 * bnk + k) * P:(4 * bnk + k + 1) * P], K["ident"])
                        last.then_inc(tp_ready, 1)

                def transpose_h(i):
                    pe.wait_ge(h_ready, i + 1)
                    for bnk in range(2):
                        if isinstance(i, int) and i == TILES - 1:
                            pe.wait_ge(hT_ready, 2 * i + bnk - 1)
                        for k in range(4):
                            last = nc.tensor.transpose(tp[:, bnk, k, :], hn[:, (4 * bnk + k) * P:(4 * bnk + k + 1) * P], K["ident"])
                        last.then_inc(tp_ready, 1)

                def product(i, c):
                    pe.wait_ge(r_ready, 2 * i + c + 1)
                    split_product(nc, acc[:, c, :], [[p_[:, k, :] for k in range(KC)] for p_ in (xh, xl)],
                                  w.columns(slice(c * HALF, (c + 1) * HALF))).then_inc(acc_ready, 1)

                def route(i):
                    pe.wait_ge(hT_ready, 2 * i + 2)
                    pe.wait_ge(lg_done, i + 1)
                    for k in range(KC):
                        last = nc.tensor.matmul(lg[:, 0, 0:NL], hT[:, k, :], wr[:, k, :], start=(k == 0), stop=(k == KC - 1))
                    last.then_inc(lg_ready, 1)

                def tile(i, last=False):
                    pe.wait_ge(x_lo, 2 * i + 2)
                    product(i, 0)
                    transpose_h(i - 1)
                    product(i, 1)
                    if not last:
                        transpose_x(i + 1)
                    route(i - 1)

                transpose_x(0)
                w.wait(pe)
                pe.wait_ge(x_lo, 2)
                product(0, 0)
                product(0, 1)
                transpose_x(1)
                pe.wait_ge(small_in, 16 * 6)
                with pe.Fori(1, TILES - 1) as i:
                    tile(i)
                tile(TILES - 1, last=True)
                transpose_h(TILES - 1)
                route(TILES - 1)

            @block.scalar
            def _(act):
                def x_his(i, n):
                    for bnk in range(2):
                        act.wait_ge(tp_ready, 2 * n + bnk + 1)
                        part_hi(act, xh[:, 4 * bnk:4 * bnk + 4, :], tp[:, bnk, :, :]).then_inc(x_hi, 1)

                def h_copies(n):
                    for bnk in range(2):
                        act.wait_ge(tp_ready, 2 * n + bnk + 1)
                        act.copy(hT[:, 4 * bnk:4 * bnk + 4, :], tp[:, bnk, :, :]).then_inc(hT_ready, 1)

                x_his(0, 0)
                w.split_hi(act)
                x_his(1, 1)
                with act.Fori(1, TILES - 1) as i:
                    h_copies(2 * i)
                    x_his(i + 1, 2 * i + 1)
                h_copies(2 * TILES - 2)
                h_copies(2 * TILES - 1)

            @block.vector
            def _(dve):
                dve.sem_inc(r_ready, 1)
                dve.sem_inc(r_ready, 1)
                dve.sem_inc(lg_done, 1)
                dve.sem_inc(stored, 16)

                def x_los(i):
                    for bnk in range(2):
                        dve.wait_ge(x_hi, 2 * i + bnk + 1)
                        part_lo(dve, xl[:, 4 * bnk:4 * bnk + 4, :], tp[:, bnk, :, :], xh[:, 4 * bnk:4 * bnk + 4, :]).then_inc(x_lo, 1)

                def norm(i, ch, last=False):
                    dve.wait_ge(res_in, 16 * i + 16)
                    for c in range(2):
                        s = slice(c * HALF, (c + 1) * HALF)
                        dve.wait_ge(acc_ready, 2 * i + c + 1)
                        dve.scalar_tensor_tensor(r[:, s], res[:, s], ALPHA, acc[:, c, :], ALU.mult, ALU.add).then_inc(r_ready, 1)
                    if not last:
                        x_los(i + 1)
                    dve.wait_ge(r_ready, 2 * i + 4)
                    layer_norm_steps(dve, ch, r, stats, mv, ms_ready)
                    dve.wait_ge(stored, 16 * i + 16)
                    if not (isinstance(i, int) and i == 0):
                        dve.wait_ge(tp_ready, 4 * i + 2)
                    affine(dve, ch, r, mv, gb, rstd, rstd_ready, i, hn, h_ready)

                def put_logits(i):
                    dve.wait_ge(lg_ready, i + 1)
                    dve.tensor_tensor(logits[:, bass.ds(i, 1), :], lg[:, 0:1, 0:NL], br[:, :].unsqueeze(1), ALU.add).then_inc(lg_done, 1)

                x_los(0)
                w.split_lo(dve)
                dve.wait_ge(small_in, 16 * 6)
                norm(0, Chain(dve, own))
                with dve.Fori(1, TILES - 1) as i:
                    norm(i, Chain(dve, own, 4 * i))
                    put_logits(i - 1)
                norm(TILES - 1, Chain(dve, own, 4 * (TILES - 1)), last=True)
                put_logits(TILES - 2)
                put_logits(TILES - 1)

            @block.gpsimd
            def _(pool):
                pool.memset(half[:, :], -0.5).then_inc(rstd_ready, 1)
                pool.wait_ge(rstd_ready, 1)
                with pool.Fori(0, TILES) as i:
                    pool.wait_ge(ms_ready, i + 1)
                    pool.tensor_tensor(rstd[:, :], mv[:, 1:2], half[:, :], ALU.pow).then_inc(rstd_ready, 1)


def phase_route(nc, K, name, logits, gates, dest_i, tok_i, blk_i, pairs_i):
    T = TILES
    NL = GROUPS + EXPERTS
    with Phase(nc, name) as ph:
        def t3(n, w=EXPERTS):
            return ph.sb(n, [P, T, w])

        def t2(n, w=T):
            return ph.sb(n, [P, w])

        gmax, gsum, v1, v2, ex, w1, w2 = (t2(n) for n in ("gmax", "gsum", "v1", "v2", "ex", "w1", "w2"))
        ge, G4, rank4 = t3("ge", GROUPS), t3("G4", GROUPS), t3("rank4", GROUPS)
        em, em2, M1, M2, M, S, R, Q, q1, Dst, tmp = (t3(n) for n in (
            "em", "em2", "M1", "M2", "M", "S", "R", "Q", "q1", "Dst", "tmp"))
        S8 = t2("S8", EXPERTS)
        ones = ph.sb("ones", [P, P])
        cnt, nov, cum, ob, obe, zero = (t2(n, EXPERTS) for n in ("cnt", "nov", "cum", "ob", "obe", "zero"))
        d1, d2, s1, s2, b1, b2 = (t2(n) for n in ("d1", "d2", "s1", "s2", "b1", "b2"))
        A = ph.sb("A", [P, T, 2, P])
        B = ph.sb("B", [P, T, 2, BCOLS])
        over = ph.sb("over", [P, OVER + 2, EXPERTS])
        over2 = ph.sb("over2", [P, OVER + 2, EXPERTS])
        bexp = ph.sb("bexp", [P, BCOLS])
        tot = ph.sb("tot", [P, 2])
        evens = ph.sb("evens", [P, 8])
        pr = ph.ps("pr_ps", [P, T, EXPERTS])
        pc = ph.ps("pc", [P, EXPERTS])
        pt = ph.ps("pt", [P, BCOLS])
        own, m_ready, ranked, exp_in, exp_out, ab_ready, tok_ready = (ph.sem(n) for n in (
            "own", "m_ready", "ranked", "exp_in", "exp_out", "ab_ready", "tok_ready"))
        with nc.Block() as block:
            @block.scalar
            def _(act):
                act.wait_ge(exp_in, 1)
                act.activation(ge[:, :, :], ge[:, :, :], ACT.Exp).then_inc(exp_out, 1)
                act.wait_ge(exp_in, 2)
                act.activation(ex[:, :], ex[:, :], ACT.Exp).then_inc(exp_out, 1)

            @block.tensor
            def _(pe):
                pe.wait_ge(m_ready, 1)
                nc.tensor.matmul(pr[:, :, :], K["before"], M[:, :, :], start=True, stop=False)
                nc.tensor.matmul(pr[:, :, :], ones[:, :], S[:, :, :], start=False, stop=True)
                nc.tensor.matmul(pc[:, :], ones[:, :], S8[:, :], start=True, stop=True).then_inc(ranked, 1)
                pe.wait_ge(ab_ready, 1)
                for t in range(T):
                    for c in range(2):
                        last = nc.tensor.matmul(pt[:, :], A[:, t, c, :], B[:, t, c, :], start=(t + c == 0),
                                                stop=(t == T - 1 and c == 1))
                last.then_inc(tok_ready, 1)

            @block.vector
            def _(dve):
                ch = Chain(dve, own)

                def step(ins):
                    ch(ins)
                    ch.wait()

                def tt(o, a, b, op):
                    step(dve.tensor_tensor(o, a, b, op))

                def ts(o, a, x, op, y=None, op2=None):
                    step(dve.tensor_scalar(o, a, x, y, op, *([op2] if op2 is not None else [])))

                def wide(a, w):
                    return a.unsqueeze(2).to_broadcast([P, T, w])

                def first_max(out, src, top, w, work, rev):
                    tt(work, src, wide(top, w), ALU.is_equal)
                    tt(work, work, rev, ALU.mult)
                    step(dve.reduce_max(w1[:, :], work, axis=AX.X))
                    tt(out, work, wide(w1[:, :], w), ALU.is_equal)

                step(dve.memset(ones[:, :], 1.0))
                step(dve.memset(zero[:, :], 0.0))
                rev = tmp[:, :, :]
                revs = ph.sb("revs", [P, EXPERTS])
                ts(revs[:, :], K["iota"][:, 0:EXPERTS], -1.0, ALU.mult, float(EXPERTS), ALU.add)
                revx = revs[:, :].unsqueeze(1).to_broadcast([P, T, EXPERTS])
                revg = revs[:, 0:GROUPS].unsqueeze(1).to_broadcast([P, T, GROUPS])
                gl, el = logits[:, :, 0:GROUPS], logits[:, :, GROUPS:NL]
                step(dve.reduce_max(gmax[:, :], gl, axis=AX.X))
                first_max(G4[:, :, :], gl, gmax[:, :], GROUPS, rank4[:, :, :], revg)
                dve.tensor_tensor(ge[:, :, :], gl, wide(gmax[:, :], GROUPS), ALU.subtract).then_inc(exp_in, 1)
                gx = G4[:, :, :].unsqueeze(3).to_broadcast([P, T, GROUPS, PER_GROUP])
                e4 = em[:, :, :].rearrange("p t (g e) -> p t g e", g=GROUPS)
                q4 = q1[:, :, :].rearrange("p t (g e) -> p t g e", g=GROUPS)
                for t in range(T):
                    step(dve.tensor_copy(q4[:, t], gx[:, t]))
                tt(em[:, :, :], el, q1[:, :, :], ALU.mult)
                ts(q1[:, :, :], q1[:, :, :], -NEG, ALU.mult, NEG, ALU.add)
                tt(em[:, :, :], em[:, :, :], q1[:, :, :], ALU.add)
                step(dve.reduce_max(v1[:, :], em[:, :, :], axis=AX.X))
                first_max(M1[:, :, :], em[:, :, :], v1[:, :], EXPERTS, tmp[:, :, :], revx)
                step(dve.scalar_tensor_tensor(em2[:, :, :], M1[:, :, :], 3 * NEG, em[:, :, :], ALU.mult, ALU.add))
                step(dve.reduce_max(v2[:, :], em2[:, :, :], axis=AX.X))
                first_max(M2[:, :, :], em2[:, :, :], v2[:, :], EXPERTS, tmp[:, :, :], revx)
                dve.tensor_tensor(ex[:, :], v2[:, :], v1[:, :], ALU.subtract).then_inc(exp_in, 1)
                tt(M[:, :, :], M1[:, :, :], M2[:, :, :], ALU.add)
                step(dve.tensor_copy(S[:, 0, :], zero[:, :]))
                for t in range(1, T):
                    tt(S[:, t, :], S[:, t - 1, :], M[:, t - 1, :], ALU.add)
                dve.tensor_tensor(S8[:, :], S[:, T - 1, :], M[:, T - 1, :], ALU.add).then_inc(m_ready, 1)
                dve.wait_ge(exp_out, 2)
                step(dve.reduce_sum(gsum[:, :], ge[:, :, :], axis=AX.X))
                ts(w1[:, :], ex[:, :], 1.0, ALU.add)
                tt(w1[:, :], w1[:, :], gsum[:, :], ALU.mult)
                step(dve.reciprocal(gates[:, 0, :], w1[:, :]))
                tt(gates[:, 1, :], gates[:, 0, :], ex[:, :], ALU.mult)
                dve.wait_ge(ranked, 1)
                step(dve.tensor_copy(R[:, :, :], pr[:, :, :]))
                step(dve.tensor_copy(cnt[:, :], pc[:, :]))
                ts(Q[:, :, :], R[:, :, :], float(P), ALU.is_ge)
                ts(nov[:, :], cnt[:, :], float(P), ALU.is_gt)
                for m in range(2, T):
                    step(dve.scalar_tensor_tensor(Q[:, :, :], R[:, :, :], float(m * P), Q[:, :, :], ALU.is_ge, ALU.add))
                    step(dve.scalar_tensor_tensor(nov[:, :], cnt[:, :], float(m * P), nov[:, :], ALU.is_gt, ALU.add))
                step(dve.tensor_tensor_scan(cum[:, :], nov[:, :], zero[:, :], 0.0, ALU.add, ALU.add))
                tt(ob[:, :], cum[:, :], nov[:, :], ALU.subtract)
                step(dve.tensor_copy(tot[:, 0:1], cum[:, EXPERTS - 1:EXPERTS]))
                ts(obe[:, :], ob[:, :], float(EXPERTS - 1), ALU.add)
                tt(obe[:, :], obe[:, :], K["iota"][:, 0:EXPERTS], ALU.subtract)
                ts(q1[:, :, :], Q[:, :, :], 1.0, ALU.min)
                tt(tmp[:, :, :], q1[:, :, :], obe[:, :].unsqueeze(1).to_broadcast([P, T, EXPERTS]), ALU.mult)
                tt(tmp[:, :, :], tmp[:, :, :], Q[:, :, :], ALU.add)
                tt(tmp[:, :, :], tmp[:, :, :], K["iota"][:, 0:EXPERTS].unsqueeze(1).to_broadcast([P, T, EXPERTS]), ALU.add)
                step(dve.scalar_tensor_tensor(R[:, :, :], Q[:, :, :], -float(P), R[:, :, :], ALU.mult, ALU.add))
                for Mk, s, b in ((M1, s1, b1), (M2, s2, b2)):
                    tt(S[:, :, :], Mk[:, :, :], R[:, :, :], ALU.mult)
                    step(dve.reduce_sum(s[:, :], S[:, :, :], axis=AX.X))
                    tt(S[:, :, :], Mk[:, :, :], tmp[:, :, :], ALU.mult)
                    step(dve.reduce_sum(b[:, :], S[:, :, :], axis=AX.X))
                for n, (s, b, d) in enumerate(((s1, b1, d1), (s2, b2, d2))):
                    step(dve.scalar_tensor_tensor(d[:, :], b[:, :], float(P), s[:, :], ALU.mult, ALU.add))
                    step(dve.tensor_copy(dest_i[:, n, :], d[:, :]))
                for t in range(T):
                    for c, (s, b) in enumerate(((s1, b1), (s2, b2))):
                        ch(dve.tensor_scalar(A[:, t, c, :], K["iota"], s[:, t:t + 1], None, ALU.is_equal))
                        ch(dve.tensor_scalar(B[:, t, c, :], K["iota"][:, 0:BCOLS], b[:, t:t + 1], K["token"][:, t:t + 1],
                                             ALU.is_equal, ALU.mult))
                ch.wait()
                step(dve.tensor_copy(evens[:, :], K["iota"][:, 0:8]))
                dve.sem_inc(ab_ready, 1)
                bi = K["iota"][:, 0:OVER + 2].unsqueeze(2).to_broadcast([P, OVER + 2, EXPERTS])

                def over_b(a):
                    return a.unsqueeze(1).to_broadcast([P, OVER + 2, EXPERTS])

                tt(over[:, :, :], bi, over_b(ob[:, :]), ALU.is_ge)
                tt(over2[:, :, :], bi, over_b(cum[:, :]), ALU.is_lt)
                tt(over[:, :, :], over[:, :, :], over2[:, :, :], ALU.mult)
                tt(over[:, :, :], over[:, :, :], over_b(K["iota"][:, 0:EXPERTS]), ALU.mult)
                step(dve.reduce_sum(bexp[:, EXPERTS:BCOLS], over[:, :, :], axis=AX.X))
                step(dve.tensor_copy(bexp[:, 0:EXPERTS], K["iota"][:, 0:EXPERTS]))
                step(dve.tensor_copy(blk_i[:, :], bexp[:, :]))
                ts(evens[:, :], evens[:, :], 2.0, ALU.mult)
                ts(evens[:, :], evens[:, :], tot[:, 0:1], ALU.is_lt)
                step(dve.reduce_sum(tot[:, 1:2], evens[:, :], axis=AX.X))
                ts(tot[:, 1:2], tot[:, 1:2], float(EXPERTS // 2), ALU.add)
                step(dve.tensor_copy(pairs_i[:, :], tot[:, 1:2]))
                dve.wait_ge(tok_ready, 1)
                step(dve.tensor_copy(tok_i[:, :], pt[:, :]))


class ExpertWeights(Phase):
    NAMES = ("gate", "up", "down")

    def __init__(self, nc, name, w_gate, w_up, w_down):
        super().__init__(nc, name)
        self.sources = dict(zip(self.NAMES, (w_gate, w_up, w_down)))

    def __enter__(self):
        super().__enter__()
        self.raw = {n: self.sb(n, [P, KC * DE]) for n in self.NAMES}
        self.loaded = {n: self.sem(f"{n}_in") for n in self.NAMES}
        return self

    def load(self, sp, n, e):
        src = self.sources[n][e:e + 1, :, :] if isinstance(e, int) else self.sources[n][bass.ds(e, 1), :, :]
        rows_ = src.shape[-2] // P
        sp.dma_start(self.raw[n][:, :].rearrange("p (k n) -> p k n", k=rows_),
                     src.rearrange("o (k p) n -> p (o k) n", p=P)).then_inc(self.loaded[n], 16)

    def load_first(self, sp, n):
        self.load(sp, self.NAMES[n], 0)


def phase_experts(nc, K, name, h, weights, tok_i, blk_i, pairs_i, y):
    FC = DE // P
    PIECES = 4
    PW = KC * DE // PIECES
    with Phase(nc, name) as ph:
        hi, lo = ({n: ph.sb(f"{n}_{part}", [P, KC * DE], F32R) for n in weights.NAMES} for part in ("hi", "lo"))
        idx = ph.sb("idx", [P, 2, 1], I32)
        xg = ph.sb("xg", [P, 2, D])
        xh, xl = ph.sb("xh", [P, KC, P], F32R), ph.sb("xl", [P, KC, P], F32R)
        sg, hh = ph.sb("sg", [P, DE]), ph.sb("hh", [P, DE])
        hTh, hTl = ph.sb("hTh", [P, FC, P], F32R), ph.sb("hTl", [P, FC, P], F32R)
        ysb = ph.sb("y", [P, 2, D])
        tp = ph.ps("tp", [P, 2, 4, P])
        gp, up = ph.ps("gp", [P, HALF]), ph.ps("up", [P, HALF])
        hp = ph.ps("hp", [P, FC, P])
        yp = ph.ps("yp", [P, 2, HALF])
        x_in, idx_ready, tp_ready, x_hi, x_lo, g_ready, gu_ready, silu_done, h_ready, hp_ready, hT_hi, hT_lo = (
            ph.sem(n) for n in ("x_in", "idx_ready", "tp_ready", "x_hi", "x_lo", "g_ready", "gu_ready", "silu_done",
                                "h_ready", "hp_ready", "hT_hi", "hT_lo"))
        y_ready, y_done = ph.sem("y_ready"), ph.sem("y_done")
        w_hi, w_lo = ({n: ph.sem(f"{n}_{part}_ready") for n in weights.NAMES} for part in ("hi", "lo"))
        stored = [ph.sem(f"stored{u}") for u in range(2)]

        def pairs(eng):
            return eng.value_load(pairs_i[0:1, 0:1], min_val=EXPERTS // 2, max_val=BLOCKS // 2)

        def operand(parts, ks, cols):
            return [[p_[:, k, cols] for k in range(ks)] for p_ in parts]

        def matrix(n, ks):
            return [part[n][:, :].rearrange("p (k n) -> p k n", k=ks) for part in (hi, lo)]

        with nc.Block() as block:
            @block.sync
            def _(sp):
                n = pairs(sp)

                def load(m, b, e):
                    sp.wait_ge(w_lo[m], PIECES * b)
                    settle(sp)
                    weights.load(sp, m, e)

                with sp.Fori(0, n) as p:
                    for u in range(2):
                        b = 2 * p + u
                        e = sp.value_load(blk_i[0:1, bass.ds(b + 1, 1)], min_val=0, max_val=EXPERTS - 1)
                        for m in weights.NAMES:
                            load(m, b + 1, e)

            @block.gpsimd
            def _(pool):
                n = pairs(pool)

                def gather(b, u):
                    pool.tensor_copy(idx[:, u, :], tok_i[:, bass.ds(b, 1)] if not isinstance(b, int) else tok_i[:, b:b + 1]).then_inc(idx_ready, 1)
                    pool.wait_ge(idx_ready, b + 1)
                    settle(pool)
                    pool.indirect_dma_start(out=xg[:, u, :], out_offset=None, in_=h,
                                            in_offset=bass.IndirectOffsetOnAxis(ap=idx[:, u, :], axis=0)).then_inc(x_in, 16)

                gather(0, 0)
                with pool.Fori(0, n) as p:
                    for u in range(2):
                        b = 2 * p + u
                        pool.wait_ge(tp_ready, 2 * b + 2)
                        gather(b + 1, 1 - u)
                pool.wait_ge(x_in, n * 32 + 16)
                settle(pool)

            @block.tensor
            def _(pe):
                n = pairs(pe)

                def transposes(b, u):
                    pe.wait_ge(x_in, 16 * b + 16)
                    for bnk in range(2):
                        for k in range(4):
                            last = nc.tensor.transpose(tp[:, bnk, k, :], xg[:, u, (4 * bnk + k) * P:(4 * bnk + k + 1) * P], K["ident"])
                        last.then_inc(tp_ready, 1)

                transposes(0, 0)
                x_parts = operand((xh, xl), KC, slice(None))
                h_parts = operand((hTh, hTl), FC, slice(None))
                with pe.Fori(0, n) as p:
                    for u in range(2):
                        b = 2 * p + u
                        pe.wait_ge(x_lo, 2 * b + 2)
                        pe.wait_ge(h_ready, b + 1)
                        for m, bank, ready in (("gate", gp, g_ready), ("up", up, gu_ready)):
                            pe.wait_ge(w_lo[m], PIECES * b + PIECES)
                            split_product(nc, bank[:, :], x_parts, operand(matrix(m, KC), KC, slice(None))).then_inc(ready, 1)
                        transposes(b + 1, 1 - u)
                        pe.wait_ge(h_ready, b + 2)
                        for k in range(FC):
                            last = nc.tensor.transpose(hp[:, k, :], hh[:, k * P:(k + 1) * P], K["ident"])
                        last.then_inc(hp_ready, 1)
                        pe.wait_ge(w_lo["down"], PIECES * b + PIECES)
                        pe.wait_ge(hT_lo, b + 1)
                        for c in range(2):
                            pe.wait_ge(y_done, 2 * b + c + 1)
                            split_product(nc, yp[:, c, :], h_parts,
                                          operand(matrix("down", FC), FC, slice(c * HALF, (c + 1) * HALF))).then_inc(y_ready, 1)

            @block.scalar
            def _(act):
                n = pairs(act)
                for u in range(2):
                    act.sem_inc(stored[u], 16)

                def x_his(b):
                    for bnk in range(2):
                        act.wait_ge(tp_ready, 2 * b + bnk + 1)
                        part_hi(act, xh[:, 4 * bnk:4 * bnk + 4, :], tp[:, bnk, :, :]).then_inc(x_hi, 1)

                def w_his(m, b):
                    act.wait_ge(weights.loaded[m], 16 * b + 16)
                    for q in range(PIECES):
                        s = slice(q * PW, (q + 1) * PW)
                        part_hi(act, hi[m][:, s], weights.raw[m][:, s]).then_inc(w_hi[m], 1)

                def store(b, u):
                    act.wait_ge(y_done, 2 * b + 4)
                    act.dma_start(y[bass.ds(b * P, P), :], ysb[:, u, :]).then_inc(stored[u], 16)

                w_his("gate", 0)
                x_his(0)
                w_his("up", 0)
                w_his("down", 0)
                with act.Fori(0, n) as p:
                    for u in range(2):
                        b = 2 * p + u
                        act.wait_ge(g_ready, b + 1)
                        act.wait_ge(h_ready, b + 1)
                        act.activation(sg[:, :], gp[:, :], ACT.Silu).then_inc(silu_done, 1)
                        w_his("gate", b + 1)
                        x_his(b + 1)
                        act.wait_ge(hp_ready, b + 1)
                        part_hi(act, hTh[:, :, :], hp[:, :, :]).then_inc(hT_hi, 1)
                        w_his("up", b + 1)
                        act.wait_ge(y_ready, 2 * b + 2)
                        w_his("down", b + 1)
                        store(b, u)
                for u in range(2):
                    act.wait_ge(stored[u], n * 16 + 16)
                    settle(act)

            @block.vector
            def _(dve):
                n = pairs(dve)
                dve.sem_inc(h_ready, 1)
                dve.sem_inc(y_done, 2)

                def x_los(b):
                    for bnk in range(2):
                        dve.wait_ge(x_hi, 2 * b + bnk + 1)
                        part_lo(dve, xl[:, 4 * bnk:4 * bnk + 4, :], tp[:, bnk, :, :], xh[:, 4 * bnk:4 * bnk + 4, :]).then_inc(x_lo, 1)

                def w_los(m, b):
                    for q in range(PIECES):
                        s = slice(q * PW, (q + 1) * PW)
                        dve.wait_ge(w_hi[m], PIECES * b + q + 1)
                        part_lo(dve, lo[m][:, s], weights.raw[m][:, s], hi[m][:, s]).then_inc(w_lo[m], 1)

                w_los("gate", 0)
                x_los(0)
                w_los("up", 0)
                w_los("down", 0)
                with dve.Fori(0, n) as p:
                    for u in range(2):
                        b = 2 * p + u
                        w_los("gate", b + 1)
                        dve.wait_ge(silu_done, b + 1)
                        dve.wait_ge(gu_ready, b + 1)
                        dve.tensor_tensor(hh[:, :], sg[:, :], up[:, :], ALU.mult).then_inc(h_ready, 1)
                        x_los(b + 1)
                        dve.wait_ge(hT_hi, b + 1)
                        part_lo(dve, hTl[:, :, :], hp[:, :, :], hTh[:, :, :]).then_inc(hT_lo, 1)
                        w_los("up", b + 1)
                        dve.wait_ge(stored[u], 16 * p + 16)
                        for c in range(2):
                            dve.wait_ge(y_ready, 2 * b + c + 1)
                            dve.tensor_copy(ysb[:, u, c * HALF:(c + 1) * HALF], yp[:, c, :]).then_inc(y_done, 1)
                        w_los("down", b + 1)


def phase_combine(nc, K, name, h, y, gates, dest_i, g, b, out):
    with Phase(nc, name) as ph:
        gb = ph.sb("gb", [P, 2, D])
        idx = ph.sb("idx", [P, 2, 2, 1], I32)
        hin, r, hn = ph.sb("h", [P, 2, D]), ph.sb("r", [P, 2, D]), ph.sb("hn", [P, 2, D])
        yin = ph.sb("y", [P, 2, 2, D])
        stats, mv = ph.sb("stats", [P, 2, 2, 6]), ph.sb("mv", [P, 2, 2])
        rstd, half = ph.sb("rstd", [P, 2, 1]), ph.sb("half", [P, 1])
        small_in, idx_ready, scaled, used, ms_ready, rstd_ready, h_ready, own, norm_own = (
            ph.sem(n) for n in ("small_in", "idx_ready", "scaled", "used", "ms_ready", "rstd_ready", "h_ready", "own", "norm_own"))
        h_in, y_in, stored = ([ph.sem(f"{n}{u}") for u in range(2)] for n in ("h_in", "y_in", "stored"))
        PAIRS = TILES // 2

        with nc.Block() as block:
            @block.sync
            def _(sp):
                def load(i, u):
                    sp.dma_start(hin[:, u, :], rows(h, i)).then_inc(h_in[u], 16)

                def store(i, u):
                    sp.wait_ge(h_ready, i + 1)
                    sp.dma_start(rows(out, i), hn[:, u, :]).then_inc(stored[u], 16)

                load(0, 0)
                load(1, 1)
                for n, row in enumerate((g, b)):
                    sp.dma_start(gb[:, n, :], row.partition_broadcast(P)).then_inc(small_in, 16)
                with sp.Fori(0, PAIRS - 1) as p:
                    for u in range(2):
                        i = 2 * p + u
                        sp.wait_ge(used, i + 1)
                        load(i + 2, u)
                        store(i, u)
                for u in range(2):
                    store(TILES - 2 + u, u)
                for u in range(2):
                    sp.wait_ge(stored[u], 16 * (PAIRS + 1))

            @block.gpsimd
            def _(pool):
                pool.memset(half[:, :], -0.5).then_inc(rstd_ready, 1)
                pool.wait_ge(rstd_ready, 1)

                def gather(i, u):
                    col = slice(i, i + 1) if isinstance(i, int) else bass.ds(i, 1)
                    pool.tensor_copy(idx[:, u, :, :], dest_i[:, :, col]).then_inc(idx_ready, 1)
                    pool.wait_ge(idx_ready, i + 1)
                    settle(pool)
                    for c in range(2):
                        pool.indirect_dma_start(out=yin[:, u, c, :], out_offset=None, in_=y,
                                                in_offset=bass.IndirectOffsetOnAxis(ap=idx[:, u, c, :], axis=0)).then_inc(y_in[u], 16)

                def power(i, u):
                    pool.wait_ge(ms_ready, i + 1)
                    pool.tensor_tensor(rstd[:, u, :], mv[:, u, 1:2], half[:, :], ALU.pow).then_inc(rstd_ready, 1)

                gather(0, 0)
                gather(1, 1)
                with pool.Fori(0, PAIRS - 1) as p:
                    for u in range(2):
                        i = 2 * p + u
                        pool.wait_ge(used, i + 1)
                        gather(i + 2, u)
                        power(i, u)
                for u in range(2):
                    power(TILES - 2 + u, u)

            @block.scalar
            def _(act):
                with act.Fori(0, PAIRS) as p:
                    for u in range(2):
                        i = 2 * p + u
                        act.wait_ge(h_in[u], 16 * p + 16)
                        act.activation(hin[:, u, :], hin[:, u, :], ACT.Copy, scale=ALPHA).then_inc(scaled, 1)

            @block.vector
            def _(dve):
                dve.wait_ge(small_in, 32)
                for u in range(2):
                    dve.sem_inc(stored[u], 16)

                def add(i, u, turn):
                    at = slice(i, i + 1) if isinstance(i, int) else bass.ds(i, 1)
                    ch = Chain(dve, own, 4 * i)
                    dve.wait_ge(scaled, i + 1)
                    dve.wait_ge(y_in[u], 32 * turn + 32)
                    if not (isinstance(i, int) and i < 2):
                        dve.wait_ge(h_ready, i - 1)
                    ch(dve.scalar_tensor_tensor(r[:, u, :], yin[:, u, 0, :], gates[:, 0, at], hin[:, u, :], ALU.mult, ALU.add))
                    ch.wait()
                    dve.scalar_tensor_tensor(r[:, u, :], yin[:, u, 1, :], gates[:, 1, at], r[:, u, :],
                                             ALU.mult, ALU.add).then_inc(used, 1)
                    dve.wait_ge(used, i + 1)
                    layer_norm_steps(dve, ch, r[:, u], stats[:, u], mv[:, u], ms_ready)

                def norm(i, u, turn):
                    dve.wait_ge(stored[u], 16 * turn + 16)
                    affine(dve, Chain(dve, norm_own, i), r[:, u], mv[:, u], gb, rstd[:, u], rstd_ready, i, hn[:, u], h_ready)

                add(0, 0, 0)
                add(1, 1, 0)
                norm(0, 0, 0)
                add(2, 0, 1)
                norm(1, 1, 0)
                with dve.Fori(1, PAIRS - 1) as p:
                    add(2 * p + 1, 1, p)
                    norm(2 * p, 0, p)
                    add(2 * p + 2, 0, p + 1)
                    norm(2 * p + 1, 1, p)
                add(TILES - 1, 1, PAIRS - 1)
                norm(TILES - 2, 0, PAIRS - 1)
                norm(TILES - 1, 1, PAIRS - 1)


def phase_pool(nc, K, h, w_in, w_grp, ls, counts, mix):
    PADW = 16
    XB = 4
    NG = len(POOL_WINDOWS)
    CG = PG // P
    with Phase(nc, "pool") as ph:
        w = ph.sb("w", [P, KC, D])
        wg = ph.sb("wg", [P, NG, CG, PG])
        lsb = ph.sb("ls", [P, D])
        xin = ph.sb("x", [P, XB, D])
        hT = ph.sb("hT", [P, KC, SEQ])
        u = ph.sb("u", [P, PADW + SEQ])
        s = ph.sb("s", [P, 2, PADW + SEQ])
        inv_count = ph.sb("inv_count", [P, NG, SEQ])
        pT = ph.sb("pT", [P, CG, SEQ])
        ysb = ph.sb("y", [P, TILES, PG])
        tp = ph.ps("tp", [P, 2, 4, P])
        up = ph.ps("up", [P, 2, HALF])
        yp = ph.ps("yp", [P, 2, HALF])
        x_in = [ph.sem(f"x_in{u}") for u in range(XB)]
        w_in_s, small_in, tp_ready, tp_copied, u_ready, u_copied, p_ready, y_ready, y_done, stored, own, padded = (
            ph.sem(n) for n in ("w_in", "small_in", "tp_ready", "tp_copied", "u_ready", "u_copied", "p_ready",
                                "y_ready", "y_done", "stored", "own", "padded"))
        with nc.Block() as block:
            @block.sync
            def _(sp):
                for i in range(TILES):
                    if i >= XB:
                        sp.wait_ge(tp_ready, 2 * (i - XB) + 2)
                    sp.dma_start(xin[:, i % XB, :], rows(h, i)).then_inc(x_in[i % XB], 16)
                for k in range(KC):
                    sp.dma_start(w[:, k, :], w_in[k * P:(k + 1) * P, :]).then_inc(w_in_s, 16)
                for g in range(NG):
                    sp.dma_start(wg[:, g, :, :], w_grp[g].rearrange("(k p) n -> p k n", p=P)).then_inc(small_in, 16)
                sp.dma_start(lsb[:, :], ls.partition_broadcast(P)).then_inc(small_in, 16)
                sp.dma_start(inv_count[:, :, :], counts.partition_broadcast(P)).then_inc(small_in, 16)
                for g in range(NG):
                    sp.wait_ge(y_done, 2 + TILES // 2 * (g + 1))
                    sp.dma_start(mix[:, g * PG:(g + 1) * PG].rearrange("(t p) c -> p t c", p=P), ysb[:, :, :]).then_inc(stored, 16)
                sp.wait_ge(stored, 16 * NG)

            @block.tensor
            def _(pe):
                for i in range(TILES):
                    pe.wait_ge(x_in[i % XB], 16 * (i // XB) + 16)
                    for b in range(2):
                        pe.wait_ge(tp_copied, 2 * i + b + 1)
                        for k in range(4):
                            last = nc.tensor.transpose(tp[:, b, k, :], xin[:, i % XB, (4 * b + k) * P:(4 * b + k + 1) * P], K["ident"])
                        last.then_inc(tp_ready, 1)
                pe.wait_ge(w_in_s, 16 * KC)
                pe.wait_ge(small_in, 16 * (NG + 2))
                pe.wait_ge(tp_copied, 2 + 2 * TILES)

                def channels(ct):
                    for c in range(2):
                        pe.wait_ge(u_copied, 2 * ct + c + 1)
                        for k in range(KC):
                            last = nc.tensor.matmul(up[:, c, :], w[:, k, ct * P:(ct + 1) * P], hT[:, k, c * HALF:(c + 1) * HALF],
                                                    start=(k == 0), stop=(k == KC - 1))
                        last.then_inc(u_ready, 1)

                def outputs(g):
                    pe.wait_ge(p_ready, CG * (g + 1))
                    for t in range(TILES):
                        if t % 2 == 0:
                            pe.wait_ge(y_done, TILES // 2 * g + t // 2 + 1)
                        for k in range(CG):
                            last = nc.tensor.matmul(yp[:, t // 2 % 2, t % 2 * PG:(t % 2 + 1) * PG], pT[:, k, t * P:(t + 1) * P],
                                                    wg[:, g, k, :], start=(k == 0), stop=(k == CG - 1))
                        if t % 2:
                            last.then_inc(y_ready, 1)

                channels(0)
                channels(1)
                for g in range(NG):
                    if g + 1 < NG:
                        channels(CG * (g + 1))
                    outputs(g)
                    if g + 1 < NG:
                        channels(CG * (g + 1) + 1)

            @block.scalar
            def _(act):
                act.sem_inc(tp_copied, 2)
                act.sem_inc(u_copied, 2)
                with act.Fori(0, TILES) as i:
                    for b in range(2):
                        act.wait_ge(tp_ready, 2 * i + b + 1)
                        act.activation(hT[:, 4 * b:4 * b + 4, bass.ds(i * P, P)], tp[:, b, :, :], ACT.Copy).then_inc(tp_copied, 1)
                act.wait_ge(padded, 1)
                for ct in range(KC):
                    if ct > 0:
                        act.wait_ge(p_ready, ct)
                    for c in range(2):
                        act.wait_ge(u_ready, 2 * ct + c + 1)
                        act.copy(u[:, PADW + c * HALF:PADW + (c + 1) * HALF], up[:, c, :]).then_inc(u_copied, 1)

            @block.vector
            def _(dve):
                ch = Chain(dve, own)
                ch(dve.memset(s[:, :, 0:PADW], 0.0))
                dve.memset(u[:, 0:PADW], 0.0).then_inc(padded, 1)
                ch.wait()
                dve.wait_ge(padded, 1)
                dve.sem_inc(y_done, 2)

                def window(ct):
                    g = ct // CG
                    dve.wait_ge(u_copied, 2 * ct + 4)
                    src, step, n = u[:, :], 1, 0
                    while step < POOL_WINDOWS[g]:
                        ch(dve.tensor_tensor(s[:, n % 2, PADW:], src[:, PADW:], src[:, PADW - step:PADW + SEQ - step], ALU.add))
                        ch.wait()
                        src, step, n = s[:, n % 2, :], 2 * step, n + 1
                    ch(dve.tensor_tensor(s[:, n % 2, PADW:], src[:, PADW:], inv_count[:, g, :], ALU.mult))
                    ch.wait()
                    if ct % CG == 0 and g > 0:
                        dve.wait_ge(y_ready, TILES // 2 * g)
                    dve.tensor_tensor(pT[:, ct % CG, :], s[:, n % 2, PADW:], u[:, PADW:], ALU.subtract).then_inc(p_ready, 1)
                    dve.wait_ge(p_ready, ct + 1)

                def outputs(g):
                    if g > 0:
                        dve.wait_ge(stored, 16 * g)
                    for t in range(0, TILES, 2):
                        dve.wait_ge(y_ready, TILES // 2 * g + t // 2 + 1)
                        dve.tensor_tensor(ysb[:, t:t + 2, :], yp[:, t // 2 % 2, :].rearrange("p (a c) -> p a c", a=2),
                                          lsb[:, g * PG:(g + 1) * PG].unsqueeze(1).to_broadcast([P, 2, PG]), ALU.mult).then_inc(y_done, 1)

                dve.wait_ge(small_in, 16 * (NG + 2))
                window(0)
                window(1)
                for g in range(NG):
                    outputs(g)
                    if g + 1 < NG:
                        window(CG * (g + 1))
                        window(CG * (g + 1) + 1)


def phase_project(nc, K, name, x, w_in, q_norm, w_uq, kv_norm, w_ukv, mod, tabs, proj, mq, mk, mkv):
    PIECES = [(COLS["mz"][0], COLS["mz"][1]), (COLS["mq"][0], COLS["mkr"][1]), (COLS["rq"][0], COLS["rk"][1]),
              (COLS["rv"][0], COLS["rz"][1]), (COLS["gq"][0], COLS["gv"][1]), (COLS["gg"][0], COLS["gz"][1])]
    assert sum(b - a for a, b in PIECES) == IN_COLS and max(b - a for a, b in PIECES) <= HALF
    LATENT, ROTATED = 1, 2
    AB, SLOTS, LAG = 3, 4, 2
    NP = len(PIECES)
    LW = MQR + MKVR
    with Phase(nc, name) as ph:
        raw = ph.sb("raw", [P, KC, HALF])
        wh, wl = ph.sb("wh", [P, 2, KC, HALF], F32R), ph.sb("wl", [P, 2, KC, HALF], F32R)
        hh, hl = ph.sb("hh", [P, KC, SEQ], F32R), ph.sb("hl", [P, KC, SEQ], F32R)
        mod_sb, tab_sb = ph.sb("mod", [P, 2, D]), ph.sb("tabs", [P, 2, TILES, RD // 2])
        xin, h = ph.sb("x", [P, 2, D]), ph.sb("h", [P, 2, D])
        row = ph.sb("row", [P, SLOTS, HALF])
        wq, wkv = ph.sb("wq", [P, 2, MH * MQ]), ph.sb("wkv", [P, D])
        ln = ph.sb("ln", [P, LW])
        ss, ms_x, rstd, half = (ph.sb(n, [P, TILES]) for n in ("ss", "ms_x", "rstd", "half"))
        ks = ph.sb("ks", [P, 4, 16])
        kpe = ph.sb("kpe", [P, TILES, ROPE_D])
        lsq, lat, latT = ph.sb("lsq", [P, LW]), ph.sb("lat", [P, 2, LW]), ph.sb("latT", [P, 3, P])
        ms, lr = ph.sb("ms", [P, 2]), ph.sb("lr", [P, 2])
        q_sb, k_sb = ([b[:, u, 0:MH * MQ].rearrange("p (h c) -> p h c", h=MH) for u in range(2)] for b in (xin, h))
        kv_sb = [mod_sb[:, u, :].rearrange("p (h c) -> p h c", h=MH) for u in range(2)]
        rt = [b[:, u, MH * MQ:].rearrange("p (h c) -> p h c", h=8) for b in (xin, h) for u in range(2)]
        tp = ph.ps("tp", [P, 2, 4, P])
        acc = ph.ps("acc", [P, AB, HALF])
        lt = ph.ps("lt", [P, 4, P])
        lp = ph.ps("lp", [P, 2, HALF])
        (raw_in, mod_in, tab_in, small_in, x_sq, x_pow, h_ready, tp_ready, h_hi, h_lo, w_hi, w_lo, acc_ready, acc_done,
         row_done, ms_ready, lr_ready, lat_ready, lt_ready, latT_ready, lp_ready, lp_copied, mla_done,
         own, pool_own) = (ph.sem(n) for n in (
            "raw_in", "mod_in", "tab_in", "small_in", "x_sq", "x_pow", "h_ready", "tp_ready", "h_hi", "h_lo", "w_hi",
            "w_lo", "acc_ready", "acc_done", "row_done", "ms_ready", "lr_ready", "lat_ready", "lt_ready", "latT_ready",
            "lp_ready", "lp_copied", "mla_done", "own", "pool_own"))
        mla_stored = [ph.sem(f"mla_stored{u}") for u in range(2)]
        x_in = [ph.sem(f"x_in{u}") for u in range(2)]
        stored = [ph.sem(f"stored{u}") for u in range(SLOTS)]

        def width(s):
            return PIECES[s][1] - PIECES[s][0]

        def latent_tile(s, t):
            j = TILES * (s - LATENT) + t - LAG
            return j if 0 <= j < TILES else None

        steps = [(s, t, TILES * s + t) for s in range(NP) for t in range(TILES)]

        with nc.Block() as block:
            @block.sync
            def _(sp):
                def load_raw(s):
                    if s > 0:
                        sp.wait_ge(w_lo, KC * s)
                    sp.dma_start(raw[:, :, 0:width(s)], w_in[:, PIECES[s][0]:PIECES[s][1]].rearrange("(k p) n -> p k n", p=P)).then_inc(raw_in, 16)

                def load_x(i):
                    if i >= 2:
                        sp.wait_ge(h_ready, i - 1)
                    sp.dma_start(xin[:, i % 2, :], rows(x, i)).then_inc(x_in[i % 2], 16)

                load_x(0)
                for n in range(2):
                    sp.dma_start(mod_sb[:, n, :], mod[n:n + 1, :].partition_broadcast(P)).then_inc(mod_in, 16)
                load_x(1)
                load_raw(0)
                sp.dma_start(tab_sb[:, :, :, :], tabs).then_inc(tab_in, 16)
                sp.dma_start(ln[:, 0:MQR], q_norm.partition_broadcast(P)).then_inc(small_in, 16)
                sp.dma_start(ln[:, MQR:], kv_norm.partition_broadcast(P)).then_inc(small_in, 16)
                sp.dma_start(wq[:, :, :], w_uq.rearrange("(k p) n -> p k n", p=P)).then_inc(small_in, 16)
                sp.dma_start(wkv[:, :], w_ukv).then_inc(small_in, 16)
                load_x(2)
                load_raw(1)
                for i in range(3, TILES):
                    load_x(i)
                for s, t, n in steps:
                    sp.wait_ge(row_done, n + 1)
                    sp.dma_start(rows(proj, t)[:, PIECES[s][0]:PIECES[s][1]], row[:, n % SLOTS, 0:width(s)]).then_inc(stored[n % SLOTS], 16)
                    j = latent_tile(s, t)
                    if j is not None:
                        sp.wait_ge(mla_done, j + 1)
                        for dst, src in ((mq, q_sb), (mk, k_sb), (mkv, kv_sb)):
                            sp.dma_start(rows(dst, j), src[j % 2].rearrange("p h c -> p (h c)")).then_inc(mla_stored[j % 2], 16)
                    if t == TILES - 1 and s + 2 < NP:
                        load_raw(s + 2)
                for u in range(SLOTS):
                    sp.wait_ge(stored[u], 16 * (len(steps) // SLOTS + 1))
                for u in range(2):
                    sp.wait_ge(mla_stored[u], 48 * (TILES // 2 + 1))

            @block.gpsimd
            def _(pool):
                ch = Chain(pool, pool_own)
                ch(pool.memset(half[:, :], -0.5))
                ch.wait()
                for i in range(TILES):
                    pool.wait_ge(x_sq, i + 1)
                    ch(pool.tensor_scalar(ms_x[:, i:i + 1], ss[:, i:i + 1], 1.0 / D, RMS_EPS, ALU.mult, ALU.add))
                    ch.wait()
                    pool.tensor_tensor(rstd[:, i:i + 1], ms_x[:, i:i + 1], half[:, 0:1], ALU.pow).then_inc(x_pow, 1)
                for i in range(TILES):
                    pool.wait_ge(ms_ready, i + 1)
                    pool.tensor_tensor(lr[:, :], ms[:, :], half[:, 0:2], ALU.pow).then_inc(lr_ready, 1)

            @block.tensor
            def _(pe):
                def transposes(i):
                    pe.wait_ge(h_ready, i + 1)
                    for b in range(2):
                        pe.wait_ge(h_lo, 2 * i + b + 1)
                        for k in range(4):
                            last = nc.tensor.transpose(tp[:, b, k, :], h[:, i % 2, (4 * b + k) * P:(4 * b + k + 1) * P], K["ident"])
                        last.then_inc(tp_ready, 1)

                def latent_transposes(j):
                    pe.wait_ge(lat_ready, j + 1)
                    for k in range(3):
                        last = nc.tensor.transpose(lt[:, k, :], lat[:, j % 2, k * P:(k + 1) * P], K["ident"])
                    last.then_inc(lt_ready, 1)

                def latent_products(j):
                    pe.wait_ge(small_in, 64)
                    pe.wait_ge(latT_ready, j + 1)
                    for c in range(4):
                        pe.wait_ge(lp_copied, 4 * j + c + 1)
                        if c < 2:
                            n = MH * MQ // 2
                            for k in range(2):
                                last = nc.tensor.matmul(lp[:, c % 2, 0:n], latT[:, k, :], wq[:, k, c * n:(c + 1) * n],
                                                        start=(k == 0), stop=(k == 1))
                        else:
                            last = nc.tensor.matmul(lp[:, c % 2, :], latT[:, 2, :], wkv[:, (c - 2) * HALF:(c - 1) * HALF],
                                                    start=True, stop=True)
                        last.then_inc(lp_ready, 1)

                transposes(0)
                for s, t, n in steps:
                    if s == 0 and t + 1 < TILES:
                        transposes(t + 1)
                    j = latent_tile(s, t)
                    if j is not None:
                        latent_transposes(j)
                    if t == 0:
                        pe.wait_ge(w_lo, KC * (s + 1))
                    if s == 0:
                        pe.wait_ge(h_lo, 2 * t + 4)
                    pe.wait_ge(acc_done, n + 1)
                    split_product(nc, acc[:, n % AB, 0:width(s)],
                                  [[p_[:, k, t * P:(t + 1) * P] for k in range(KC)] for p_ in (hh, hl)],
                                  [[p_[:, s % 2, k, 0:width(s)] for k in range(KC)] for p_ in (wh, wl)]).then_inc(acc_ready, 1)
                    if j is not None:
                        latent_products(j)

            @block.scalar
            def _(act):
                act.sem_inc(acc_done, AB)
                act.sem_inc(lp_copied, 2)
                for u in range(2):
                    act.sem_inc(mla_stored[u], 48)
                for u in range(SLOTS):
                    act.sem_inc(stored[u], 16)

                def square(i):
                    act.wait_ge(x_in[i % 2], 16 * (i // 2) + 16)
                    if i >= 2:
                        act.wait_ge(tp_ready, 2 * (i - 1))
                    act.activation(h[:, i % 2, :], xin[:, i % 2, :], ACT.Square, accum_out=ss[:, i:i + 1]).then_inc(x_sq, 1)

                def h_his(i):
                    for b in range(2):
                        act.wait_ge(tp_ready, 2 * i + b + 1)
                        part_hi(act, hh[:, 4 * b:4 * b + 4, i * P:(i + 1) * P], tp[:, b, :, :]).then_inc(h_hi, 1)

                def w_his(s, k):
                    act.wait_ge(raw_in, 16 * s + 16)
                    part_hi(act, wh[:, s % 2, k, 0:width(s)], raw[:, k, 0:width(s)]).then_inc(w_hi, 1)

                square(0)
                square(1)
                for k in range(KC):
                    w_his(0, k)
                h_his(0)
                for s, t, n in steps:
                    if s == 0:
                        if t + 1 < TILES:
                            h_his(t + 1)
                        if t + 2 < TILES:
                            square(t + 2)
                    j = latent_tile(s, t)
                    if j is not None:
                        act.wait_ge(lt_ready, j + 1)
                        act.copy(latT[:, :, :], lt[:, 0:3, :]).then_inc(latT_ready, 1)
                    act.wait_ge(acc_ready, n + 1)
                    act.wait_ge(stored[n % SLOTS], 16 * (n // SLOTS) + 16)
                    act.copy(row[:, n % SLOTS, 0:width(s)], acc[:, n % AB, 0:width(s)]).then_inc(acc_done, 1)
                    if s + 1 < NP:
                        for k in split_turn(t):
                            w_his(s + 1, k)
                    if j is not None:
                        act.wait_ge(mla_stored[j % 2], 48 * (j // 2) + 48)
                        for c in range(4):
                            act.wait_ge(lp_ready, 4 * j + c + 1)
                            dst = (q_sb if c < 2 else kv_sb)[j % 2]
                            m = MH // 2
                            act.copy(dst[:, c % 2 * m:(c % 2 + 1) * m, :],
                                     lp[:, c % 2, 0:m * dst.shape[-1]].rearrange("p (h c) -> p h c", h=m)).then_inc(lp_copied, 1)

            @block.vector
            def _(dve):
                dve.sem_inc(h_lo, 2)
                ch = Chain(dve, own)

                def make_h(i):
                    dve.wait_ge(x_pow, i + 1)
                    ch(dve.scalar_tensor_tensor(h[:, i % 2, :], xin[:, i % 2, :], rstd[:, i:i + 1], mod_sb[:, 0, :], ALU.mult, ALU.mult))
                    ch.wait()
                    dve.tensor_tensor(h[:, i % 2, :], h[:, i % 2, :], mod_sb[:, 1, :], ALU.add).then_inc(h_ready, 1)

                def h_los(i):
                    for b in range(2):
                        dve.wait_ge(h_hi, 2 * i + b + 1)
                        part = (slice(None), slice(4 * b, 4 * b + 4), slice(i * P, (i + 1) * P))
                        part_lo(dve, hl[part], tp[:, b, :, :], hh[part]).then_inc(h_lo, 1)

                def w_los(s, k):
                    dve.wait_ge(w_hi, KC * s + k + 1)
                    part_lo(dve, wl[:, s % 2, k, 0:width(s)], raw[:, k, 0:width(s)], wh[:, s % 2, k, 0:width(s)]).then_inc(w_lo, 1)

                def rotate(r1, r2, o1, o2, cos, sin, tmp):
                    ch(dve.tensor_tensor(tmp[0], r1, cos, ALU.mult))
                    ch(dve.tensor_tensor(tmp[1], r2, sin, ALU.mult))
                    ch(dve.tensor_tensor(tmp[2], r2, cos, ALU.mult))
                    ch(dve.tensor_tensor(tmp[3], r1, sin, ALU.mult))
                    ch.wait()
                    ch(dve.tensor_tensor(o1, tmp[0], tmp[1], ALU.subtract))
                    ch(dve.tensor_tensor(o2, tmp[2], tmp[3], ALU.add))
                    ch.wait()

                def angles(i, heads, step):
                    return [tab_sb[:, k, i:i + 1, ::step].to_broadcast([P, heads, RD // 2 // step]) for k in range(2)]

                def retention_qk(i, r):
                    g = r[:, 0:2 * RH * RD].rearrange("p (h c) -> p h c", c=RD)
                    cos, sin = angles(i, 2 * RH, 1)
                    rotate(g[:, :, 0:32], g[:, :, 32:64], g[:, :, 0:32], g[:, :, 32:64], cos, sin, rt)

                def latents(i, r):
                    kr = r[:, LW:LW + ROPE_D].unsqueeze(1)
                    cos, sin = angles(i, 1, 2)
                    rotate(kr[:, :, 0:16], kr[:, :, 16:32], kpe[:, i:i + 1, 0:16], kpe[:, i:i + 1, 16:32], cos, sin,
                           [ks[:, m:m + 1, :] for m in range(4)])
                    ch(dve.tensor_tensor(lsq[:, :], r[:, 0:LW], r[:, 0:LW], ALU.mult))
                    ch.wait()
                    if i:
                        dve.wait_ge(lr_ready, i)
                    ch(dve.reduce_sum(ms[:, 0:1], lsq[:, 0:MQR], axis=AX.X))
                    ch(dve.reduce_sum(ms[:, 1:2], lsq[:, MQR:], axis=AX.X))
                    ch.wait()
                    ch(dve.tensor_scalar(ms[:, 0:1], ms[:, 0:1], 1.0 / MQR, RMS_EPS, ALU.mult, ALU.add))
                    dve.tensor_scalar(ms[:, 1:2], ms[:, 1:2], 1.0 / MKVR, RMS_EPS, ALU.mult, ALU.add).then_inc(ms_ready, 1)
                    ch.wait()
                    dve.wait_ge(lr_ready, i + 1)
                    if i >= 2:
                        dve.wait_ge(lt_ready, i - 1)
                    o = lat[:, i % 2, :]
                    ch(dve.scalar_tensor_tensor(o[:, 0:MQR], r[:, 0:MQR], lr[:, 0:1], ln[:, 0:MQR], ALU.mult, ALU.mult))
                    ch(dve.scalar_tensor_tensor(o[:, MQR:], r[:, MQR:LW], lr[:, 1:2], ln[:, MQR:], ALU.mult, ALU.mult))
                    ch.wait()
                    dve.sem_inc(lat_ready, 1)

                def finish_mla(j):
                    dve.wait_ge(lp_copied, 4 * j + 6)
                    cos, sin = angles(j, MH, 2)
                    q, k, kv = q_sb[j % 2], k_sb[j % 2], kv_sb[j % 2]
                    a, b = q[:, :, NOPE:NOPE + 16], q[:, :, NOPE + 16:MQ]
                    rotate(a, b, a, b, cos, sin, [r[:, :, 0:16] for r in rt])
                    ch(dve.tensor_copy(k[:, :, 0:NOPE], kv[:, :, 0:NOPE]))
                    ch(dve.tensor_copy(k[:, :, NOPE:MQ], kpe[:, j:j + 1, :].to_broadcast([P, MH, ROPE_D])))
                    ch.wait()
                    dve.sem_inc(mla_done, 1)

                dve.wait_ge(mod_in, 32)
                make_h(0)
                make_h(1)
                for k in range(KC):
                    w_los(0, k)
                h_los(0)
                dve.wait_ge(tab_in, 16)
                dve.wait_ge(small_in, 64)
                for s, t, n in steps:
                    if s == 0:
                        if t + 1 < TILES:
                            h_los(t + 1)
                        if t + 2 < TILES:
                            make_h(t + 2)
                    dve.wait_ge(acc_done, n + 1 + AB)
                    if s == ROTATED:
                        retention_qk(t, row[:, n % SLOTS, :])
                    if s == LATENT:
                        latents(t, row[:, n % SLOTS, :])
                    dve.sem_inc(row_done, 1)
                    if s + 1 < NP:
                        for k in split_turn(t):
                            w_los(s + 1, k)
                    j = latent_tile(s, t)
                    if j is not None:
                        finish_mla(j)


def mla_attention(nc, K, name, mq, mk, mkv, out):
    def tiles(ap, base, step, width):
        return lambda h: ap[:, bass.ds(h * step + base, width)].rearrange("(t p) c -> p t c", p=P)

    phase_attention(nc, K, name, tiles(mq, 0, MQ, MQ), tiles(mk, 0, MQ, MQ), tiles(mkv, NOPE, NOPE + MV, MV),
                    tiles(out, 0, MV, MV), 1, MQ, MV, K["chunked"], MQ ** -0.5)


def phase_mix_out(nc, K, name, proj, mla_o, x, w_g2, b_g2, gla_norm, w_out, mod, final_norm, out):
    final = final_norm is not None
    with Phase(nc, name) as ph:
        w = ph.sb("w", [P, KC, D])
        g2 = ph.sb("g2", [GRANK, P])
        bg = ph.sb("bg", [P, 1])
        gn = ph.sb("gn", [P, GDV])
        gate = ph.sb("gate", [P, D])
        row = ph.sb("row", [P, IN_COLS])
        vv = ph.sb("vv", [P, 2, 256])
        mo = ph.sb("mo", [P, MH * MV])
        rT = ph.sb("rT", [P, 2, P])
        rkT = ph.sb("rkT", [P, RH, P])
        rqw = ph.sb("rqw", [P, 2, P])
        rkw = ph.sb("rkw", [P, RH * RD])
        gT = ph.sb("gT", [P, 2, P])
        ggT = ph.sb("ggT", [GRANK, P])
        z, ab, mn, sg, la, cum = (ph.sb(n, [P, P]) for n in ("z", "ab", "mn", "sg", "la", "cum"))
        last2, elast = ph.sb("last2", [P, 2]), ph.sb("elast", [P, 2])
        epos, eneg, el = (ph.sb(n, [P, P]) for n in ("epos", "eneg", "el"))
        qpos, qneg, kpos, kneg, kwT, kw = (ph.sb(n, [P, P]) for n in ("qpos", "qneg", "kpos", "kneg", "kwT", "kw"))
        kposm, knegm = ph.sb("kposm", [P, GH, P]), ph.sb("knegm", [P, GH, P])
        a_r, a_g = ph.sb("a_r", [P, RH, CH]), ph.sb("a_g", [P, GH, CH])
        past = ph.sb("past", [P, GH, CH], I32)
        um_r, um_g = ph.sb("um_r", [P, 2, 2, P]), ph.sb("um_g", [P, 2, 256])
        s_r, s_g = ph.sb("s_r", [P, 3, 2, P]), ph.sb("s_g", [P, 3, 256])
        o, osq = ph.sb("o", [P, 8, 64]), ph.sb("osq", [P, 8, 64])
        ms, rs, half = ph.sb("ms", [P, 8]), ph.sb("rs", [P, 8]), ph.sb("half", [P, 8])
        zs = ph.sb("zs", [P, D])
        mixed = ph.sb("mixed", [P, D])
        mT = ph.sb("mT", [P, KC, P])
        xr, xn = ph.sb("xr", [P, D]), ph.sb("xn", [P, D])
        if final:
            fn, junk = ph.sb("fn", [P, D]), ph.sb("junk", [P, D])
            fs, fr = ph.sb("fs", [P, 2]), ph.sb("fr", [P, 1])
        tA, tB, sc, pf = (ph.ps(n, [P, 4, P]) for n in ("tA", "tB", "sc", "pf"))
        u0, u1, op, acc = (ph.ps(n, [P, HALF]) for n in ("u0", "u1", "op", "acc"))
        S = {n: ph.sem(n) for n in (
            "w_in", "small_in", "row_in", "v_in", "x_in", "t_ready", "t_copied", "z_ready", "z_done", "mt_ready", "mt_copied",
            "acc_ready", "x_part", "kwt_ready", "kw_ready", "rs_ready", "gs_ready", "ar_ready", "ag_ready", "u_ready",
            "s_ready", "o_ready", "rk_ready", "ab_ready", "sg_ready", "cum_ready", "exps_ready", "q_ready", "silu_done",
            "zg_ready", "ms_ready", "rms_ready", "mix_ready", "o_copied", "xn_ready", "fs_ready", "fr_ready", "stored",
            "own", "res_own", "act_own", "pool_own", "kwt_done")}
        col = {n: row[:, a:b] for n, (a, b) in COLS.items()}
        scale_g = GDK ** -0.5

        with nc.Block() as block:
            @block.sync
            def _(sp):
                def load_row(i):
                    sp.dma_start(row[:, :], rows(proj, i)).then_inc(S["row_in"], 16)

                def load_values(i):
                    r = rows(proj, i)
                    for n, c in enumerate(("rv", "gv")):
                        sp.dma_start(vv[:, n, :], r[:, COLS[c][0]:COLS[c][1]]).then_inc(S["v_in"], 16)
                    sp.dma_start(mo[:, :], rows(mla_o, i)).then_inc(S["v_in"], 16)

                def store(i):
                    sp.wait_ge(S["xn_ready"], i + 1)
                    sp.dma_start(rows(out, i), xn[:, :]).then_inc(S["stored"], 16)

                def turn(i):
                    sp.wait_ge(S["zg_ready"], i + 1)
                    sp.wait_ge(S["rs_ready"], i + 1)
                    load_row(i + 1)
                    sp.wait_ge(S["mix_ready"], i + 1)
                    load_values(i + 1)

                load_row(0)
                load_values(0)
                sp.dma_start(g2[:, :], w_g2).then_inc(S["small_in"], 16)
                with nc.allow_non_contiguous_dma(reason="one bias per partition"):
                    sp.dma_start(bg[:, :], b_g2.rearrange("o (p a) -> p (o a)", a=1)).then_inc(S["small_in"], 16)
                sp.dma_start(gn[:, :], gla_norm.partition_broadcast(P)).then_inc(S["small_in"], 16)
                sp.dma_start(gate[:, :], mod[2:3, :].partition_broadcast(P)).then_inc(S["small_in"], 16)
                if final:
                    sp.dma_start(fn[:, :], final_norm.partition_broadcast(P)).then_inc(S["small_in"], 16)
                for k in range(KC):
                    sp.dma_start(w[:, k, :], w_out[k * P:(k + 1) * P, :]).then_inc(S["w_in"], 16)
                sp.dma_start(xr[:, :], rows(x, 0)).then_inc(S["x_in"], 16)
                turn(0)
                with sp.Fori(1, TILES - 1) as i:
                    turn(i)
                    store(i - 1)
                    sp.dma_start(xr[:, :], rows(x, i)).then_inc(S["x_in"], 16)
                store(TILES - 2)
                sp.dma_start(xr[:, :], rows(x, TILES - 1)).then_inc(S["x_in"], 16)
                store(TILES - 1)
                sp.wait_ge(S["stored"], 16 * (TILES + 1))

            @block.gpsimd
            def _(pool):
                pool.memset(half[:, :], -0.5).then_inc(S["pool_own"], 1)
                pool.memset(s_r[:, 2, :, :], 0.0).then_inc(S["pool_own"], 1)
                pool.memset(s_g[:, 2, :], 0.0).then_inc(S["pool_own"], 1)
                pool.memset(rkT[:, :, :], 0.0).then_inc(S["pool_own"], 1)
                pool.wait_ge(S["pool_own"], 4)
                pool.wait_ge(S["small_in"], 80 if final else 64)

                def final_power(i):
                    pool.wait_ge(S["fs_ready"], i + 1)
                    pool.tensor_tensor(fr[:, :], fs[:, 1:2], half[:, 0:1], ALU.pow).then_inc(S["fr_ready"], 1)

                def tile(i):
                    pool.wait_ge(S["row_in"], 16 * i + 16)
                    pool.tensor_tensor(rkw[:, :].rearrange("p (h c) -> p h c", h=RH), col["rk"].rearrange("p (h c) -> p h c", h=RH),
                                       K["rkw"].unsqueeze(2).to_broadcast([P, RH, RD]), ALU.mult).then_inc(S["rk_ready"], 1)
                    pool.wait_ge(S["t_copied"], 3 * i + 1)
                    pool.tensor_tensor(rqw[:, :, :], rT[:, :, :], K["rqw"].rearrange("p (a c) -> p a c", a=2),
                                       ALU.mult).then_inc(S["rk_ready"], 1)
                    pool.wait_ge(S["silu_done"], 3 * i + 3)
                    g = zs[:, 768:].rearrange("p (h c) -> p h c", h=GH)
                    pool.tensor_tensor(g, g, gn[:, :].unsqueeze(1).to_broadcast([P, GH, GDV]), ALU.mult).then_inc(S["zg_ready"], 1)
                    pool.wait_ge(S["ms_ready"], i + 1)
                    pool.tensor_tensor(rs[:, :], ms[:, :], half[:, :], ALU.pow).then_inc(S["rms_ready"], 1)
                    if final and not (isinstance(i, int) and i == 0):
                        final_power(i - 1)

                tile(0)
                with pool.Fori(1, TILES) as i:
                    tile(i)
                if final:
                    final_power(TILES - 1)

            @block.tensor
            def _(pe):
                T, M = nc.tensor.transpose, nc.tensor.matmul

                def open_tile(i):
                    pe.wait_ge(S["row_in"], 16 * i + 16)
                    for n in range(4):
                        last = T(tA[:, n, :], row[:, n * P:(n + 1) * P], K["ident"])
                    last.then_inc(S["t_ready"], 1)
                    T(tB[:, 0, :], col["gq"], K["ident"])
                    T(tB[:, 1, :], col["gk"], K["ident"])
                    T(tB[0:GRANK, 2, :], col["gg"], K["ident"]).then_inc(S["t_ready"], 1)

                def gate_and_retention(i):
                    pe.wait_ge(S["small_in"], 80 if final else 64)
                    pe.wait_ge(S["t_copied"], 3 * i + 3)
                    M(tB[:, 3, :], g2[:, :], ggT[:, :], start=True, stop=True).then_inc(S["z_ready"], 1)
                    for h in range(RH):
                        for c in range(2):
                            t = slice(c * CH, (c + 1) * CH)
                            last = M(sc[t, h // 2, h % 2 * CH:(h % 2 + 1) * CH], rkT[:, h, t], rT[:, h // 2, t],
                                     start=True, stop=True)
                    last.then_inc(S["rs_ready"], 1)

                def mixed_transposes(i):
                    pe.wait_ge(S["mix_ready"], i + 1)
                    for b, bank in enumerate((tA, tB)):
                        if b == 1 and not (isinstance(i, int) and i == TILES - 1):
                            pe.wait_ge(S["z_done"], i + 2)
                        for k in range(4):
                            last = T(bank[:, k, :], mixed[:, (4 * b + k) * P:(4 * b + k + 1) * P], K["ident"])
                        last.then_inc(S["mt_ready"], 1)
                    pe.wait_ge(S["w_in"], 16 * KC)
                    pe.wait_ge(S["mt_copied"], 2 * i + 2)

                def project(i, c, chunks=range(KC)):
                    if chunks[0] == 0:
                        pe.wait_ge(S["x_part"], 2 * i + c + 1)
                    for k in chunks:
                        last = M(acc[:, :], mT[:, k, :], w[:, k, c * HALF:(c + 1) * HALF], start=(k == 0), stop=(k == KC - 1))
                    if chunks[-1] == KC - 1:
                        last.then_inc(S["acc_ready"], 1)

                def scores_and_updates(i):
                    pe.wait_ge(S["q_ready"], i + 1)
                    T(sc[:, 2, :], kwT[:, :], K["ident"]).then_inc(S["kwt_ready"], 1)
                    for n, (k_, q_) in enumerate(((knegm, qpos), (kposm, qneg))):
                        for h in range(GH):
                            for c in range(2):
                                t = slice(c * CH, (c + 1) * CH)
                                last = M(pf[t, 2 * n + h // 2, h % 2 * CH:(h % 2 + 1) * CH], k_[:, h, t], q_[:, t], start=True, stop=True)
                    last.then_inc(S["gs_ready"], 1)
                    pe.wait_ge(S["v_in"], 48 * i + 48)
                    pe.wait_ge(S["rk_ready"], 2 * i + 2)
                    pe.wait_ge(S["kw_ready"], i + 1)
                    for c in range(2):
                        t = slice(c * CH, (c + 1) * CH)
                        for p in range(2):
                            M((u0, u1)[c][:, p * P:(p + 1) * P], rkw[t, p * P:(p + 1) * P], vv[t, 0, p * P:(p + 1) * P],
                              start=True, stop=True)
                        last = M((u0, u1)[c][:, 256:512], kw[t, :], vv[t, 1, :], start=True, stop=True)
                    last.then_inc(S["u_ready"], 1)

                def outputs(i):
                    pe.wait_ge(S["ar_ready"], i + 1)
                    pe.wait_ge(S["ag_ready"], i + 1)
                    pe.wait_ge(S["s_ready"], i + 1)
                    for c in range(2):
                        t = slice(c * CH, (c + 1) * CH)
                        for p in range(2):
                            M(op[t, p * P:(p + 1) * P], rqw[:, p, t], s_r[:, c, p, :], start=True, stop=False)
                            for h in (2 * p, 2 * p + 1):
                                M(op[t, h * RD:(h + 1) * RD], a_r[t, h, :], vv[t, 0, h * RD:(h + 1) * RD], start=False, stop=(h % 2 == 1))
                        M(op[t, 256:512], qpos[:, t], s_g[:, c, :], start=True, stop=False)
                        for h in range(GH):
                            last = M(op[t, 256 + h * GDV:256 + (h + 1) * GDV], a_g[t, h, :], vv[t, 1, h * GDV:(h + 1) * GDV],
                                     start=False, stop=(h == GH - 1))
                    last.then_inc(S["o_ready"], 1)

                def tile(i, last=False):
                    gate_and_retention(i)
                    mixed_transposes(i - 1)
                    project(i - 1, 0)
                    scores_and_updates(i)
                    project(i - 1, 1, range(KC // 2))
                    outputs(i)
                    if not last:
                        open_tile(i + 1)
                    project(i - 1, 1, range(KC // 2, KC))

                open_tile(0)
                gate_and_retention(0)
                scores_and_updates(0)
                outputs(0)
                open_tile(1)
                with pe.Fori(1, TILES - 1) as i:
                    tile(i)
                tile(TILES - 1, last=True)
                mixed_transposes(TILES - 1)
                project(TILES - 1, 0)
                project(TILES - 1, 1)

            @block.scalar
            def _(act):
                def copies(i):
                    act.wait_ge(S["t_ready"], 2 * i + 1)
                    act.copy(rT[:, :, :], tA[:, 0:2, :])
                    for h in range(2):
                        r = slice(RD * h, RD * h + RD)
                        last = act.copy(rkT[r, h::2, :], tA[r, 2:4, :])
                    last.then_inc(S["t_copied"], 1)
                    act.wait_ge(S["t_ready"], 2 * i + 2)
                    act.copy(gT[:, :, :], tB[:, 0:2, :]).then_inc(S["t_copied"], 1)
                    act.copy(ggT[:, :], tB[0:GRANK, 2, :]).then_inc(S["t_copied"], 1)

                def mixed_copies(i):
                    for b, bank in enumerate((tA, tB)):
                        act.wait_ge(S["mt_ready"], 2 * i + b + 1)
                        act.copy(mT[:, 4 * b:4 * b + 4, :], bank[:, :, :]).then_inc(S["mt_copied"], 1)

                def gates(i):
                    ch = Chain(act, S["act_own"], i)
                    act.wait_ge(S["ab_ready"], i + 1)
                    ch(act.activation(ab[:, :], ab[:, :], ACT.Exp, scale=-1.0))
                    ch.wait()
                    act.activation(sg[:, :], ab[:, :], ACT.Ln, bias=1.0).then_inc(S["sg_ready"], 1)
                    act.wait_ge(S["cum_ready"], i + 1)
                    act.activation(epos[:, :], cum[:, :], ACT.Exp, scale=1.0 / 16).then_inc(S["exps_ready"], 1)
                    act.activation(eneg[:, :], cum[:, :], ACT.Exp, scale=-1.0 / 16).then_inc(S["exps_ready"], 1)
                    for c in range(2):
                        t = slice(c * CH, (c + 1) * CH)
                        act.activation(el[:, t], cum[:, t], ACT.Exp, scale=-1.0 / 16, bias=last2[:, c:c + 1]).then_inc(S["exps_ready"], 1)
                    act.activation(elast[:, :], last2[:, :], ACT.Exp).then_inc(S["exps_ready"], 1)

                def silus(i):
                    for n, (c, a) in enumerate((("rz", 0), ("mz", 256), ("gz", 768))):
                        width = COLS[c][1] - COLS[c][0]
                        act.activation(zs[:, a:a + width], col[c], ACT.Silu).then_inc(S["silu_done"], 1)

                act.sem_inc(S["stored"], 16)
                act.wait_ge(S["pool_own"], 4)
                copies(0)
                gates(0)
                silus(0)
                with act.Fori(1, TILES) as i:
                    copies(i)
                    mixed_copies(i - 1)
                    gates(i)
                    act.wait_ge(S["mix_ready"], i)
                    silus(i)
                mixed_copies(TILES - 1)

            @block.vector
            def _(dve):
                dve.sem_inc(S["x_part"], 1)
                n_res = 5 if final else 2
                n_tile = 31

                def residual(i, c):
                    ch = Chain(dve, S["res_own"], n_res * i + c)
                    if c == 0:
                        dve.wait_ge(S["x_in"], 16 * i + 16)
                        dve.wait_ge(S["stored"], 16 * i + 16)
                    s = slice(c * HALF, (c + 1) * HALF)
                    dve.wait_ge(S["acc_ready"], 2 * i + c + 1)
                    dve.tensor_tensor(xn[:, s], acc[:, :], gate[:, s], ALU.mult).then_inc(S["x_part"], 1)
                    dve.wait_ge(S["x_part"], 2 * i + c + 2)
                    ch(dve.tensor_tensor(xn[:, s], xn[:, s], xr[:, s], ALU.add))
                    if c == 1:
                        ch.wait()
                        if final:
                            ch(dve.tensor_tensor(junk[:, :], xn[:, :], xn[:, :], ALU.mult))
                            ch.wait()
                            ch(dve.reduce_sum(fs[:, 0:1], junk[:, :], axis=AX.X))
                            ch.wait()
                            dve.tensor_scalar(fs[:, 1:2], fs[:, 0:1], 1.0 / D, RMS_EPS, ALU.mult, ALU.add).then_inc(S["fs_ready"], 1)
                        else:
                            dve.sem_inc(S["xn_ready"], 1)

                def finish(i):
                    if final:
                        ch = Chain(dve, S["res_own"], n_res * i + 4)
                        dve.wait_ge(S["fr_ready"], i + 1)
                        ch(dve.scalar_tensor_tensor(xn[:, :], xn[:, :], fr[:, 0:1], fn[:, :], ALU.mult, ALU.mult))
                        ch.wait()
                        dve.sem_inc(S["xn_ready"], 1)

                def tile(i, finished=None):
                    ch = Chain(dve, S["own"], n_tile * i + 1)
                    dve.wait_ge(S["z_ready"], i + 1)
                    ch(dve.tensor_scalar(z[:, :], tB[:, 3, :], bg[:, 0:1], None, ALU.add))
                    ch.wait()
                    dve.sem_inc(S["z_done"], 1)
                    dve.scalar_tensor_tensor(ab[:, :], z[:, :], -1.0, z[:, :], ALU.mult, ALU.max).then_inc(S["ab_ready"], 1)
                    ch(dve.tensor_scalar(mn[:, :], z[:, :], 0.0, None, ALU.min))
                    if finished is not None:
                        residual(finished, 1)
                    dve.wait_ge(S["rs_ready"], i + 1)
                    dve.tensor_tensor(a_r[:, :, :], sc[:, 0:2, :].rearrange("p a (b c) -> p (a b) c", c=CH),
                                      K["decay"].rearrange("p (h c) -> p h c", h=RH), ALU.mult).then_inc(S["ar_ready"], 1)
                    ch.wait()
                    dve.wait_ge(S["sg_ready"], i + 1)
                    ch(dve.tensor_tensor(la[:, :], mn[:, :], sg[:, :], ALU.subtract))
                    ch.wait()
                    ch(dve.tensor_tensor_scan(cum[:, :], K["scan"], la[:, :], 0.0, ALU.mult, ALU.add))
                    ch.wait()
                    dve.tensor_scalar(last2[:, :], cum[:, CH - 1::CH], 1.0 / 16, None, ALU.mult).then_inc(S["cum_ready"], 1)
                    if finished is not None:
                        finish(finished)
                    dve.wait_ge(S["exps_ready"], 5 * i + 5)
                    ch(dve.tensor_tensor(qpos[:, :], gT[:, 0, :], epos[:, :], ALU.mult))
                    ch(dve.tensor_tensor(qneg[:, :], gT[:, 0, :], eneg[:, :], ALU.mult))
                    for dst, e in ((kneg, eneg), (kpos, epos), (kwT, el)):
                        ch(dve.scalar_tensor_tensor(dst[:, :], gT[:, 1, :], scale_g, e[:, :], ALU.mult, ALU.mult))
                    ch.wait()
                    hm = K["ghead"].unsqueeze(2).to_broadcast([P, GH, P])
                    ch(dve.tensor_tensor(knegm[:, :, :], kneg[:, :].unsqueeze(1).to_broadcast([P, GH, P]), hm, ALU.mult))
                    ch(dve.tensor_tensor(kposm[:, :, :], kpos[:, :].unsqueeze(1).to_broadcast([P, GH, P]), hm, ALU.mult))
                    ch.wait()
                    dve.sem_inc(S["q_ready"], 1)
                    if not (isinstance(i, int) and i == 0):
                        residual(i - 1, 0)
                    dve.wait_ge(S["kwt_ready"], i + 1)
                    dve.tensor_copy(kw[:, :], sc[:, 2, :]).then_inc(S["kw_ready"], 1)
                    dve.wait_ge(S["gs_ready"], i + 1)
                    ch(dve.tensor_copy(a_g[:, :, :], pf[:, 2:4, :].rearrange("p a (b c) -> p (a b) c", c=CH)))
                    ch.wait()
                    settle(dve)
                    dve.copy_predicated(a_g[:, :, :], past[:, :, :], pf[:, 0:2, :].rearrange("p a (b c) -> p (a b) c", c=CH)).then_inc(S["ag_ready"], 1)
                    dve.wait_ge(S["u_ready"], i + 1)
                    for c, bank in enumerate((u0, u1)):
                        ch(dve.tensor_tensor(um_r[:, c, :, :], bank[:, 0:256].rearrange("p (a c) -> p a c", a=2),
                                             K["rbd"].unsqueeze(1).to_broadcast([P, 2, P]), ALU.mult))
                        ch(dve.tensor_tensor(um_g[:, c, :], bank[:, 256:512], K["gbd"], ALU.mult))
                    ch(dve.tensor_copy(s_r[:, 0, :, :], s_r[:, 2, :, :]))
                    ch(dve.tensor_copy(s_g[:, 0, :], s_g[:, 2, :]))
                    ch.wait()
                    for c in range(2):
                        for p in range(2):
                            ch(dve.scalar_tensor_tensor(s_r[:, c + 1, p, :], s_r[:, c, p, :], K["ra"][:, p:p + 1], um_r[:, c, p, :], ALU.mult, ALU.add))
                        ch(dve.scalar_tensor_tensor(s_g[:, c + 1, :], s_g[:, c, :], elast[:, c:c + 1], um_g[:, c, :], ALU.mult, ALU.add))
                        ch.wait()
                    dve.sem_inc(S["s_ready"], 1)
                    dve.wait_ge(S["o_ready"], i + 1)
                    ch(dve.tensor_copy(o[:, :, :], op[:, :].rearrange("p (h c) -> p h c", h=8)))
                    ch.wait()
                    ch(dve.tensor_tensor(osq[:, :, :], o[:, :, :], o[:, :, :], ALU.mult))
                    ch.wait()
                    ch(dve.reduce_sum(ms[:, :], osq[:, :, :], axis=AX.X))
                    ch.wait()
                    dve.tensor_scalar(ms[:, :], ms[:, :], 1.0 / 64, RMS_EPS, ALU.mult, ALU.add).then_inc(S["ms_ready"], 1)
                    dve.wait_ge(S["zg_ready"], i + 1)
                    ch(dve.tensor_tensor(mixed[:, 256:768], mo[:, :], zs[:, 256:768], ALU.mult))
                    dve.wait_ge(S["rms_ready"], i + 1)
                    ch(dve.tensor_tensor(o[:, :, :], o[:, :, :], rs[:, :].unsqueeze(2).to_broadcast([P, 8, 64]), ALU.mult))
                    ch.wait()
                    o2 = o[:, :, :].rearrange("p h c -> p (h c)")
                    ch(dve.tensor_tensor(mixed[:, 0:256], o2[:, 0:256], zs[:, 0:256], ALU.mult))
                    ch(dve.tensor_tensor(mixed[:, 768:], o2[:, 256:], zs[:, 768:], ALU.mult))
                    ch.wait()
                    dve.sem_inc(S["mix_ready"], 1)
                    assert ch.n == n_tile, ch.n

                ch = Chain(dve, S["own"])
                ch(dve.tensor_copy(past[:, :, :], K["past"].unsqueeze(1).to_broadcast([P, GH, CH])))
                ch.wait()
                dve.wait_ge(S["small_in"], 80 if final else 64)
                dve.wait_ge(S["pool_own"], 4)
                tile(0)
                tile(1)
                with dve.Fori(2, TILES) as i:
                    tile(i, finished=i - 2)
                residual(TILES - 2, 1)
                finish(TILES - 2)
                residual(TILES - 1, 0)
                residual(TILES - 1, 1)
                finish(TILES - 1)


def program(nc, A, consts, out):
    def scratch(name, *shape):
        return nc.dram_tensor(f"scratch_{name}", shape, F32, kind="Internal").ap()

    qkv, mix, y = scratch("qkv", SEQ, QKV), scratch("mix", SEQ, D), scratch("y", BLOCKS * P, D)
    h = [scratch(f"h{n}", SEQ, D) for n in range(4)]
    proj, mla_o, x1 = scratch("proj", SEQ, IN_COLS), scratch("mla_o", SEQ, MH * MV), scratch("x1", SEQ, D)
    mods, tabs = scratch("mods", 2, 3, D), scratch("tabs", P, 2, TILES, RD // 2)
    mq, mk, mkv = scratch("mq", SEQ, MH * MQ), scratch("mk", SEQ, MH * MQ), scratch("mkv", SEQ, MH * (NOPE + MV))

    with ExitStack() as stack:
        def held(name, shape, dt=F32):
            return stack.enter_context(nc.sbuf_tensor(name, shape, dt))

        logits = held("logits", [P, TILES, GROUPS + EXPERTS])
        gates, dest_i = held("gates", [P, 2, TILES]), held("dest_i", [P, 2, TILES], I32)
        tok_i, blk_i, pairs_i = held("tok_i", [P, BCOLS], I32), held("blk_i", [P, BCOLS], I32), held("pairs_i", [P, 1], I32)

        def moe_layer(K, l, mix_w, h_in, h_mid, h_out):
            r = slice(l, l + 1)
            with ExpertWeights(nc, f"weights{l}", A["moe_w_gate"][l], A["moe_w_up"][l], A["moe_w_down"][l]) as weights:
                phase_out_norm(nc, K, f"out{l}", mix, mix_w, h_in, A["ln_g"][l, 0:1, :], A["ln_b"][l, 0:1, :],
                               A["moe_w_grp_router"][l], A["moe_b_grp_router"][r, :], A["moe_w_exp_router"][l],
                               A["moe_b_exp_router"][r, :], h_mid, logits, weights)
                phase_route(nc, K, f"route{l}", logits, gates, dest_i, tok_i, blk_i, pairs_i)
                phase_experts(nc, K, f"experts{l}", h_mid, weights, tok_i, blk_i, pairs_i, y)
            phase_combine(nc, K, f"combine{l}", h_mid, y, gates, dest_i, A["ln_g"][l, 1:2, :], A["ln_b"][l, 1:2, :], h_out)

        def body(K):
            x = A["x"][0]
            phase_qkv(nc, K, x, A["attn_w_qkv"][0], qkv, y, A["positions_2"], tabs)
            diff_attention(nc, K, qkv, [A[f"attn_{n}"] for n in ("lq1", "lk1", "lq2", "lk2")], A["attn_sub_g"], mix,
                           (A["c_2"], A["ada_w_2"], A["ada_b_2"], A["norm_w_2"], mods))
            moe_layer(K, 0, A["attn_w_o"][0], x, h[0], h[1])
            phase_pool(nc, K, h[1], A["pool_w_in"][0], A["pool_w_grp"][0], A["pool_scale"], A["inverse_counts"], mix)
            moe_layer(K, 1, A["pool_w_out"][0], h[1], h[2], h[3])
            src = h[3]
            for l in range(2):
                r = slice(l, l + 1)
                mod = mods[l]
                phase_project(nc, K, f"project{l}", src, A["w_in_2"][l], A["mla_q_norm_2"][r, :], A["w_uq_2"][l],
                              A["mla_kv_norm_2"][r, :], A["w_ukv_2"][l], mod, tabs, proj, mq, mk, mkv)
                mla_attention(nc, K, f"mla{l}", mq, mk, mkv, mla_o)
                phase_mix_out(nc, K, f"mixout{l}", proj, mla_o, src, A["gla_w_g2_2"][l], A["gla_b_g2_2"][r, :],
                              A["gla_norm_2"][r, :], A["w_out_2"][l], mod,
                              A["final_norm_2"].rearrange("(a n) -> a n", a=1) if l == 1 else None, out[0] if l == 1 else x1)
                src = x1

        with_constants(nc, stack, consts, body)


_INS = ["x", "attn_w_qkv", "attn_w_o", "attn_lq1", "attn_lk1", "attn_lq2", "attn_lk2", "attn_sub_g", "pool_w_in",
        "pool_w_grp", "pool_scale", "pool_w_out", "ln_g", "ln_b", "moe_w_grp_router", "moe_b_grp_router",
        "moe_w_exp_router", "moe_b_exp_router", "moe_w_gate", "moe_w_up", "moe_w_down", "c_2", "positions_2",
        "norm_w_2", "ada_w_2", "ada_b_2", "w_in_2", "mla_q_norm_2", "w_uq_2", "mla_kv_norm_2", "w_ukv_2",
        "gla_w_g2_2", "gla_b_g2_2", "gla_norm_2", "w_out_2", "final_norm_2"]


def kernel(**inputs):
    import concourse.bacc as bacc
    from concourse.bass_utils import run_bass_kernel_spmd

    nc = bacc.Bacc("TRN2", target_bir_lowering=False, num_devices=1)
    arrays, args = {}, {}
    for name in _INS:
        a = np.ascontiguousarray(inputs[name])
        arrays[f"in_{name}_dram"] = a
        args[name] = nc.dram_tensor(f"in_{name}_dram", a.shape, mybir.dt.from_np(a.dtype), kind="ExternalInput").ap()
    packed = np.concatenate(list(constant_parts().values()), axis=1)
    arrays["consts_dram"] = packed
    consts = nc.dram_tensor("consts_dram", packed.shape, F32, kind="ExternalInput").ap()
    arrays["counts_dram"] = inverse_counts()
    args["inverse_counts"] = nc.dram_tensor("counts_dram", arrays["counts_dram"].shape, F32, kind="ExternalInput").ap()
    out = nc.dram_tensor("out_0_dram", (1, SEQ, D), F32, kind="ExternalOutput").ap()
    program(nc, args, consts, out)
    r = run_bass_kernel_spmd(nc, [arrays], core_ids=[0])
    return r.results[0]["out_0_dram"]
```
